# Optimizing a Trainium2 kernel written in Bass

```python
import jax, jax.numpy as jnp
from jax import lax
import numpy as np

D_MODEL = 1024
BATCH = 1
SEQ = 256
DEPTH = 2

CONV_CH = 512
CONV_WIDTH = 31
RET_HEADS = 4
RET_DK = 128
RET_DV = 256
RET_CHUNK = 128
RET_ROPE_BASE = 10000.0
NSA_HEADS = 8
NSA_GROUPS = 2
NSA_HPG = NSA_HEADS // NSA_GROUPS
NSA_DH = 64
NSA_N_BRANCH = 3
CMP_BLOCK = 32
CMP_STRIDE = 16
CMP_HIDDEN = 256
SEL_BLOCK = 64
SEL_TOPK = 16
SEL_QBLOCK = 64
WINDOW = 512
WIN_QBLOCK = 128
ROPE_THETA = 500000.0
ROT_DIM = NSA_DH // 4
N_EXPERTS = 64
N_EXPERT_GROUPS = 8
TOPK_GROUPS = 4
TOPK = 8
D_EXPERT = 256
D_SHARED = 256
ROUTED_SCALE = 2.5
MOE_TOKEN_BLOCK = 128
N_BRANCHES = 3
DN_ALPHA = (2.0 * DEPTH) ** 0.25
DN_BETA = (8.0 * DEPTH) ** -0.25
LN_EPS = 1e-5
NEG = -1e30

IN_WIDTHS = (CONV_CH, CONV_CH,
             RET_HEADS * RET_DK, RET_HEADS * RET_DK, RET_HEADS * RET_DV, RET_HEADS * RET_DV,
             NSA_HEADS * NSA_DH,
             NSA_GROUPS * NSA_DH, NSA_GROUPS * NSA_DH, NSA_GROUPS * NSA_DH,
             NSA_GROUPS * NSA_DH, NSA_GROUPS * NSA_DH, NSA_GROUPS * NSA_DH,
             NSA_HEADS * NSA_N_BRANCH,
             N_BRANCHES * D_MODEL)
D_IN = sum(IN_WIDTHS)

kernel_name = "hybrid_conv_retnet_nsa_moe_deepnorm"

def layer_norm(x, g, b):
    xf = x.astype(jnp.float32)
    mu = jnp.mean(xf, -1, keepdims=True)
    var = jnp.mean(jnp.square(xf - mu), -1, keepdims=True)
    y = (xf - mu) * lax.rsqrt(var + LN_EPS)
    return (y * g.astype(jnp.float32) + b.astype(jnp.float32)).astype(x.dtype)

def rope(x, pos, inv_freq):
    half = inv_freq.shape[0]
    rd = 2 * half
    ang = pos.astype(jnp.float32)[:, :, None, None] * inv_freq
    cos, sin = jnp.cos(ang), jnp.sin(ang)
    x1 = x[..., :half].astype(jnp.float32)
    x2 = x[..., half:rd].astype(jnp.float32)
    rot = jnp.concatenate([x1 * cos - x2 * sin, x2 * cos + x1 * sin], -1).astype(x.dtype)
    return jnp.concatenate([rot, x[..., rd:]], -1)

def nsa_inv_freq():
    return jnp.power(jnp.float32(ROPE_THETA), -jnp.arange(0, ROT_DIM, 2, dtype=jnp.float32) / ROT_DIM)

def conformer_conv(a, b, dw, db, ln_g, ln_b, w_pw):
    u = a * jax.nn.sigmoid(b)
    u = lax.conv_general_dilated(u, dw[:, None, :], window_strides=(1,),
                                 padding=[(CONV_WIDTH - 1, 0)],
                                 dimension_numbers=("NWC", "WIO", "NWC"),
                                 feature_group_count=CONV_CH) + db
    u = jax.nn.silu(layer_norm(u, ln_g, ln_b))
    return u @ w_pw

def retention(q, k, v, g, pos, w_o):
    B, T, _ = q.shape
    H, C = RET_HEADS, RET_CHUNK
    nc = T // C
    inv = 1.0 / jnp.power(jnp.float32(RET_ROPE_BASE), jnp.linspace(0.0, 1.0, RET_DK // 2, dtype=jnp.float32))
    q = rope(q.reshape(B, T, H, RET_DK), pos, inv)
    k = rope(k.reshape(B, T, H, RET_DK), pos, inv) * (RET_DK ** -0.5)
    v = v.reshape(B, T, H, RET_DV)
    log_gamma = jnp.log1p(-jnp.exp2(-5.0 - jnp.arange(H, dtype=jnp.float32)))
    idx = jnp.arange(C, dtype=jnp.float32)
    diff = idx[:, None] - idx[None, :]
    dmat = jnp.where(diff >= 0, jnp.exp(log_gamma[:, None, None] * jnp.maximum(diff, 0.0)), 0.0).astype(q.dtype)
    xi = jnp.exp(log_gamma[:, None] * (idx + 1.0)).astype(q.dtype)
    zeta = jnp.exp(log_gamma[:, None] * (C - 1.0 - idx)).astype(q.dtype)
    chunk_decay = jnp.exp(log_gamma * C).astype(q.dtype)

    def chunks(t, d):
        return t.reshape(B, nc, C, H, d).transpose(1, 0, 3, 2, 4)

    def step(R, inp):
        qi, ki, vi = inp
        inner = jnp.einsum("bhcd,bhsd->bhcs", qi, ki) * dmat
        o = (jnp.einsum("bhcs,bhsv->bhcv", inner, vi)
             + jnp.einsum("bhcd,bhdv->bhcv", qi, R) * xi[None, :, :, None])
        R = R * chunk_decay[None, :, None, None] + jnp.einsum(
            "bhsd,bhsv->bhdv", ki, vi * zeta[None, :, :, None])
        return R, o

    R0 = jnp.zeros((B, H, RET_DK, RET_DV), q.dtype)
    _, o = lax.scan(step, R0, (chunks(q, RET_DK), chunks(k, RET_DK), chunks(v, RET_DV)))
    o = o.transpose(1, 0, 3, 2, 4).reshape(B, T, H, RET_DV)
    of = o.astype(jnp.float32)
    mu = jnp.mean(of, -1, keepdims=True)
    var = jnp.mean(jnp.square(of - mu), -1, keepdims=True)
    o = ((of - mu) * lax.rsqrt(var + LN_EPS)).astype(v.dtype).reshape(B, T, H * RET_DV)
    return (jax.nn.silu(g) * o) @ w_o

def nsa(q, kc, vc, ks, vs, kw, vw, gl, pos, pe_k, w1_k, w2_k, pe_v, w1_v, w2_v, w_o):
    B, T, _ = q.shape
    G, HPG, DH = NSA_GROUPS, NSA_HPG, NSA_DH
    inv = nsa_inv_freq()
    q = (rope(q.reshape(B, T, NSA_HEADS, DH), pos, inv) * (DH ** -0.5)).reshape(B, T, G, HPG, DH)
    t_idx = np.arange(T)

    n_cmp = (T - CMP_BLOCK) // CMP_STRIDE + 1
    blk_idx = np.arange(n_cmp)[:, None] * CMP_STRIDE + np.arange(CMP_BLOCK)[None, :]
    end = blk_idx[:, -1]

    def compress(t, pe, w1, w2):
        tb = t.reshape(B, T, G, DH)[:, blk_idx] + pe[None, None, :, None, :]
        tb = tb.transpose(0, 1, 3, 2, 4).reshape(B, n_cmp, G, CMP_BLOCK * DH)
        return jax.nn.silu(tb @ w1) @ w2

    k_cmp = rope(compress(kc, pe_k, w1_k, w2_k), pos[:, end], inv)
    v_cmp = compress(vc, pe_v, w1_v, w2_v)
    cmp_ok = end[None, :] <= t_idx[:, None]
    s = jnp.einsum("btghd,bngd->bghtn", q, k_cmp).astype(jnp.float32)
    p = jnp.where(cmp_ok, jax.nn.softmax(jnp.where(cmp_ok, s, NEG), axis=-1), 0.0)
    o_cmp = jnp.einsum("bghtn,bngd->btghd", p.astype(v_cmp.dtype), v_cmp)

    n_sel = T // SEL_BLOCK
    topk = min(SEL_TOPK, n_sel)
    ii = np.arange(n_cmp)[:, None]
    jj = np.arange(n_sel)[None, :]
    lo = np.maximum(ii * CMP_STRIDE, jj * SEL_BLOCK)
    hi = np.minimum(ii * CMP_STRIDE + CMP_BLOCK, (jj + 1) * SEL_BLOCK)
    overlap = jnp.asarray(np.maximum(hi - lo, 0).astype(np.float32) / CMP_BLOCK)
    imp = jnp.einsum("bghtn,nj->bgtj", p, overlap)
    cur = t_idx // SEL_BLOCK
    jsel = np.arange(n_sel)[None, :]
    eligible = jsel <= cur[:, None]
    forced = (jsel == 0) | (jsel == cur[:, None]) | (jsel == cur[:, None] - 1)
    imp = jnp.where(forced, jnp.inf, jnp.where(eligible, imp, -jnp.inf))
    _, sel_idx = lax.top_k(imp, topk)

    ks = rope(ks.reshape(B, T, G, DH), pos, inv)
    ks_blocks = ks.reshape(B, n_sel, SEL_BLOCK, G, DH).transpose(0, 3, 1, 2, 4)
    vs_blocks = vs.reshape(B, n_sel, SEL_BLOCK, G, DH).transpose(0, 3, 1, 2, 4)
    nqb = T // SEL_QBLOCK
    q_sb = q.reshape(B, nqb, SEL_QBLOCK, G, HPG, DH).transpose(1, 0, 2, 3, 4, 5)
    idx_sb = sel_idx.reshape(B, G, nqb, SEL_QBLOCK, topk).transpose(2, 0, 1, 3, 4)
    t0_sb = jnp.arange(nqb, dtype=jnp.int32) * SEL_QBLOCK
    bi = jnp.arange(B)[:, None, None, None]
    gi = jnp.arange(G)[None, :, None, None]

    def sel_block(args):
        qb, ib, t0 = args
        kg = ks_blocks[bi, gi, ib].reshape(B, G, SEL_QBLOCK, topk * SEL_BLOCK, DH)
        vg = vs_blocks[bi, gi, ib].reshape(B, G, SEL_QBLOCK, topk * SEL_BLOCK, DH)
        tok = (ib[..., None] * SEL_BLOCK + jnp.arange(SEL_BLOCK)).reshape(B, G, SEL_QBLOCK, topk * SEL_BLOCK)
        tq = t0 + jnp.arange(SEL_QBLOCK)
        ok = (tok <= tq[None, None, :, None])[:, :, None]
        sc = jnp.einsum("bqghd,bgqsd->bghqs", qb, kg).astype(jnp.float32)
        pr = jax.nn.softmax(jnp.where(ok, sc, NEG), axis=-1)
        return jnp.einsum("bghqs,bgqsd->bqghd", pr.astype(vg.dtype), vg)

    o_slc = lax.map(sel_block, (q_sb, idx_sb, t0_sb))
    o_slc = o_slc.transpose(1, 0, 2, 3, 4, 5).reshape(B, T, G, HPG, DH)

    kw = rope(kw.reshape(B, T, G, DH), pos, inv)
    kw_pad = jnp.pad(kw, ((0, 0), (WINDOW, 0), (0, 0), (0, 0)))
    vw_pad = jnp.pad(vw.reshape(B, T, G, DH), ((0, 0), (WINDOW, 0), (0, 0), (0, 0)))
    nwb = T // WIN_QBLOCK
    span = WINDOW + WIN_QBLOCK
    q_wb = q.reshape(B, nwb, WIN_QBLOCK, G, HPG, DH).transpose(1, 0, 2, 3, 4, 5)
    t0_wb = jnp.arange(nwb, dtype=jnp.int32) * WIN_QBLOCK

    def win_block(args):
        qb, t0 = args
        kb = lax.dynamic_slice_in_dim(kw_pad, t0, span, axis=1)
        vb = lax.dynamic_slice_in_dim(vw_pad, t0, span, axis=1)
        tq = t0 + jnp.arange(WIN_QBLOCK)
        tk = t0 - WINDOW + jnp.arange(span)
        d = tq[:, None] - tk[None, :]
        ok = (d >= 0) & (d < WINDOW) & (tk[None, :] >= 0)
        sc = jnp.einsum("bqghd,bsgd->bghqs", qb, kb).astype(jnp.float32)
        pr = jax.nn.softmax(jnp.where(ok, sc, NEG), axis=-1)
        return jnp.einsum("bghqs,bsgd->bqghd", pr.astype(vb.dtype), vb)

    o_win = lax.map(win_block, (q_wb, t0_wb))
    o_win = o_win.transpose(1, 0, 2, 3, 4, 5).reshape(B, T, G, HPG, DH)

    gates = jax.nn.sigmoid(gl).reshape(B, T, G, HPG, NSA_N_BRANCH)
    o = gates[..., 0, None] * o_cmp + gates[..., 1, None] * o_slc + gates[..., 2, None] * o_win
    return o.reshape(B, T, NSA_HEADS * DH) @ w_o

def hybrid_mixer(x, pos, w_in, conv_dw, conv_db, conv_ln_g, conv_ln_b, conv_w_pw, ret_w_o,
                 pe_k, w1_k, w2_k, pe_v, w1_v, w2_v, nsa_w_o, w_out):
    B, T, D = x.shape
    z = x @ w_in
    splits = [int(c) for c in np.cumsum(IN_WIDTHS)[:-1]]
    (c_a, c_b, r_q, r_k, r_v, r_g, n_q, n_kc, n_vc, n_ks, n_vs, n_kw, n_vw, n_g, m_g) = jnp.split(z, splits, axis=-1)
    y_conv = conformer_conv(c_a, c_b, conv_dw, conv_db, conv_ln_g, conv_ln_b, conv_w_pw)
    y_ret = retention(r_q, r_k, r_v, r_g, pos, ret_w_o)
    y_nsa = nsa(n_q, n_kc, n_vc, n_ks, n_vs, n_kw, n_vw, n_g, pos, pe_k, w1_k, w2_k, pe_v, w1_v, w2_v, nsa_w_o)
    gm = jax.nn.sigmoid(m_g).reshape(B, T, N_BRANCHES, D)
    m = gm[:, :, 0] * y_conv + gm[:, :, 1] * y_ret + gm[:, :, 2] * y_nsa
    return m @ w_out

def moe(x, router_w, router_b, w1, w3, w2, ws1, ws3, ws2):
    B, T, D = x.shape
    N = B * T
    xt = x.reshape(N, D)
    s = jax.nn.sigmoid((xt @ router_w).astype(jnp.float32))
    sb = s + router_b.astype(jnp.float32)
    per_group = N_EXPERTS // N_EXPERT_GROUPS
    grp_score = lax.top_k(sb.reshape(N, N_EXPERT_GROUPS, per_group), 2)[0].sum(-1)
    _, gidx = lax.top_k(grp_score, TOPK_GROUPS)
    gmask = jnp.sum(jax.nn.one_hot(gidx, N_EXPERT_GROUPS, dtype=jnp.float32), -2) > 0
    emask = jnp.repeat(gmask, per_group, axis=-1)
    _, eidx = lax.top_k(jnp.where(emask, sb, -jnp.inf), TOPK)
    w = jnp.take_along_axis(s, eidx, -1)
    w = w / jnp.sum(w, -1, keepdims=True) * ROUTED_SCALE
    gates = jnp.sum(jax.nn.one_hot(eidx, N_EXPERTS, dtype=jnp.float32) * w[..., None], -2).astype(x.dtype)
    nb = N // MOE_TOKEN_BLOCK

    def block(args):
        xb, gb = args
        h = jax.nn.silu(jnp.einsum("nd,edf->nef", xb, w1)) * jnp.einsum("nd,edf->nef", xb, w3)
        return jnp.einsum("nef,efd->nd", h * gb[..., None], w2)

    y = lax.map(block, (xt.reshape(nb, MOE_TOKEN_BLOCK, D), gates.reshape(nb, MOE_TOKEN_BLOCK, N_EXPERTS)))
    shared = (jax.nn.silu(xt @ ws1) * (xt @ ws3)) @ ws2
    return (y.reshape(N, D) + shared).reshape(B, T, D)

def setup_inputs(seed: int = 0) -> dict:
    key = jax.random.key(seed)
    ks = jax.random.split(key, 32)
    L, D = DEPTH, D_MODEL

    def nrm(k, shape, scale):
        return jax.random.normal(k, shape, jnp.float32) * scale

    return {
        "x": nrm(ks[0], (BATCH, SEQ, D), 1.0),
        "positions": jnp.arange(SEQ, dtype=jnp.int32)[None, :]
                     + jax.random.randint(ks[1], (BATCH, 1), 0, 1024, dtype=jnp.int32),
        "w_in": nrm(ks[2], (L, D, D_IN), D ** -0.5),
        "conv_dw": nrm(ks[3], (L, CONV_WIDTH, CONV_CH), CONV_WIDTH ** -0.5),
        "conv_db": nrm(ks[4], (L, CONV_CH), 0.01),
        "conv_ln_g": 1.0 + nrm(ks[5], (L, CONV_CH), 0.01),
        "conv_ln_b": nrm(ks[6], (L, CONV_CH), 0.01),
        "conv_w_pw": nrm(ks[7], (L, CONV_CH, D), DN_BETA * CONV_CH ** -0.5),
        "ret_w_o": nrm(ks[8], (L, RET_HEADS * RET_DV, D), DN_BETA * (RET_HEADS * RET_DV) ** -0.5),
        "nsa_pe_k": nrm(ks[9], (L, CMP_BLOCK, NSA_DH), 0.1),
        "nsa_w1_k": nrm(ks[10], (L, CMP_BLOCK * NSA_DH, CMP_HIDDEN), (CMP_BLOCK * NSA_DH) ** -0.5),
        "nsa_w2_k": nrm(ks[11], (L, CMP_HIDDEN, NSA_DH), CMP_HIDDEN ** -0.5),
        "nsa_pe_v": nrm(ks[12], (L, CMP_BLOCK, NSA_DH), 0.1),
        "nsa_w1_v": nrm(ks[13], (L, CMP_BLOCK * NSA_DH, CMP_HIDDEN), (CMP_BLOCK * NSA_DH) ** -0.5),
        "nsa_w2_v": nrm(ks[14], (L, CMP_HIDDEN, NSA_DH), CMP_HIDDEN ** -0.5),
        "nsa_w_o": nrm(ks[15], (L, NSA_HEADS * NSA_DH, D), DN_BETA * (NSA_HEADS * NSA_DH) ** -0.5),
        "w_out": nrm(ks[16], (L, D, D), DN_BETA * D ** -0.5),
        "ln1_g": 1.0 + nrm(ks[17], (L, D), 0.01),
        "ln1_b": nrm(ks[18], (L, D), 0.01),
        "router_w": nrm(ks[19], (L, D, N_EXPERTS), D ** -0.5),
        "router_b": nrm(ks[20], (L, N_EXPERTS), 0.01),
        "moe_w1": nrm(ks[21], (L, N_EXPERTS, D, D_EXPERT), DN_BETA * D ** -0.5),
        "moe_w3": nrm(ks[22], (L, N_EXPERTS, D, D_EXPERT), DN_BETA * D ** -0.5),
        "moe_w2": nrm(ks[23], (L, N_EXPERTS, D_EXPERT, D), DN_BETA * D_EXPERT ** -0.5),
        "shared_w1": nrm(ks[24], (L, D, D_SHARED), DN_BETA * D ** -0.5),
        "shared_w3": nrm(ks[25], (L, D, D_SHARED), DN_BETA * D ** -0.5),
        "shared_w2": nrm(ks[26], (L, D_SHARED, D), DN_BETA * D_SHARED ** -0.5),
        "ln2_g": 1.0 + nrm(ks[27], (L, D), 0.01),
        "ln2_b": nrm(ks[28], (L, D), 0.01),
    }

def reference(x, positions, w_in, conv_dw, conv_db, conv_ln_g, conv_ln_b, conv_w_pw, ret_w_o,
              nsa_pe_k, nsa_w1_k, nsa_w2_k, nsa_pe_v, nsa_w1_v, nsa_w2_v, nsa_w_o, w_out,
              ln1_g, ln1_b, router_w, router_b, moe_w1, moe_w3, moe_w2,
              shared_w1, shared_w3, shared_w2, ln2_g, ln2_b):
    for l in range(DEPTH):
        h = hybrid_mixer(x, positions, w_in[l], conv_dw[l], conv_db[l], conv_ln_g[l], conv_ln_b[l],
                         conv_w_pw[l], ret_w_o[l], nsa_pe_k[l], nsa_w1_k[l], nsa_w2_k[l],
                         nsa_pe_v[l], nsa_w1_v[l], nsa_w2_v[l], nsa_w_o[l], w_out[l])
        x = layer_norm(DN_ALPHA * x + h, ln1_g[l], ln1_b[l])
        h = moe(x, router_w[l], router_b[l], moe_w1[l], moe_w3[l], moe_w2[l],
                shared_w1[l], shared_w3[l], shared_w2[l])
        x = layer_norm(DN_ALPHA * x + h, ln2_g[l], ln2_b[l])
    return x


_drawn_inputs = setup_inputs


def setup_inputs(seed=0):
    import zlib

    import numpy as np

    out = dict(_drawn_inputs(seed))
    spreads = {}
    factors = {'conv_db': 8.0,
     'conv_ln_g': 8.0,
     'conv_ln_b': 8.0,
     'nsa_pe_k': 8.0,
     'nsa_w1_k': 5.811,
     'nsa_w2_k': 6.148,
     'nsa_pe_v': 8.0,
     'ln1_g': 3.414,
     'ln1_b': 3.609,
     'router_b': 3.895,
     'ln2_g': 3.775,
     'ln2_b': 3.66}
    for name, (base, spread) in spreads.items():
        noise = np.random.default_rng([zlib.crc32(name.encode()), seed]).standard_normal(out[name].shape)
        drawn = base * np.exp(spread * noise) if base else spread * noise
        out[name] = __import__('jax').numpy.asarray(drawn.astype(out[name].dtype))
    for name, factor in factors.items():
        out[name] = (out[name] * factor).astype(out[name].dtype)
    return out
```

```python
from contextlib import ExitStack

import numpy as np

import concourse.bass as bass
from concourse import mybir

F32 = mybir.dt.float32
I32 = mybir.dt.int32
ALU = mybir.AluOpType
ACT = mybir.ActivationFunctionType
AX = mybir.AxisListType

P = 128
L = 2
T = 256
TT = T // P
D = 1024
KD = D // P
CH = 512
KC = CH // P
TAPS = 31
RH, RDK, RDV = 4, 128, 256
NH, NG, DH = 8, 2, 64
HPG = NH // NG
CB, CS = 32, 16
NCMP = (T - CB) // CS + 1
CHID = 256
ROT = DH // 4
NE, NEG_, TOPG, TOPK = 64, 8, 4, 8
FE = 256
SCALE_ROUTED = 2.5
ALPHA = (2.0 * L) ** 0.25
EPS = 1e-5
NEG = -1e30
BANK = 512

WIDTHS = (CH, CH, RH * RDK, RH * RDK, RH * RDV, RH * RDV, NH * DH) + (NG * DH,) * 6 + (NH * 3, 3 * D)
(Z_CA, Z_CB, Z_RQ, Z_RK, Z_RV, Z_RG, Z_NQ, Z_KC, Z_VC, Z_KS, Z_VS, Z_KW, Z_VW, Z_NG, Z_MG, D_IN) = \
    [sum(WIDTHS[:i]) for i in range(len(WIDTHS) + 1)]
FULL_BLOCKS = D_IN // BANK
LAST_COLS = D_IN - FULL_BLOCKS * BANK

ITEMS = ["in"] * (FULL_BLOCKS + 1) + ["conv_pw", "ret_o0", "ret_o1", "w1_k0", "w1_k1", "w1_v0", "w1_v1",
                                      "nsa_o", "out0", "out1"]
RING = 2
SLOT = KD * BANK
EXPERT = 3 * KD * FE
E_SLOTS = 4
E_ALL = NE + 1
Z0 = RING * SLOT
ARENA = max(Z0 + TT * D_IN, E_SLOTS * EXPERT)

CHAN_ROWS = TAPS + 3
RF = RDK // 2
NF = ROT // 2
FR = RF + NF
CONSTS = {"ident": P, "decay": RH * 3 * P, "mask": 2 * P, "cmp_add": TT * NCMP, "cmp_01": TT * NCMP, "freq": FR}


def shape_constants():
    f = np.float32
    p = np.arange(P)
    out = {"ident": np.eye(P, dtype=f)}
    log_gamma = np.log1p(-np.exp2(f(-5.0) - np.arange(RH, dtype=f))).astype(f)
    diff = np.arange(T)[None, :] - p[:, None]
    full = np.where(diff >= 0, np.exp(log_gamma[:, None, None] * np.maximum(diff, 0).astype(f)), 0) * f(RDK ** -0.5)
    out["decay"] = np.concatenate([full, full[:, :, :P]], 2).transpose(1, 0, 2).reshape(P, -1)
    tri = np.where(p[None, :] <= p[:, None], 0.0, NEG)
    out["mask"] = np.concatenate([np.zeros((P, P)), tri], 1)
    end = np.arange(NCMP) * CS + CB - 1
    ok = end[None, None, :] <= (np.arange(TT)[None, :, None] * P + p[:, None, None])
    out["cmp_add"] = np.where(ok, 0.0, NEG).reshape(P, -1)
    out["cmp_01"] = np.where(ok, 1.0, 0.0).reshape(P, -1)
    ret = f(1.0) / np.power(f(10000.0), np.linspace(0.0, 1.0, RF, dtype=f))
    nsa = np.power(f(500000.0), -np.arange(0, ROT, 2, dtype=f) / f(ROT))
    out["freq"] = np.tile(np.concatenate([ret, nsa])[None], (P, 1))
    return np.concatenate([out[k].reshape(P, n).astype(f) for k, n in CONSTS.items()], 1)


class Counts:

    def __init__(self, engine):
        self.engine = engine
        self.at = {}

    def done(self, ins, sem):
        ins.then_inc(sem, 1)
        self.at[sem.name] = self.at.get(sem.name, 0) + 1
        self.engine.wait_ge(sem, self.at[sem.name])


def build(nc, a, out):
    with ExitStack() as ctx:
        def sb(name, shape, dt=F32):
            return ctx.enter_context(nc.sbuf_tensor(name, shape, dt))

        def sem(name):
            return ctx.enter_context(nc.semaphore(name))

        consts = sb("consts", [P, sum(CONSTS.values())])
        c_at = dict(zip(CONSTS, np.cumsum([0] + list(CONSTS.values())).tolist()))

        def const(name):
            return consts[:, c_at[name]:c_at[name] + CONSTS[name]]

        ident = const("ident")
        decay = const("decay").rearrange("p (h c) -> p h c", h=RH)
        mask = const("mask")
        cmp_add = const("cmp_add").rearrange("p (t n) -> p t n", t=TT)
        cmp_01 = const("cmp_01").rearrange("p (t n) -> p t n", t=TT)
        arena = sb("arena", [P, ARENA])
        ring = arena[:, 0:RING * SLOT].rearrange("p (s n) -> p s n", s=RING)
        z = arena[:, Z0:Z0 + TT * D_IN].rearrange("p (t n) -> p t n", t=TT)
        experts = arena[:, 0:E_SLOTS * EXPERT].rearrange("p (s n) -> p s n", s=E_SLOTS)
        x = sb("x", [P, TT, D])
        xT = sb("xT", [P, KD, T])
        yT = sb("yT", [P, KD, T])
        norm = sb("norm", [P, 4, D])
        qkT = sb("qkT", [P, RH, 2, T])
        nqT = sb("nqT", [DH, TT, NH, P])
        nkT = sb("nkT", [DH, 2, NG, T])
        cT = sb("cT", [DH, 2, NG, T])
        shared_buf = sb("shared_buf", [P, 2 * CB * NG * NCMP + 8])
        blocks_kv = shared_buf[0:DH, 0:2 * CB * NG * NCMP].rearrange("p (v c g n) -> p v c g n", v=2, c=CB, g=NG)
        u_pad = shared_buf[:, 0:KC * (TAPS - 1 + T)].rearrange("p (k t) -> p k t", k=KC)
        E = sb("E", [P, 2, 4 * T])
        conv_acc = E[:, 0, :].rearrange("p (k t) -> p k t", k=KC)
        PT = sb("PT", [P, 4 * T])
        ret_p = PT[:, 0:2 * 3 * P].rearrange("p (b c) -> p b c", b=2)
        chan = sb("chan", [P, KC, CHAN_ROWS])
        chan_raw = sb("chan_raw", [CHAN_ROWS, CH])
        pe_raw = sb("pe_raw", [CB, 2, DH])
        peT = sb("peT", [DH, 2, CB])
        w2_kv = sb("w2_kv", [P, 2, 2, DH])
        hidT = sb("hidT", [P, 2, 2, NG * NCMP])
        k_cmp = sb("k_cmp", [NG * NCMP, DH])
        k_cmpT = sb("k_cmpT", [DH, NG * NCMP])
        v_cmp = sb("v_cmp", [NCMP, NG, DH])
        pcT = yT[0:NCMP, :, :].rearrange("p k t -> p (k t)").rearrange("p (t h q) -> p t h q", t=TT, h=NH)
        Ec = sb("Ec", [P, TT, NH, NCMP])
        pos_i = sb("pos_i", [P, TT + 1], I32)
        pos = sb("pos", [P, TT + 1])
        cos = sb("cos", [P, TT + 1, FR])
        sin = sb("sin", [P, TT + 1, FR])
        turn_n = sb("turn_n", [P, TT + 1, FR])
        stats = sb("stats", [P, 2 * RH * TT, 6])
        mv = sb("mv", [P, 2 * RH, 2])
        rstd = sb("rstd", [P, 2 * RH])
        negmax = sb("negmax", [P, TT * NH])
        den = sb("den", [P, 2 * TT * NG, HPG])
        coef = sb("coef", [P, TT * NH])
        router_w = sb("router_w", [P, KD, NE])
        router_b = sb("router_b", [P, NE])
        score = sb("score", [P, TT, NE])
        biased = sb("biased", [P, TT, NE])
        best = sb("best", [P, TT, NEG_, 8])
        group = sb("group", [P, TT, NEG_ + 8 - TOPG])
        group_out = sb("group_out", [P, TT, NEG_ + 8 - TOPG])
        top = sb("top", [P, 8])
        marked = sb("marked", [P, TT, NE])
        total = sb("total", [P, TT])
        gates = sb("gates", [P, TT, E_ALL])
        silu_a = sb("silu_a", [P, TT, FE])
        hidden = qkT[:, 0, :, :]
        hiddenT = qkT[:, 1, :, :]

        ps = ctx.enter_context(nc.psum_tensor("ps", [P, 8, BANK], F32))

        def banks(b, n):
            return ps[:, b:b + n, :].rearrange("p b n -> p (b n)")

        boot = sem("boot")
        boot_dma = sem("boot_dma")
        boot_step = sem("boot_step")
        boot_sin = sem("boot_sin")
        engine_at_end = sem("engine_at_end")
        all_at_end = sem("all_at_end")
        layer_open = sem("layer_open")
        layer_entered = sem("layer_entered")
        sp_passed = sem("sp_passed")
        stored = sem("stored")
        layer_sems = []

        def lsem(name):
            layer_sems.append(sem(name))
            return layer_sems[-1]

        ring_loaded = [lsem(f"ring_loaded{s}") for s in range(RING)]
        item_done = lsem("item_done")
        chan_loaded, pe_loaded, w2_loaded = lsem("chan_loaded"), lsem("pe_loaded"), lsem("w2_loaded")
        norm_loaded, router_loaded = lsem("norm_loaded"), lsem("router_loaded")
        dve_step, act_step, pool_step = lsem("dve_step"), lsem("act_step"), lsem("pool_step")
        x_turned = lsem("x_turned")
        xT_act, xT_dve = lsem("xT_act"), lsem("xT_dve")
        z_written = lsem("z_written")
        conv_gate = lsem("conv_gate")
        u_ready, u_turned, uT_ready = lsem("u_ready"), lsem("u_turned"), lsem("uT_ready")
        params_turned, params_ready = lsem("params_turned"), lsem("params_ready")
        pad_zeroed = lsem("pad_zeroed")
        conv_tap = lsem("conv_tap")
        conv_back = lsem("conv_back")
        var_ready, std_ready = lsem("var_ready"), lsem("std_ready")
        conv_normed, conv_turned, conv_silu = lsem("conv_normed"), lsem("conv_turned"), lsem("conv_silu")
        gates_ready, ret_gate_ready = lsem("gates_ready"), lsem("ret_gate_ready")
        y_taken = lsem("y_taken")
        ret_roped, nsa_roped = lsem("ret_roped"), lsem("nsa_roped")
        qk_turned, qk_ready = lsem("qk_turned"), lsem("qk_ready")
        ret_scores, ret_masked, ret_o, ret_o_copied = \
            lsem("ret_scores"), lsem("ret_masked"), lsem("ret_o"), lsem("ret_o_copied")
        ret_gated, ret_turned, yT_act, yT_dve = \
            lsem("ret_gated"), lsem("ret_turned"), lsem("yT_act"), lsem("yT_dve")
        nq_turned, nq_ready, nk_turned, nk_act, nk_dve = \
            lsem("nq_turned"), lsem("nq_ready"), lsem("nk_turned"), lsem("nk_act"), lsem("nk_dve")
        blocks_ready, hid_ready = lsem("blocks_ready"), lsem("hid_ready")
        kv_cmp_done, kv_cmp_ready, k_cmp_turned, k_cmp_ready = \
            lsem("kv_cmp_done"), lsem("kv_cmp_ready"), lsem("k_cmp_turned"), lsem("k_cmp_ready")
        cmp_scores, cmp_shifted, cmp_exp, cmp_p, cmp_turned, cmp_pT, cmp_o, cmp_o_taken = \
            [lsem(f"cmp_{n}") for n in ("scores", "shifted", "exp", "p", "turned", "pT", "o", "o_taken")]
        at_scores, at_masked, at_max, at_exp, at_turned, at_pT, at_o, at_o_taken = \
            [lsem(f"at_{n}") for n in ("scores", "masked", "max", "exp", "turned", "pT", "o", "o_taken")]
        nsa_ready, nsa_turned, nsa_oT = lsem("nsa_ready"), lsem("nsa_turned"), lsem("nsa_oT")
        m_ready, m_turned, mT_act, mT_dve = lsem("m_ready"), lsem("m_turned"), lsem("mT_act"), lsem("mT_dve")
        x1_ready, x1_turned, x1T_act, x1T_dve = \
            lsem("x1_ready"), lsem("x1_turned"), lsem("x1T_act"), lsem("x1T_dve")
        router_done, score_ready = lsem("router_done"), lsem("score_ready")
        expert_loaded = [lsem(f"expert_loaded{s}") for s in range(E_SLOTS)]
        up_done = lsem("up_done")
        silu_done = lsem("silu_done")
        hidden_done = lsem("hidden_done")
        hidden_turned = lsem("hidden_turned")
        hiddenT_ready = lsem("hiddenT_ready")
        expert_used = lsem("expert_used")
        numbers = [s.num for s in layer_sems]
        assert numbers == list(range(numbers[0], numbers[-1] + 1))

        w_in = a["w_in"].rearrange("l (p k) n -> l p k n", k=KD)
        moe_w1 = a["moe_w1"].rearrange("l e (p k) f -> l e p k f", k=KD)
        moe_w3 = a["moe_w3"].rearrange("l e (p k) f -> l e p k f", k=KD)
        moe_w2 = a["moe_w2"].rearrange("l e (p j) n -> l e p j n", j=2)

        at = {name: n for n, name in enumerate(ITEMS)}

        def ring_slot(item):
            return ring[:, item % RING, :]

        def expert_parts(s):
            w = experts[:, s, :]
            n = KD * FE
            return (w[:, 0:n].rearrange("p (k f) -> p k f", k=KD), w[:, n:2 * n].rearrange("p (k f) -> p k f", k=KD),
                    w[:, 2 * n:3 * n].rearrange("p (j n) -> p j n", j=2))

        m_buf = z[:, :, 0:D]
        ret_out = z[:, :, Z_RQ:Z_RQ + RH * RDV]
        nsa_out = z[:, :, Z_NQ:Z_NQ + NH * DH]
        UNITS = [(br, tt, g) for br in range(2) for tt in range(TT) for g in range(NG)]

        def layer_end(eng, l):
            eng.sem_inc(engine_at_end, 1)
            eng.wait_ge(layer_open, l + 2)
            eng.sem_inc(layer_entered, 1)

        block = ctx.enter_context(nc.Block())

        @block.sync
        def _(sp):
            sp.dma_start(x[:, :, :], a["x"].rearrange("b (t p) d -> p (b t) d", p=P)).then_inc(boot, 16)
            sp.wait_ge(layer_open, 1)
            with sp.Fori(0, L) as l:
                for n in range(2):
                    sp.dma_start(ring_slot(n).rearrange("p (k n) -> p k n", k=KD),
                                 w_in[l, :, :, n * BANK:(n + 1) * BANK]).then_inc(ring_loaded[n], 16)
                sp.dma_start(chan_raw[0:TAPS, :], a["conv_dw"][l]).then_inc(chan_loaded, 16)
                for i, n in enumerate(("conv_db", "conv_ln_g", "conv_ln_b")):
                    sp.dma_start(chan_raw[TAPS + i:TAPS + i + 1, :], a[n][bass.ds(l, 1), :]).then_inc(chan_loaded, 16)
                for i, v in enumerate("kv"):
                    sp.dma_start(pe_raw[:, i, :], a[f"nsa_pe_{v}"][l]).then_inc(pe_loaded, 16)
                    sp.dma_start(w2_kv[:, i, :, :], a[f"nsa_w2_{v}"].rearrange("l (h p) d -> l p h d", p=P)[l]) \
                        .then_inc(w2_loaded, 16)
                for i, n in enumerate(("ln1_g", "ln1_b", "ln2_g", "ln2_b")):
                    sp.dma_start(norm[:, i, :], a[n][bass.ds(l, 1), :].to_broadcast([P, D])).then_inc(norm_loaded, 16)
                sp.dma_start(router_w[:, :, :], a["router_w"].rearrange("l (p k) e -> l p k e", k=KD)[l]) \
                    .then_inc(router_loaded, 16)
                sp.dma_start(router_b[:, :], a["router_b"][bass.ds(l, 1), :].to_broadcast([P, NE])) \
                    .then_inc(router_loaded, 16)
                with sp.Fori(0, (FULL_BLOCKS - 2) // 2) as i:
                    for j in range(2):
                        sp.wait_ge(item_done, 2 * i + j + 1)
                        sp.sem_inc(sp_passed, 1)
                        sp.dma_start(ring_slot(j).rearrange("p (k n) -> p k n", k=KD),
                                     w_in[l, :, :, bass.ds(i * (2 * BANK) + (j + 2) * BANK, BANK)]) \
                            .then_inc(ring_loaded[j], 16)
                sources = {
                    "in": (w_in[l, :, :, FULL_BLOCKS * BANK:D_IN], LAST_COLS),
                    "conv_pw": (a["conv_w_pw"].rearrange("l (p k) n -> l p k n", k=KC)[l], D),
                    "nsa_o": (a["nsa_w_o"].rearrange("l (p k) n -> l p k n", k=KC)[l], D),
                }
                for h in range(2):
                    cols = slice(h * BANK, (h + 1) * BANK)
                    sources[f"ret_o{h}"] = (a["ret_w_o"].rearrange("l (p k) n -> l p k n", k=KD)[l, :, :, cols], BANK)
                    sources[f"out{h}"] = (a["w_out"].rearrange("l (p k) n -> l p k n", k=KD)[l, :, :, cols], BANK)
                    for v in "kv":
                        w1 = a[f"nsa_w1_{v}"].rearrange("l (c d) h -> l d c h", d=DH)
                        sources[f"w1_{v}{h}"] = (w1[l, :, h * CB // 2:(h + 1) * CB // 2, :], CHID)
                for n in range(FULL_BLOCKS, len(ITEMS)):
                    src, cols = sources[ITEMS[n]]
                    parts, k = src.shape[0], src.shape[1]
                    sp.wait_ge(item_done, n - RING + 1)
                    sp.dma_start(ring_slot(n)[0:parts, 0:k * cols].rearrange("p (k n) -> p k n", k=k), src) \
                        .then_inc(ring_loaded[n % RING], 16)

                def load_expert(s, w1, w3, w2):
                    for dst, src in zip(expert_parts(s), (w1, w3, w2)):
                        sp.dma_start(dst, src).then_inc(expert_loaded[s], 16)

                sp.wait_ge(item_done, len(ITEMS))
                load_expert(0, a["shared_w1"].rearrange("l (p k) f -> l p k f", k=KD)[l],
                            a["shared_w3"].rearrange("l (p k) f -> l p k f", k=KD)[l],
                            a["shared_w2"].rearrange("l (p j) n -> l p j n", j=2)[l])
                for e in range(1, E_SLOTS):
                    load_expert(e, moe_w1[l, e - 1], moe_w3[l, e - 1], moe_w2[l, e - 1])
                with sp.Fori(0, NE // E_SLOTS - 1) as i:
                    for s in range(E_SLOTS):
                        sp.wait_ge(expert_used, i * E_SLOTS + s + 1)
                        sp.sem_inc(sp_passed, 1)
                        e = i * E_SLOTS + (E_SLOTS + s - 1)
                        load_expert(s, moe_w1[l, e], moe_w3[l, e], moe_w2[l, e])
                sp.wait_ge(expert_used, NE - E_SLOTS + 1)
                load_expert(0, moe_w1[l, NE - 1], moe_w3[l, NE - 1], moe_w2[l, NE - 1])
                layer_end(sp, l)
            sp.dma_start(out.rearrange("b (t p) d -> p (b t) d", p=P), x[:, :, :]).then_inc(stored, 16)
            sp.wait_ge(stored, 16)

        @block.gpsimd
        def _(pool):
            pool.dma_start(consts[:, :], a["consts"]).then_inc(boot_dma, 16)
            pool.memset(pos_i[:, :], 0).then_inc(boot_step, 1)
            pool.wait_ge(boot_step, 1)
            pool.dma_start(pos_i[:, 0:TT], a["positions"].rearrange("b (t p) -> p (b t)", p=P),
                           allow_slow_non_contiguous=True).then_inc(boot_dma, 16)
            ends = a["positions"].rearrange("b (n s) -> (b n) s", s=CS)[1:1 + NCMP, CS - 1:CS]
            for g in range(NG):
                pool.dma_start(pos_i[g * NCMP:(g + 1) * NCMP, TT:TT + 1], ends, allow_slow_non_contiguous=True).then_inc(boot_dma, 16)
            pool.sem_inc(layer_open, 1)
            with pool.Fori(0, L) as l:
                pool.wait_ge(engine_at_end, 4 * l + 4)
                pool.sem_inc(all_at_end, 1)
                pool.sem_clear(range(numbers[0], numbers[-1] + 1))
                pool.sem_inc(layer_open, 1)

        @block.tensor
        def _(pe):
            def turn_model(src, banks_at):
                for k in range(KD):
                    for t in range(TT):
                        last = pe.transpose(ps[:, banks_at + k // 2, (k % 2 * TT + t) * P:(k % 2 * TT + t + 1) * P],
                                            src[:, t, k::KD], ident)
                return last

            def item_ready(n):
                pe.wait_ge(ring_loaded[n % RING], 16 * (n // RING + 1))

            def project(n, pair):
                cols = BANK if n != FULL_BLOCKS else LAST_COLS
                w = ring_slot(n)[:, 0:KD * cols].rearrange("p (k n) -> p k n", k=KD)
                for t in range(TT):
                    for k in range(KD):
                        last = pe.matmul(ps[:, 2 * pair + t, 0:cols], xT[:, k, t * P:(t + 1) * P], w[:, k, :],
                                         start=(k == 0), stop=(k == KD - 1))
                last.then_inc(item_done, 1)

            def full_output(act, k_chunks, half, n):
                item_ready(n)
                w = ring_slot(n)[:, 0:k_chunks * BANK].rearrange("p (k n) -> p k n", k=k_chunks)
                for t in range(TT):
                    for k in range(k_chunks):
                        last = pe.matmul(ps[:, 2 * t + half, :], act[:, k, t * P:(t + 1) * P], w[:, k, :],
                                         start=(k == 0), stop=(k == k_chunks - 1))
                return last

            def wide_output(act, n):
                item_ready(n)
                w = ring_slot(n).rearrange("p (k n) -> p k n", k=KC)
                for t in range(TT):
                    for h in range(2):
                        for k in range(KC):
                            last = pe.matmul(ps[:, 2 * t + h, :], act[:, k, t * P:(t + 1) * P],
                                             w[:, k, h * BANK:(h + 1) * BANK], start=(k == 0), stop=(k == KC - 1))
                return last

            pe.wait_ge(boot, 16)
            pe.wait_ge(boot_dma, 64)
            pe.wait_ge(layer_open, 1)
            with pe.Fori(0, L) as l:
                turn_model(x, 4).then_inc(x_turned, 1)
                pe.wait_ge(xT_act, 1)
                pe.wait_ge(xT_dve, 1)

                def start_block(n):
                    item_ready(n)
                    if n >= 2:
                        pe.wait_ge(z_written, n - 1)
                    project(n, n % 2)

                for n in range(3):
                    start_block(n)
                pe.wait_ge(chan_loaded, 64)
                for k in range(KC):
                    pe.transpose(ps[:, 6, k * CHAN_ROWS:(k + 1) * CHAN_ROWS], chan_raw[:, k::KC],
                                 ident[0:CHAN_ROWS, 0:CHAN_ROWS])
                pe.wait_ge(pe_loaded, 32)
                for v in range(2):
                    last = pe.transpose(ps[0:DH, 7, v * CB:(v + 1) * CB], pe_raw[:, v, :], ident[0:CB, 0:CB])
                last.then_inc(params_turned, 1)
                pe.wait_ge(u_ready, 1)
                for k in range(KC):
                    for t in range(TT):
                        last = pe.transpose(ps[:, 4 + k // 2, (k % 2 * TT + t) * P:(k % 2 * TT + t + 1) * P],
                                            z[:, t, Z_CA + k:Z_CA + CH:KC], ident)
                last.then_inc(u_turned, 1)
                start_block(3)
                with pe.Fori(0, (FULL_BLOCKS - 4) // 2) as i:
                    for j in range(2):
                        pe.wait_ge(ring_loaded[j], i * 16 + 48)
                        pe.wait_ge(z_written, 2 * i + j + 3)
                        project(j, j)
                start_block(FULL_BLOCKS)

                pe.wait_ge(conv_tap, TAPS * KC)
                pe.wait_ge(uT_ready, 1)
                for t in range(TT):
                    for k in range(KC):
                        last = pe.transpose(ps[:, 4 + t, k * P:(k + 1) * P], conv_acc[:, k, t * P:(t + 1) * P], ident)
                last.then_inc(conv_back, 1)
                pe.wait_ge(ret_roped, 1)
                pe.wait_ge(params_ready, 2)
                for h in range(RH):
                    if h >= 2:
                        pe.wait_ge(qk_ready, h - 1)
                    for i, off in enumerate((Z_RQ, Z_RK)):
                        for t in range(TT):
                            last = pe.transpose(ps[:, 6 + h % 2, (i * TT + t) * P:(i * TT + t + 1) * P],
                                                z[:, t, off + h * RDK:off + (h + 1) * RDK], ident)
                    last.then_inc(qk_turned, 1)
                pe.wait_ge(conv_normed, 1)
                for k in range(KC):
                    for t in range(TT):
                        last = pe.transpose(ps[:, 4 + k // 2, (k % 2 * TT + t) * P:(k % 2 * TT + t + 1) * P],
                                            z[:, t, Z_CA + k * P:Z_CA + (k + 1) * P], ident)
                last.then_inc(conv_turned, 1)
                pe.wait_ge(conv_silu, KC)
                pe.wait_ge(z_written, FULL_BLOCKS + 1)
                wide_output(yT, at["conv_pw"]).then_inc(item_done, 1)

                def ret_score(h):
                    pe.wait_ge(qk_ready, h + 1)
                    if h >= 2:
                        pe.wait_ge(ret_masked, h - 1)
                    pe.matmul(ps[:, 4 + h % 2, 0:T], qkT[:, h, 1, 0:P], qkT[:, h, 0, :], start=True, stop=True)
                    pe.matmul(ps[:, 4 + h % 2, T:T + P], qkT[:, h, 1, P:T], qkT[:, h, 0, P:T],
                              start=True, stop=True).then_inc(ret_scores, 1)

                def ret_values(h):
                    pe.wait_ge(ret_masked, h + 1)
                    if h >= 2:
                        pe.wait_ge(ret_o_copied, h - 1)
                    o = ps[:, 6 + h % 2, :]
                    v = [z[:, t, Z_RV + h * RDV:Z_RV + (h + 1) * RDV] for t in range(TT)]
                    pe.matmul(o[:, 0:RDV], ret_p[:, h % 2, 0:P], v[0], start=True, stop=True)
                    pe.matmul(o[:, RDV:2 * RDV], ret_p[:, h % 2, P:2 * P], v[0], start=True, stop=False)
                    pe.matmul(o[:, RDV:2 * RDV], ret_p[:, h % 2, 2 * P:3 * P], v[1], start=False, stop=True) \
                        .then_inc(ret_o, 1)

                ret_score(0)
                for h in range(RH):
                    if h + 1 < RH:
                        ret_score(h + 1)
                    ret_values(h)
                pe.wait_ge(ret_gated, 1)
                turn_model(ret_out, 4).then_inc(ret_turned, 1)
                pe.wait_ge(yT_act, 1)
                pe.wait_ge(yT_dve, 1)
                pe.wait_ge(y_taken, 1)
                full_output(yT, KD, 0, at["ret_o0"]).then_inc(item_done, 1)
                full_output(yT, KD, 1, at["ret_o1"]).then_inc(item_done, 1)

                pe.wait_ge(nsa_roped, 1)
                for t in range(TT):
                    for g in range(NG):
                        for h in range(HPG):
                            c = Z_NQ + (g * HPG + h) * DH
                            last = pe.transpose(ps[0:DH, 4 + t * NG + g, h * P:(h + 1) * P], z[:, t, c:c + DH], ident)
                last.then_inc(nq_turned, 1)
                pe.wait_ge(nq_ready, 4)
                for b, off in enumerate((Z_KS, Z_KW, Z_KC, Z_VC)):
                    for g in range(NG):
                        for t in range(TT):
                            last = pe.transpose(ps[0:DH, 4 + b, (g * TT + t) * P:(g * TT + t + 1) * P],
                                                z[:, t, off + g * DH:off + (g + 1) * DH], ident)
                last.then_inc(nk_turned, 1)
                pe.wait_ge(blocks_ready, 8)
                pe.wait_ge(nk_dve, 2)
                for v, name in enumerate("kv"):
                    for c in range(CB):
                        n = at[f"w1_{name}{c * 2 // CB}"]
                        if c % (CB // 2) == 0:
                            item_ready(n)
                        w = ring_slot(n)[0:DH, :].rearrange("p (c h) -> p c h", c=CB // 2)
                        for half in range(2):
                            last = pe.matmul(ps[:, 6 + half, v * 32:v * 32 + NG * NCMP],
                                             w[:, c % (CB // 2), half * P:(half + 1) * P],
                                             blocks_kv[:, v, c, :, :], start=(c == 0), stop=(c == CB - 1))
                        if c % (CB // 2) == CB // 2 - 1:
                            last.then_inc(item_done, 1)
                pe.wait_ge(hid_ready, 2)
                pe.wait_ge(w2_loaded, 32)
                pe.wait_ge(nk_act, 2)
                for half in range(2):
                    pe.matmul(ps[0:NG * NCMP, 4, 0:DH], hidT[:, 0, half, :], w2_kv[:, 0, half, :],
                              start=(half == 0), stop=(half == 1))
                for g in range(NG):
                    for half in range(2):
                        last = pe.matmul(ps[0:NCMP, 5, g * DH:(g + 1) * DH],
                                         hidT[:, 1, half, g * NCMP:(g + 1) * NCMP], w2_kv[:, 1, half, :],
                                         start=(half == 0), stop=(half == 1))
                last.then_inc(kv_cmp_done, 1)
                pe.wait_ge(kv_cmp_ready, 1)
                pe.transpose(ps[0:DH, 6, 0:NG * NCMP], k_cmp[:, :], ident[0:NG * NCMP, 0:NG * NCMP]) \
                    .then_inc(k_cmp_turned, 1)
                pe.wait_ge(k_cmp_ready, 1)
                for t in range(TT):
                    for h in range(NH):
                        g = h // HPG
                        last = pe.matmul(ps[:, 4, (t * NH + h) * NCMP:(t * NH + h + 1) * NCMP], nqT[:, t, h, :],
                                         k_cmpT[:, g * NCMP:(g + 1) * NCMP], start=True, stop=True)
                last.then_inc(cmp_scores, 1)
                pe.wait_ge(cmp_p, 1)
                pe.wait_ge(y_taken, 2)
                for t in range(TT):
                    for h in range(NH):
                        i = t * NH + h
                        last = pe.transpose(ps[0:NCMP, i // 4, (i % 4) * P:(i % 4 + 1) * P], Ec[:, t, h, :], ident)
                last.then_inc(cmp_turned, 1)
                pe.wait_ge(cmp_pT, 2)
                for t in range(TT):
                    for h in range(NH):
                        last = pe.matmul(ps[:, 6 + t, h * DH:(h + 1) * DH], pcT[:, t, h, :], v_cmp[:, h // HPG, :],
                                         start=True, stop=True)
                last.then_inc(cmp_o, 1)

                def scores(u):
                    br, t, g = UNITS[u]
                    keys = (t + 1) * P
                    if u >= 2:
                        pe.wait_ge(at_masked, u - 1)
                    for h in range(HPG):
                        c = h * keys
                        last = pe.matmul(ps[:, 2 * (u % 2) + c // BANK, c % BANK:c % BANK + keys],
                                         nqT[:, t, g * HPG + h, :], nkT[:, br, g, 0:keys], start=True, stop=True)
                    last.then_inc(at_scores, 1)

                def turn_probs(u):
                    br, t, g = UNITS[u]
                    pe.wait_ge(at_exp, u + 1)
                    if u >= 1:
                        pe.wait_ge(at_pT, u)
                    e = E[:, u % 2, 0:HPG * (t + 1) * P].rearrange("p (h k) -> p h k", h=HPG)
                    for kc in range(t + 1):
                        for h in range(HPG):
                            last = pe.transpose(ps[:, 4 + kc, h * P:(h + 1) * P], e[:, h, kc * P:(kc + 1) * P], ident)
                    last.then_inc(at_turned, 1)

                def values(u):
                    br, t, g = UNITS[u]
                    pe.wait_ge(at_pT, u + 1)
                    if u >= 2:
                        pe.wait_ge(at_o_taken, u - 1)
                    off = (Z_VS, Z_VW)[br] + g * DH
                    for h in range(HPG):
                        for kc in range(t + 1):
                            last = pe.matmul(ps[:, 6 + u % 2, h * DH:(h + 1) * DH],
                                             PT[:, (kc * HPG + h) * P:(kc * HPG + h + 1) * P],
                                             z[:, kc, off:off + DH], start=(kc == 0), stop=(kc == t))
                    last.then_inc(at_o, 1)

                scores(0)
                pe.wait_ge(cmp_o_taken, TT)
                for u in range(len(UNITS)):
                    if u + 1 < len(UNITS):
                        scores(u + 1)
                    turn_probs(u)
                    values(u)
                pe.wait_ge(nsa_ready, 1)
                for k in range(KC):
                    for t in range(TT):
                        last = pe.transpose(ps[:, 4 + k // 2, (k % 2 * TT + t) * P:(k % 2 * TT + t + 1) * P],
                                            z[:, t, Z_NQ + k:Z_NQ + NH * DH:KC], ident)
                last.then_inc(nsa_turned, 1)
                pe.wait_ge(nsa_oT, 1)
                wide_output(yT, at["nsa_o"]).then_inc(item_done, 1)

                pe.wait_ge(m_ready, 1)
                turn_model(m_buf, 4).then_inc(m_turned, 1)
                pe.wait_ge(mT_act, 1)
                pe.wait_ge(mT_dve, 1)
                full_output(xT, KD, 0, at["out0"]).then_inc(item_done, 1)
                full_output(xT, KD, 1, at["out1"]).then_inc(item_done, 1)

                pe.wait_ge(x1_ready, 1)
                turn_model(x, 4).then_inc(x1_turned, 1)
                pe.wait_ge(x1T_act, 1)
                pe.wait_ge(x1T_dve, 1)
                pe.wait_ge(router_loaded, 32)
                for t in range(TT):
                    for k in range(KD):
                        last = pe.matmul(ps[:, 7, t * NE:(t + 1) * NE], xT[:, k, t * P:(t + 1) * P], router_w[:, k, :],
                                         start=(k == 0), stop=(k == KD - 1))
                last.then_inc(router_done, 1)

                zero = mask[0:1, 0:P]
                for b in range(4):
                    pe.matmul(ps[:, b, :], zero, zero.unsqueeze(1).to_broadcast([1, BANK // P, P]), start=True, stop=False, skip_group_check=True)

                def up(s, t):
                    w13 = experts[:, s, 0:2 * KD * FE].rearrange("p (w k f) -> p k w f", w=2, k=KD)
                    for k in range(KD):
                        last = pe.matmul(ps[:, 4 + t, :], xT[:, k, t * P:(t + 1) * P], w13[:, k, :, :],
                                         start=(k == 0), stop=(k == KD - 1))
                    last.then_inc(up_done, 1)

                def turn_hidden():
                    for j in range(2):
                        for t in range(TT):
                            last = pe.transpose(ps[:, 6, (j * TT + t) * P:(j * TT + t + 1) * P],
                                                hidden[:, t, j::2], ident)
                    last.then_inc(hidden_turned, 1)

                def down(s, final):
                    w2 = expert_parts(s)[2]
                    for t in range(TT):
                        for h in range(2):
                            for j in range(2):
                                last = pe.matmul(ps[:, 2 * t + h, :], hiddenT[:, j, t * P:(t + 1) * P],
                                                 w2[:, j, h * BANK:(h + 1) * BANK], start=False,
                                                 stop=(final and j == 1), skip_group_check=True)
                    last.then_inc(expert_used, 1)

                pe.wait_ge(expert_loaded[0], 48)
                for t in range(TT):
                    up(0, t)
                with pe.Fori(0, NE // E_SLOTS) as i:
                    for j in range(E_SLOTS):
                        s = (j + 1) % E_SLOTS
                        v = i * E_SLOTS + j + 1
                        pe.wait_ge(expert_loaded[s], i * 48 + (48 if s else 96))
                        pe.wait_ge(silu_done, v * 2 - 1)
                        pe.wait_ge(hidden_done, v * 2 - 1)
                        up(s, 0)
                        pe.wait_ge(hidden_done, v * 2)
                        turn_hidden()
                        up(s, 1)
                        pe.wait_ge(hiddenT_ready, v)
                        down(j, False)
                pe.wait_ge(hidden_done, 2 * E_ALL)
                turn_hidden()
                pe.wait_ge(hiddenT_ready, E_ALL)
                down(NE % E_SLOTS, True)
                pe.wait_ge(expert_used, E_ALL)
                layer_end(pe, l)

        @block.scalar
        def _(act):
            act.wait_ge(boot_step, 14)
            act.activation(sin[:, :, :], turn_n[:, :, :], ACT.Sin).then_inc(boot_sin, 1)
            act.activation(cos[:, :, :], cos[:, :, :], ACT.Sin).then_inc(boot_sin, 1)
            act.wait_ge(boot_sin, 2)
            act.wait_ge(layer_open, 1)
            with act.Fori(0, L) as l:
                c = Counts(act)

                def copy(dst, src, signal=act_step):
                    c.done(act.activation(dst, src, ACT.Copy), signal)

                xT_flat = xT[:, :, :].rearrange("p k t -> p (k t)")
                yT_flat = yT[:, :, :].rearrange("p k t -> p (k t)")
                act.wait_ge(x_turned, 1)
                copy(xT_flat[:, 0:2 * BANK], banks(4, 2), xT_act)

                def z_block(n):
                    cols = BANK if n != FULL_BLOCKS else LAST_COLS
                    act.wait_ge(item_done, n + 1)
                    pair = 2 * (n % 2)
                    copy(z[:, :, n * BANK:n * BANK + cols], ps[:, pair:pair + 2, 0:cols], z_written)

                z_block(0)
                z_block(1)
                c.done(act.activation(z[:, :, Z_CB:Z_CB + CH], z[:, :, Z_CB:Z_CB + CH], ACT.Sigmoid), conv_gate)
                z_block(2)
                act.wait_ge(params_turned, 1)
                copy(chan[:, :, :].rearrange("p k r -> p (k r)"), ps[:, 6, 0:KC * CHAN_ROWS], params_ready)
                copy(peT[:, :, :].rearrange("p v c -> p (v c)"), ps[0:DH, 7, 0:2 * CB], params_ready)
                act.wait_ge(u_turned, 1)
                act.wait_ge(pad_zeroed, 1)
                for b in range(2):
                    dst = u_pad[:, 2 * b:2 * b + 2, TAPS - 1:TAPS - 1 + T]
                    copy(dst, ps[:, 4 + b, :].rearrange("p (k t) -> p k t", k=2), act_step if b == 0 else uT_ready)
                z_block(3)
                with act.Fori(0, (FULL_BLOCKS - 4) // 2) as i:
                    for j in range(2):
                        act.wait_ge(item_done, 2 * i + j + 5)
                        act.activation(z[:, :, bass.ds(i * (2 * BANK) + (j + 4) * BANK, BANK)],
                                       ps[:, 2 * j:2 * j + 2, :], ACT.Copy).then_inc(z_written, 1)
                c.at[z_written.name] = FULL_BLOCKS
                act.wait_ge(z_written, FULL_BLOCKS)
                z_block(FULL_BLOCKS)
                c.done(act.activation(z[:, :, Z_NG:D_IN], z[:, :, Z_NG:D_IN], ACT.Sigmoid), gates_ready)
                c.done(act.activation(z[:, :, Z_RG:Z_RG + RH * RDV], z[:, :, Z_RG:Z_RG + RH * RDV], ACT.Silu),
                       ret_gate_ready)

                def root(n):
                    act.wait_ge(var_ready, c.at.get(std_ready.name, 0) + 1)
                    c.done(act.activation(rstd[:, 0:n], rstd[:, 0:n], ACT.Sqrt), std_ready)

                for h in range(RH):
                    act.wait_ge(qk_turned, h + 1)
                    copy(qkT[:, h, :, :].rearrange("p i t -> p (i t)"), ps[:, 6 + h % 2, :], qk_ready)
                root(TT)
                act.wait_ge(conv_turned, 1)
                for k in range(KC):
                    c.done(act.activation(yT[:, k, :], ps[:, 4 + k // 2, (k % 2) * T:(k % 2 + 1) * T], ACT.Silu,
                                          bias=chan[:, k, TAPS + 2:TAPS + 3], scale=chan[:, k, TAPS + 1:TAPS + 2]),
                           conv_silu)
                for h in range(RH):
                    act.wait_ge(ret_o, h + 1)
                    copy(ret_out[:, :, h * RDV:(h + 1) * RDV],
                         ps[:, 6 + h % 2, :].rearrange("p (t v) -> p t v", t=TT), ret_o_copied)
                root(RH * TT)
                act.wait_ge(ret_turned, 1)
                copy(yT_flat[:, 0:2 * BANK], banks(4, 2), yT_act)
                act.wait_ge(nq_turned, 1)
                for t in range(TT):
                    for g in range(NG):
                        c.done(act.activation(nqT[:, t, g * HPG:(g + 1) * HPG, :].rearrange("p h q -> p (h q)"),
                                              ps[0:DH, 4 + t * NG + g, :], ACT.Copy, scale=DH ** -0.5), nq_ready)
                act.wait_ge(nk_turned, 1)
                for b in range(2):
                    copy(nkT[:, b, :, :].rearrange("p g t -> p (g t)"), ps[0:DH, 4 + b, :], nk_act)
                act.wait_ge(item_done, at["w1_v1"] + 1)
                for half in range(2):
                    c.done(act.activation(hidT[:, :, half, :],
                                          ps[:, 6 + half, 0:64].rearrange("p (v n) -> p v n", v=2)[:, :, 0:NG * NCMP],
                                          ACT.Silu), hid_ready)
                act.wait_ge(k_cmp_turned, 1)
                copy(k_cmpT[:, :], ps[0:DH, 6, 0:NG * NCMP], k_cmp_ready)
                act.wait_ge(cmp_shifted, 1)
                c.done(act.activation(Ec[:, :, :, :], Ec[:, :, :, :], ACT.Exp), cmp_exp)
                act.wait_ge(cmp_turned, 1)
                for t in range(TT):
                    copy(pcT[:, t, :, :].rearrange("p h q -> p (h q)"), banks(2 * t, 2)[0:NCMP, :], cmp_pT)

                def exps(u):
                    br, t, g = UNITS[u]
                    keys = (t + 1) * P
                    act.wait_ge(at_max, u + 1)
                    for h in range(HPG):
                        e = E[:, u % 2, h * keys:(h + 1) * keys]
                        c.done(act.activation(e, e, ACT.Exp, bias=negmax[:, (u % 2) * HPG + h:(u % 2) * HPG + h + 1],
                                              accum_out=den[:, u, h:h + 1]), at_exp if h == HPG - 1 else act_step)

                def probs(u):
                    n = HPG * (UNITS[u][1] + 1) * P
                    act.wait_ge(at_turned, u + 1)
                    if u >= 1:
                        act.wait_ge(at_o, u)
                    copy(PT[:, 0:n], banks(4, 2)[:, 0:n], at_pT)

                exps(0)
                for u in range(len(UNITS)):
                    if u + 1 < len(UNITS):
                        exps(u + 1)
                    probs(u)
                act.wait_ge(nsa_turned, 1)
                copy(yT_flat[:, 0:2 * BANK], banks(4, 2), nsa_oT)
                act.wait_ge(m_turned, 1)
                copy(xT_flat[:, 0:2 * BANK], banks(4, 2), mT_act)
                root(TT)
                act.wait_ge(x1_turned, 1)
                copy(xT_flat[:, 0:2 * BANK], banks(4, 2), x1T_act)
                act.wait_ge(router_done, 1)
                c.done(act.activation(score[:, :, :].rearrange("p t e -> p (t e)"), ps[:, 7, 0:TT * NE], ACT.Sigmoid),
                       score_ready)

                def silu(t):
                    act.activation(silu_a[:, t, :], ps[:, 4 + t, 0:FE], ACT.Silu).then_inc(silu_done, 1)

                def copy_hidden():
                    act.activation(hiddenT.rearrange("p j t -> p (j t)"), ps[:, 6, :], ACT.Copy) \
                        .then_inc(hiddenT_ready, 1)

                for t in range(TT):
                    act.wait_ge(up_done, t + 1)
                    silu(t)
                with act.Fori(0, NE) as i:
                    act.wait_ge(hidden_turned, i + 1)
                    copy_hidden()
                    for t in range(TT):
                        act.wait_ge(up_done, i * 2 + 3 + t)
                        act.wait_ge(hidden_done, i * 2 + 1 + t)
                        silu(t)
                act.wait_ge(hidden_turned, E_ALL)
                copy_hidden()
                root(TT)
                layer_end(act, l)

        @block.vector
        def _(dve):
            magic = 1.5 * 2.0 ** 23
            c1, c2 = 6.28125, 0.0019340515136718750
            c3 = float(2 * np.pi - c1 - c2)
            boot_count = [1]

            def boot_done(ins):
                ins.then_inc(boot_step, 1)
                boot_count[0] += 1
                dve.wait_ge(boot_step, boot_count[0])

            dve.wait_ge(boot_dma, 64)
            dve.wait_ge(boot_step, 1)
            boot_done(dve.tensor_copy(pos[:, :], pos_i[:, :]))
            for i in range(TT + 1):
                boot_done(dve.tensor_scalar(sin[:, i, :], const("freq"), pos[:, i:i + 1], None, ALU.mult))
            boot_done(dve.tensor_scalar(turn_n[:, :, :], sin[:, :, :], float(1 / (2 * np.pi)), magic, ALU.mult, ALU.add))
            boot_done(dve.tensor_scalar(turn_n[:, :, :], turn_n[:, :, :], magic, None, ALU.subtract))
            for part in (c1, c2, c3):
                boot_done(dve.scalar_tensor_tensor(out=sin[:, :, :], in0=turn_n[:, :, :], scalar=-part,
                                                   in1=sin[:, :, :], op0=ALU.mult, op1=ALU.add))
            lim = 3.1415925
            boot_done(dve.tensor_scalar(turn_n[:, :, :], sin[:, :, :], lim, -lim, ALU.min, ALU.max))
            boot_done(dve.tensor_scalar(cos[:, :, :], turn_n[:, :, :], -1.0, None, ALU.mult))
            boot_done(dve.tensor_tensor(cos[:, :, :], cos[:, :, :], turn_n[:, :, :], ALU.min))
            boot_done(dve.tensor_scalar(cos[:, :, :], cos[:, :, :], float(np.pi / 2), None, ALU.add))
            assert boot_count[0] == 14, boot_count
            dve.wait_ge(boot_sin, 2)
            dve.wait_ge(layer_open, 1)

            with dve.Fori(0, L) as l:
                c = Counts(dve)

                def do(ins, signal=dve_step):
                    c.done(ins, signal)

                def tt(dst, in0, in1, op, signal=dve_step):
                    do(dve.tensor_tensor(dst, in0, in1, op), signal)

                def rope(x1, x2, co, si, tmp, signal=dve_step):
                    tt(tmp[0], x1, co, ALU.mult)
                    tt(tmp[1], x2, si, ALU.mult)
                    tt(tmp[2], x2, co, ALU.mult)
                    tt(tmp[3], x1, si, ALU.mult)
                    tt(x1, tmp[0], tmp[1], ALU.subtract)
                    tt(x2, tmp[2], tmp[3], ALU.add, signal)

                def mean_rstd(n):
                    do(dve.tensor_scalar(rstd[:, 0:n], mv[:, 0:n, 1], EPS, None, ALU.add), var_ready)
                    dve.wait_ge(std_ready, c.at[var_ready.name])
                    do(dve.reciprocal(rstd[:, 0:n], rstd[:, 0:n]))

                xT_flat = xT[:, :, :].rearrange("p k t -> p (k t)")
                yT_flat = yT[:, :, :].rearrange("p k t -> p (k t)")
                dve.wait_ge(x_turned, 1)
                do(dve.tensor_copy(xT_flat[:, 2 * BANK:], banks(6, 2)), xT_dve)
                do(dve.memset(u_pad[:, :, 0:TAPS - 1], 0.0), pad_zeroed)

                dve.wait_ge(conv_gate, 1)
                tt(z[:, :, Z_CA:Z_CA + CH], z[:, :, Z_CA:Z_CA + CH], z[:, :, Z_CB:Z_CB + CH], ALU.mult, u_ready)
                dve.wait_ge(params_ready, 2)
                dve.wait_ge(uT_ready, 1)
                for k in range(KC):
                    dve.tensor_scalar(conv_acc[:, k, :], u_pad[:, k, 0:T], chan[:, k, 0:1], chan[:, k, TAPS:TAPS + 1],
                                      ALU.mult, ALU.add).then_inc(conv_tap, 1)
                with dve.Fori(0, (TAPS - 1) // 2) as i:
                    for j in range(2):
                        for k in range(KC):
                            dve.wait_ge(conv_tap, i * (2 * KC) + (j * KC + k + 1))
                            dve.scalar_tensor_tensor(out=conv_acc[:, k, :], in0=u_pad[:, k, bass.ds(2 * i + (j + 1), T)],
                                                     scalar=chan[:, k, bass.ds(2 * i + (j + 1), 1)],
                                                     in1=conv_acc[:, k, :], op0=ALU.mult, op1=ALU.add) \
                                .then_inc(conv_tap, 1)
                dve.wait_ge(conv_tap, TAPS * KC)

                dve.wait_ge(z_written, Z_RV // BANK)
                halves = z[:, :, Z_RQ:Z_RV].rearrange("p t (h i f) -> p t h i f", i=2, f=RF)
                nh = 2 * RH
                tmp = [E[:, 1, 0:512], E[:, 1, 512:1024], PT[:, 0:512], PT[:, 512:1024]]
                tmp = [t_.rearrange("p (h f) -> p h f", h=nh) for t_ in tmp]
                for t in range(TT):
                    co, si = [w[:, t, 0:RF].unsqueeze(1).to_broadcast([P, nh, RF]) for w in (cos, sin)]
                    rope(halves[:, t, :, 0, :], halves[:, t, :, 1, :], co, si, tmp,
                         ret_roped if t == TT - 1 else dve_step)
                dve.wait_ge(z_written, Z_NG // BANK + 1)
                for t in range(TT):
                    for off, heads in ((Z_NQ, NH), (Z_KS, NG), (Z_KW, NG)):
                        v = z[:, t, off:off + heads * DH].rearrange("p (h f) -> p h f", h=heads)
                        co, si = [w[:, t, RF:FR].unsqueeze(1).to_broadcast([P, heads, NF]) for w in (cos, sin)]
                        small = [t_[:, 0:heads, 0:NF] for t_ in tmp]
                        rope(v[:, :, 0:NF], v[:, :, NF:ROT], co, si, small,
                             nsa_roped if (t, off) == (TT - 1, Z_KW) else dve_step)

                dve.wait_ge(conv_back, 1)
                for t in range(TT):
                    do(dve.bn_stats(stats[:, t, :], ps[:, 4 + t, :]))
                    do(dve.bn_aggr(mv[:, t, :], stats[:, t, :]))
                mean_rstd(TT)
                for t in range(TT):
                    do(dve.tensor_scalar(z[:, t, Z_CA:Z_CA + CH], ps[:, 4 + t, :], mv[:, t, 0:1], rstd[:, t:t + 1],
                                         ALU.subtract, ALU.mult), conv_normed if t == TT - 1 else dve_step)

                def merge(branch, signal):
                    for t in range(TT):
                        gate = z[:, t, Z_MG + branch * D:Z_MG + (branch + 1) * D]
                        last = t == TT - 1
                        if branch == 0:
                            tt(m_buf[:, t, :], gate, banks(2 * t, 2), ALU.mult, y_taken if last else dve_step)
                        else:
                            tt(E[:, t, :], gate, banks(2 * t, 2), ALU.mult, y_taken if last else dve_step)
                    if branch:
                        tt(m_buf, m_buf, E[:, :, :], ALU.add, signal)

                dve.wait_ge(item_done, at["conv_pw"] + 1)
                dve.wait_ge(gates_ready, 1)
                merge(0, None)

                def decay_scores(h):
                    dve.wait_ge(ret_scores, h + 1)
                    if h >= 2:
                        dve.wait_ge(ret_o, h - 1)
                    tt(ret_p[:, h % 2, :], ps[:, 4 + h % 2, 0:3 * P], decay[:, h, :], ALU.mult, ret_masked)

                decay_scores(0)
                for h in range(RH):
                    if h + 1 < RH:
                        decay_scores(h + 1)
                    dve.wait_ge(ret_o_copied, h + 1)
                    for t in range(TT):
                        i = h * TT + t
                        do(dve.bn_stats(stats[:, i, :], ret_out[:, t, h * RDV:(h + 1) * RDV]))
                        do(dve.bn_aggr(mv[:, i, :], stats[:, i, :]))
                mean_rstd(RH * TT)
                dve.wait_ge(ret_gate_ready, 1)
                for h in range(RH):
                    for t in range(TT):
                        i = h * TT + t
                        o = ret_out[:, t, h * RDV:(h + 1) * RDV]
                        do(dve.tensor_scalar(o, o, mv[:, i, 0:1], rstd[:, i:i + 1], ALU.subtract, ALU.mult))
                tt(ret_out, ret_out, z[:, :, Z_RG:Z_RG + RH * RDV], ALU.mult, ret_gated)
                dve.wait_ge(ret_turned, 1)
                do(dve.tensor_copy(yT_flat[:, 2 * BANK:], banks(6, 2)), yT_dve)
                dve.wait_ge(item_done, at["ret_o1"] + 1)
                merge(1, dve_step)

                dve.wait_ge(nk_turned, 1)
                for v in range(2):
                    do(dve.tensor_copy(cT[:, v, :, :].rearrange("p g t -> p (g t)"), ps[0:DH, 6 + v, :]), nk_dve)
                for v in range(2):
                    for g in range(NG):
                        by_stride = cT[:, v, g, :].rearrange("p (m s) -> p s m", s=CS)
                        for c2 in range(CB // CS):
                            tt(blocks_kv[:, v, c2 * CS:(c2 + 1) * CS, g, :], by_stride[:, :, c2:c2 + NCMP],
                               peT[:, v, c2 * CS:(c2 + 1) * CS].unsqueeze(2).to_broadcast([DH, CS, NCMP]),
                               ALU.add, blocks_ready)
                dve.wait_ge(kv_cmp_done, 1)
                kn = NG * NCMP
                do(dve.tensor_copy(k_cmp[:, :], ps[0:kn, 4, 0:DH]))
                co, si = cos[0:kn, TT, RF:FR], sin[0:kn, TT, RF:FR]
                rope(k_cmp[:, 0:NF], k_cmp[:, NF:ROT], co, si, [E[0:kn, 0, i * NF:(i + 1) * NF] for i in range(4)])
                do(dve.tensor_copy(v_cmp[:, :, :].rearrange("p g d -> p (g d)"), ps[0:NCMP, 5, 0:NG * DH]), kv_cmp_ready)

                dve.wait_ge(cmp_scores, 1)
                s = ps[:, 4, 0:TT * NH * NCMP].rearrange("p (t h n) -> p t h n", t=TT, h=NH)
                bc = [P, NH, NCMP]
                for t in range(TT):
                    tt(Ec[:, t, :, :], s[:, t, :, :], cmp_add[:, t, :].unsqueeze(1).to_broadcast(bc), ALU.add)
                flat = Ec[:, :, :, :].rearrange("p t h n -> p (t h) n")
                do(dve.tensor_reduce(negmax[:, :], flat, AX.X, ALU.max, negate=True))
                tt(flat, flat, negmax[:, :].unsqueeze(2).to_broadcast([P, TT * NH, NCMP]), ALU.add, cmp_shifted)
                dve.wait_ge(cmp_exp, 1)
                do(dve.tensor_reduce(coef[:, :], flat, AX.X, ALU.add))
                for t in range(TT):
                    tt(Ec[:, t, :, :], Ec[:, t, :, :], cmp_01[:, t, :].unsqueeze(1).to_broadcast(bc), ALU.mult,
                       cmp_p if t == TT - 1 else dve_step)
                do(dve.reciprocal(coef[:, :], coef[:, :]))
                gate3 = z[:, :, Z_NG:Z_NG + NH * 3].rearrange("p t (h b) -> p t h b", b=3)
                tt(coef[:, :].rearrange("p (t h) -> p t h", t=TT), coef[:, :].rearrange("p (t h) -> p t h", t=TT),
                   gate3[:, :, :, 0], ALU.mult)
                dve.wait_ge(cmp_o, 1)
                for t in range(TT):
                    tt(nsa_out[:, t, :].rearrange("p (h d) -> p h d", h=NH), ps[:, 6 + t, :].rearrange("p (h d) -> p h d", h=NH),
                       coef[:, t * NH:(t + 1) * NH].unsqueeze(2).to_broadcast([P, NH, DH]), ALU.mult, cmp_o_taken)

                def mask_scores(u):
                    br, t, g = UNITS[u]
                    keys = (t + 1) * P
                    dve.wait_ge(at_scores, u + 1)
                    if u >= 2:
                        dve.wait_ge(at_turned, u - 1)
                    e = E[:, u % 2, 0:HPG * keys].rearrange("p (h k) -> p h k", h=HPG)
                    sc = banks(2 * (u % 2), 2)[:, 0:HPG * keys].rearrange("p (h k) -> p h k", h=HPG)
                    mk = mask[:, 2 * P - keys:2 * P].unsqueeze(1).to_broadcast([P, HPG, keys])
                    tt(e, sc, mk, ALU.add, at_masked)
                    do(dve.tensor_reduce(negmax[:, (u % 2) * HPG:(u % 2 + 1) * HPG], e, AX.X, ALU.max, negate=True),
                       at_max)

                def add_output(u):
                    br, t, g = UNITS[u]
                    dve.wait_ge(at_o, u + 1)
                    w = coef[:, 0:HPG]
                    do(dve.reciprocal(w, den[:, u, :]))
                    tt(w, w, gate3[:, t, g * HPG:(g + 1) * HPG, br + 1], ALU.mult)
                    add = silu_a[:, 0, :].rearrange("p (h d) -> p h d", h=HPG)
                    tt(add, ps[:, 6 + u % 2, 0:HPG * DH].rearrange("p (h d) -> p h d", h=HPG),
                       w.unsqueeze(2).to_broadcast([P, HPG, DH]), ALU.mult, at_o_taken)
                    o = nsa_out[:, t, g * HPG * DH:(g + 1) * HPG * DH]
                    tt(o, o, silu_a[:, 0, :], ALU.add, nsa_ready if u == len(UNITS) - 1 else dve_step)

                mask_scores(0)
                for u in range(len(UNITS)):
                    if u + 1 < len(UNITS):
                        mask_scores(u + 1)
                    add_output(u)
                dve.wait_ge(item_done, at["nsa_o"] + 1)
                merge(2, m_ready)
                dve.wait_ge(m_turned, 1)
                do(dve.tensor_copy(xT_flat[:, 2 * BANK:], banks(6, 2)), mT_dve)

                def residual_norm(which, signal):
                    for t in range(TT):
                        do(dve.scalar_tensor_tensor(out=x[:, t, :], in0=x[:, t, :], scalar=ALPHA, in1=banks(2 * t, 2),
                                                    op0=ALU.mult, op1=ALU.add), y_taken)
                        for h in range(2):
                            do(dve.bn_stats(stats[:, 2 * t + h, :], x[:, t, h * BANK:(h + 1) * BANK]))
                        do(dve.bn_aggr(mv[:, t, :], stats[:, 2 * t:2 * t + 2, :].rearrange("p a b -> p (a b)")))
                    mean_rstd(TT)
                    for t in range(TT):
                        do(dve.tensor_scalar(x[:, t, :], x[:, t, :], mv[:, t, 0:1], rstd[:, t:t + 1],
                                             ALU.subtract, ALU.mult))
                    gain, bias = [norm[:, 2 * which + i, :].unsqueeze(1).to_broadcast([P, TT, D]) for i in range(2)]
                    tt(x[:, :, :], x[:, :, :], gain, ALU.mult)
                    tt(x[:, :, :], x[:, :, :], bias, ALU.add, signal)

                dve.wait_ge(item_done, at["out1"] + 1)
                dve.wait_ge(norm_loaded, 64)
                residual_norm(0, x1_ready)
                dve.wait_ge(x1_turned, 1)
                do(dve.tensor_copy(xT_flat[:, 2 * BANK:], banks(6, 2)), x1T_dve)

                dve.wait_ge(score_ready, 1)
                dve.wait_ge(router_loaded, 32)
                tt(biased[:, :, :], score[:, :, :], router_b[:, :].unsqueeze(1).to_broadcast([P, TT, NE]), ALU.add)
                per = NE // NEG_
                for t in range(TT):
                    for g in range(NEG_):
                        do(dve.max(best[:, t, g, :], biased[:, t, g * per:(g + 1) * per]))
                do(dve.memset(group[:, :, :], -NEG))
                tt(group[:, :, 0:NEG_], best[:, :, :, 0], best[:, :, :, 1], ALU.add)
                for t in range(TT):
                    do(dve.max(top[:, :], group[:, t, :]))
                    do(dve.match_replace(group_out[:, t, :], top[:, :], group[:, t, :], NEG))
                kept = group_out[:, :, 0:NEG_]
                do(dve.tensor_scalar(kept, kept, NEG, NEG, ALU.not_equal, ALU.mult))
                for t in range(TT):
                    e3 = biased[:, t, :].rearrange("p (g e) -> p g e", g=NEG_)
                    tt(e3, e3, group_out[:, t, 0:NEG_].unsqueeze(2).to_broadcast([P, NEG_, per]), ALU.add)
                    do(dve.max(top[:, :], biased[:, t, :]))
                    do(dve.match_replace(marked[:, t, :], top[:, :], biased[:, t, :], 2 * NEG))
                do(dve.tensor_scalar(marked[:, :, :], marked[:, :, :], 2 * NEG, None, ALU.is_equal))
                tt(marked[:, :, :], marked[:, :, :], score[:, :, :], ALU.mult)
                do(dve.tensor_reduce(total[:, :], marked[:, :, :], AX.X, ALU.add))
                do(dve.reciprocal(total[:, :], total[:, :]))
                do(dve.memset(gates[:, :, 0:1], 1.0))
                for t in range(TT):
                    do(dve.tensor_scalar(gates[:, t, 1:E_ALL], marked[:, t, :], total[:, t:t + 1], SCALE_ROUTED,
                                         ALU.mult, ALU.mult))

                def gate_hidden(v, t):
                    dve.scalar_tensor_tensor(out=hidden[:, t, :], in0=ps[:, 4 + t, FE:2 * FE],
                                             scalar=gates[:, t, bass.ds(v, 1)], in1=silu_a[:, t, :],
                                             op0=ALU.mult, op1=ALU.mult).then_inc(hidden_done, 1)

                for t in range(TT):
                    dve.wait_ge(silu_done, t + 1)
                    dve.wait_ge(up_done, t + 1)
                    gate_hidden(0, t)
                with dve.Fori(0, NE) as i:
                    for t in range(TT):
                        dve.wait_ge(silu_done, i * 2 + 3 + t)
                        dve.wait_ge(up_done, i * 2 + 3 + t)
                        dve.wait_ge(hidden_turned, i + 1)
                        gate_hidden(i + 1, t)
                dve.wait_ge(expert_used, E_ALL)
                residual_norm(1, dve_step)
                layer_end(dve, l)


_INS = ["x", "positions", "w_in", "conv_dw", "conv_db", "conv_ln_g", "conv_ln_b", "conv_w_pw", "ret_w_o",
        "nsa_pe_k", "nsa_w1_k", "nsa_w2_k", "nsa_pe_v", "nsa_w1_v", "nsa_w2_v", "nsa_w_o", "w_out",
        "ln1_g", "ln1_b", "router_w", "router_b", "moe_w1", "moe_w3", "moe_w2",
        "shared_w1", "shared_w3", "shared_w2", "ln2_g", "ln2_b"]


def kernel(**inputs):
    import numpy as _np
    import concourse.bacc as _bacc
    from concourse import mybir as _mybir
    from concourse.bass_utils import run_bass_kernel_spmd as _run

    nc = _bacc.Bacc("TRN2", target_bir_lowering=False, num_devices=1)
    arrays, args = {}, {}
    for name in _INS + ["consts"]:
        v = _np.ascontiguousarray(shape_constants() if name == "consts" else inputs[name])
        arrays[f"in_{name}_dram"] = v
        args[name] = nc.dram_tensor(f"in_{name}_dram", v.shape, _mybir.dt.from_np(v.dtype), kind="ExternalInput").ap()
    out = nc.dram_tensor("out_0_dram", (1, T, D), _mybir.dt.float32, kind="ExternalOutput").ap()
    build(nc, args, out)
    r = _run(nc, [arrays], core_ids=[0])
    return r.results[0]["out_0_dram"]
```

```python
from contextlib import ExitStack

import numpy as np

import concourse.bass as bass
from concourse import mybir

F32 = mybir.dt.float32
I32 = mybir.dt.int32
ALU = mybir.AluOpType
ACT = mybir.ActivationFunctionType
AX = mybir.AxisListType

P = 128
L = 2
T = 256
TT = T // P
D = 1024
KD = D // P
CH = 512
KC = CH // P
TAPS = 31
RH, RDK, RDV = 4, 128, 256
NH, NG, DH = 8, 2, 64
HPG = NH // NG
CB, CS = 32, 16
NCMP = (T - CB) // CS + 1
CHID = 256
ROT = DH // 4
NE, NEG_, TOPG, TOPK = 64, 8, 4, 8
FE = 256
SCALE_ROUTED = 2.5
ALPHA = (2.0 * L) ** 0.25
EPS = 1e-5
NEG = -1e30
BANK = 512

WIDTHS = (CH, CH, RH * RDK, RH * RDK, RH * RDV, RH * RDV, NH * DH) + (NG * DH,) * 6 + (NH * 3, 3 * D)
(Z_CA, Z_CB, Z_RQ, Z_RK, Z_RV, Z_RG, Z_NQ, Z_KC, Z_VC, Z_KS, Z_VS, Z_KW, Z_VW, Z_NG, Z_MG, D_IN) = \
    [sum(WIDTHS[:i]) for i in range(len(WIDTHS) + 1)]
FULL_BLOCKS = D_IN // BANK
LAST_COLS = D_IN - FULL_BLOCKS * BANK

ITEMS = ["in"] * (FULL_BLOCKS + 1) + ["conv_pw", "ret_o0", "ret_o1", "w1_k0", "w1_k1", "w1_v0", "w1_v1",
                                      "nsa_o", "out0", "out1"]
RING = 2
SLOT = KD * BANK
EXPERT = 3 * KD * FE
E_SLOTS = 4
CAP = 64
PAIRS = NE // 2
ROUNDS = T // CAP
MAX_MORE = T * TOPK // CAP
E_ALL = NE + 1
Z0 = RING * SLOT
ARENA = max(Z0 + TT * D_IN, E_SLOTS * EXPERT)

CHAN_ROWS = TAPS + 3
RF = RDK // 2
NF = ROT // 2
FR = RF + NF
CONSTS = {"ident": P, "decay": RH * T, "mask": 2 * P, "cmp_add": TT * NCMP, "cmp_01": TT * NCMP, "freq": FR,
          "before": P, "ones": P, "count": T}


def shape_constants():
    f = np.float32
    p = np.arange(P)
    out = {"ident": np.eye(P, dtype=f)}
    log_gamma = np.log1p(-np.exp2(f(-5.0) - np.arange(RH, dtype=f))).astype(f)
    diff = np.arange(T)[None, :] - p[:, None]
    full = np.where(diff >= 0, np.exp(log_gamma[:, None, None] * np.maximum(diff, 0).astype(f)), 0) * f(RDK ** -0.5)
    out["decay"] = full.transpose(1, 0, 2).reshape(P, -1)
    tri = np.where(p[None, :] <= p[:, None], 0.0, NEG)
    out["mask"] = np.concatenate([np.zeros((P, P)), tri], 1)
    end = np.arange(NCMP) * CS + CB - 1
    ok = end[None, None, :] <= (np.arange(TT)[None, :, None] * P + p[:, None, None])
    out["cmp_add"] = np.where(ok, 0.0, NEG).reshape(P, -1)
    out["cmp_01"] = np.where(ok, 1.0, 0.0).reshape(P, -1)
    ret = f(1.0) / np.power(f(10000.0), np.linspace(0.0, 1.0, RF, dtype=f))
    nsa = np.power(f(500000.0), -np.arange(0, ROT, 2, dtype=f) / f(ROT))
    out["freq"] = np.tile(np.concatenate([ret, nsa])[None], (P, 1))
    out["before"] = (p[:, None] < p[None, :])
    out["ones"] = np.ones((P, P))
    out["count"] = np.tile(np.arange(1, T + 1)[None], (P, 1))
    return np.concatenate([out[k].reshape(P, n).astype(f) for k, n in CONSTS.items()], 1)


class Counts:

    def __init__(self, engine):
        self.engine = engine
        self.at = {}

    def done(self, ins, sem):
        ins.then_inc(sem, 1)
        self.at[sem.name] = self.at.get(sem.name, 0) + 1
        self.engine.wait_ge(sem, self.at[sem.name])


def build(nc, a, out):
    with ExitStack() as ctx:
        def sb(name, shape, dt=F32):
            return ctx.enter_context(nc.sbuf_tensor(name, shape, dt))

        def sem(name):
            return ctx.enter_context(nc.semaphore(name))

        consts = sb("consts", [P, sum(CONSTS.values())])
        c_at = dict(zip(CONSTS, np.cumsum([0] + list(CONSTS.values())).tolist()))

        def const(name):
            return consts[:, c_at[name]:c_at[name] + CONSTS[name]]

        ident = const("ident")
        decay = const("decay").rearrange("p (h c) -> p h c", h=RH)
        mask = const("mask")
        cmp_add = const("cmp_add").rearrange("p (t n) -> p t n", t=TT)
        cmp_01 = const("cmp_01").rearrange("p (t n) -> p t n", t=TT)
        arena = sb("arena", [P, ARENA])
        ring = arena[:, 0:RING * SLOT].rearrange("p (s n) -> p s n", s=RING)
        z = arena[:, Z0:Z0 + TT * D_IN].rearrange("p (t n) -> p t n", t=TT)
        x = sb("x", [P, TT, D])
        xT = sb("xT", [P, KD, T])
        yT = sb("yT", [P, KD, T])
        norm = sb("norm", [P, 4, D])
        qkT = sb("qkT", [P, RH, 2, T])
        nq_buf = sb("nq_buf", [P, TT * NH * P])
        nqT = nq_buf[0:DH, :].rearrange("p (t h q) -> p t h q", t=TT, h=NH)
        nk_buf = sb("nk_buf", [P, 2, 2 * NG * T])
        nkT, cT = [nk_buf[0:DH, i, :].rearrange("p (v g t) -> p v g t", v=2, g=NG) for i in range(2)]
        shared_buf = sb("shared_buf", [P, 2 * CB * NG * NCMP + 8])
        blocks_kv = shared_buf[0:DH, 0:2 * CB * NG * NCMP].rearrange("p (v c g n) -> p v c g n", v=2, c=CB, g=NG)
        u_pad = shared_buf[:, 0:KC * (TAPS - 1 + T)].rearrange("p (k t) -> p k t", k=KC)
        E = sb("E", [P, 2, 4 * T])
        conv_acc = E[:, 0, :].rearrange("p (k t) -> p k t", k=KC)
        PT = sb("PT", [P, 4 * T])
        ret_p = PT[:, 0:2 * 3 * P].rearrange("p (b c) -> p b c", b=2)
        chan = sb("chan", [P, KC, CHAN_ROWS])
        chan_raw = sb("chan_raw", [CHAN_ROWS, CH])
        pe_raw = sb("pe_raw", [CB, 2, DH])
        peT = sb("peT", [DH, 2, CB])
        w2_kv = sb("w2_kv", [P, 2, 2, DH])
        hidT = sb("hidT", [P, 2, 2, NG * NCMP])
        k_cmp = sb("k_cmp", [NG * NCMP, DH])
        k_cmpT = sb("k_cmpT", [DH, NG * NCMP])
        v_cmp = sb("v_cmp", [NCMP, NG, DH])
        pcT = yT[0:NCMP, :, :].rearrange("p k t -> p (k t)").rearrange("p (t h q) -> p t h q", t=TT, h=NH)
        Ec = sb("Ec", [P, TT, NH, NCMP])
        pos_i = sb("pos_i", [P, TT + 1], I32)
        pos = sb("pos", [P, TT + 1])
        cos = sb("cos", [P, TT + 1, FR])
        sin = sb("sin", [P, TT + 1, FR])
        turn_n = sb("turn_n", [P, TT + 1, FR])
        stats = sb("stats", [P, 2 * RH * TT, 6])
        mv = sb("mv", [P, 2 * RH, 2])
        rstd = sb("rstd", [P, 2 * RH])
        negmax = sb("negmax", [P, TT * NH])
        den = sb("den", [P, 2 * TT * NG, HPG])
        coef = sb("coef", [P, TT * NH])
        router_w = sb("router_w", [P, KD, NE])
        router_b = sb("router_b", [P, NE])
        score = sb("score", [P, TT, NE])
        biased = sb("biased", [P, TT, NE])
        best = sb("best", [P, TT, NEG_, 8])
        group = sb("group", [P, TT, NEG_ + 8 - TOPG])
        group_out = sb("group_out", [P, TT, NEG_ + 8 - TOPG])
        top = sb("top", [P, 8])
        marked = sb("marked", [P, TT, NE])
        total = sb("total", [P, TT])
        gates = sb("gates", [P, TT, E_ALL])
        silu_a = sb("silu_a", [P, TT, FE])
        hidden = qkT[:, 0, :, :]
        hiddenT = qkT[:, 1, :, :]

        ps = ctx.enter_context(nc.psum_tensor("ps", [P, 8, BANK], F32))

        def banks(b, n):
            return ps[:, b:b + n, :].rearrange("p b n -> p (b n)")

        pick, pick_gated = [E[:, 1, i * 512:(i + 1) * 512].rearrange("p (b t a s) -> p b t a s", b=2, t=TT, a=2)
                            for i in range(2)]
        pickT = E[:, 0, :].rearrange("p (b t) -> p b t", b=4)
        xg = yT[:, :, :].rearrange("p k t -> p (k t)").rearrange("p (b k s) -> p b k s", b=2, k=KD)
        hT = PT[:, 0:512].rearrange("p (b j s) -> p b j s", b=2, j=2)
        silu_pair_buf = PT[:, 512:512 + 4 * CAP].rearrange("p (a j s) -> p a j s", a=2, j=2)
        y_slots = nq_buf[:, 0:D].rearrange("p (h n) -> p h n", h=2)
        more_xg = nq_buf[:, D:D + KD * CAP].rearrange("p (k s) -> p k s", k=KD)
        more_y = nk_buf[0:CAP, 0, :].rearrange("p (h n) -> p h n", h=2)
        more = nk_buf[:, 1, :]
        more_pick, more_gated = [more[:, i * TT * CAP:(i + 1) * TT * CAP].rearrange("p (t s) -> p t s", t=TT)
                                 for i in range(2)]
        more_pickT = more[0:CAP, 256:256 + T]
        more_silu, more_hT = [more[:, 512 + i * 2 * CAP:512 + (i + 1) * 2 * CAP].rearrange("p (j s) -> p j s", j=2)
                              for i in range(2)]
        passed = nk_buf[0:1, :, :].rearrange("p a b -> p (a b)").rearrange("p (n e) -> p n e", n=MAX_MORE)
        counts = nq_buf[0:1, D:D + NE]
        more_rows = nq_buf[0:1, D + 512:D + 512 + 4 * 2 * NE].rearrange("p (r e) -> p r e", r=4)
        place = sb("place", [P, TT, NE])
        listed = sb("listed", [1, 1 + 2 * MAX_MORE], I32)

        boot = sem("boot")
        boot_dma = sem("boot_dma")
        boot_step = sem("boot_step")
        boot_sin = sem("boot_sin")
        engine_at_end = sem("engine_at_end")
        all_at_end = sem("all_at_end")
        layer_open = sem("layer_open")
        layer_entered = sem("layer_entered")
        wait_passed = sem("wait_passed")
        stored = sem("stored")
        layer_sems = []

        def lsem(name):
            layer_sems.append(sem(name))
            return layer_sems[-1]

        ring_loaded = [lsem(f"ring_loaded{s}") for s in range(RING)]
        item_done = lsem("item_done")
        chan_loaded, pe_loaded, w2_loaded = lsem("chan_loaded"), lsem("pe_loaded"), lsem("w2_loaded")
        norm_loaded, router_loaded = lsem("norm_loaded"), lsem("router_loaded")
        dve_step, act_step, pool_step = lsem("dve_step"), lsem("act_step"), lsem("pool_step")
        x_turned = lsem("x_turned")
        xT_act, xT_dve = lsem("xT_act"), lsem("xT_dve")
        z_written = lsem("z_written")
        conv_gate = lsem("conv_gate")
        u_ready, u_turned, uT_ready = lsem("u_ready"), lsem("u_turned"), lsem("uT_ready")
        params_turned, params_ready = lsem("params_turned"), lsem("params_ready")
        pad_zeroed = lsem("pad_zeroed")
        conv_tap = lsem("conv_tap")
        conv_back = lsem("conv_back")
        var_ready, std_ready = lsem("var_ready"), lsem("std_ready")
        conv_normed, conv_turned, conv_silu = lsem("conv_normed"), lsem("conv_turned"), lsem("conv_silu")
        gates_ready, ret_gate_ready = lsem("gates_ready"), lsem("ret_gate_ready")
        y_taken = lsem("y_taken")
        ret_roped, nsa_roped = lsem("ret_roped"), lsem("nsa_roped")
        qk_turned, qk_ready = lsem("qk_turned"), lsem("qk_ready")
        ret_scores, ret_masked, ret_o, ret_o_copied = \
            lsem("ret_scores"), lsem("ret_masked"), lsem("ret_o"), lsem("ret_o_copied")
        ret_gated, ret_turned, yT_act, yT_dve = \
            lsem("ret_gated"), lsem("ret_turned"), lsem("yT_act"), lsem("yT_dve")
        nq_turned, nq_ready, nk_turned, nk_act, nk_dve = \
            lsem("nq_turned"), lsem("nq_ready"), lsem("nk_turned"), lsem("nk_act"), lsem("nk_dve")
        blocks_ready, hid_ready = lsem("blocks_ready"), lsem("hid_ready")
        kv_cmp_done, kv_cmp_ready, k_cmp_turned, k_cmp_ready = \
            lsem("kv_cmp_done"), lsem("kv_cmp_ready"), lsem("k_cmp_turned"), lsem("k_cmp_ready")
        cmp_scores, cmp_shifted, cmp_exp, cmp_p, cmp_turned, cmp_pT, cmp_o, cmp_o_taken = \
            [lsem(f"cmp_{n}") for n in ("scores", "shifted", "exp", "p", "turned", "pT", "o", "o_taken")]
        at_scores, at_masked, at_max, at_exp, at_turned, at_pT, at_o, at_o_taken = \
            [lsem(f"at_{n}") for n in ("scores", "masked", "max", "exp", "turned", "pT", "o", "o_taken")]
        nsa_ready, nsa_turned, nsa_oT = lsem("nsa_ready"), lsem("nsa_turned"), lsem("nsa_oT")
        m_ready, m_turned, mT_act, mT_dve = lsem("m_ready"), lsem("m_turned"), lsem("mT_act"), lsem("mT_dve")
        x1_ready, x1_turned, x1T_act, x1T_dve = \
            lsem("x1_ready"), lsem("x1_turned"), lsem("x1T_act"), lsem("x1T_dve")
        router_done, score_ready = lsem("router_done"), lsem("score_ready")
        up_loaded = [lsem(f"up_loaded{s}") for s in range(E_SLOTS)]
        down_loaded = [lsem(f"down_loaded{s}") for s in range(E_SLOTS)]
        up_done = lsem("up_done")
        silu_done = lsem("silu_done")
        hidden_done = lsem("hidden_done")
        hidden_turned = lsem("hidden_turned")
        hiddenT_ready = lsem("hiddenT_ready")
        expert_used = lsem("expert_used")
        chosen_ready = lsem("chosen_ready")
        places_done = lsem("places_done")
        listed_ready = lsem("listed_ready")
        pick_made, pick_ready = lsem("pick_made"), lsem("pick_ready")
        pick_turned, pickT_ready = lsem("pick_turned"), lsem("pickT_ready")
        gathered, xg_ready = lsem("gathered"), lsem("xg_ready")
        pair_up, pair_silu, h_ready = lsem("pair_up"), lsem("pair_silu"), lsem("h_ready")
        y0_done = lsem("y0_done")
        y0_ready, y1_ready = lsem("y0_ready"), lsem("y1_ready")
        main_done = lsem("main_done")
        more_loaded = [lsem(f"more_loaded{j}") for j in range(2)]
        more_pe, more_act, more_dve = lsem("more_pe"), lsem("more_act"), lsem("more_dve")
        experts_done = lsem("experts_done")
        numbers = [s.num for s in layer_sems]
        assert numbers == list(range(numbers[0], numbers[-1] + 1))

        w_in = a["w_in"].rearrange("l (p k) n -> l p k n", k=KD)
        moe_w1 = a["moe_w1"].rearrange("l e (p k) f -> l e p k f", k=KD)
        moe_w3 = a["moe_w3"].rearrange("l e (p k) f -> l e p k f", k=KD)
        moe_w2 = a["moe_w2"].rearrange("l e (p j) n -> l e p j n", j=2)

        at = {name: n for n, name in enumerate(ITEMS)}

        def ring_slot(item):
            return ring[:, item % RING, :]

        w_up = [arena[:, s * 2 * KD * FE:(s + 1) * 2 * KD * FE].rearrange("p (w k f) -> p w k f", w=2, k=KD)
                for s in range(E_SLOTS)]
        w_down = [arena[:, (2 * E_SLOTS + s) * KD * FE:(2 * E_SLOTS + s + 1) * KD * FE]
                  .rearrange("p (j n) -> p j n", j=2) for s in range(E_SLOTS)]

        m_buf = z[:, :, 0:D]
        ret_out = z[:, :, Z_RQ:Z_RQ + RH * RDV]
        nsa_out = z[:, :, Z_NQ:Z_NQ + NH * DH]
        PE_STEPS, ACT_STEPS, DVE_STEPS = 5, 3, 5
        PE_FROM = 2 * PE_STEPS
        MORE = (1, 2)

        def up_loads(p, m, b):
            return 16 * p + 8 * (1 + b - slot_of(m, b)) + 32

        def down_loads(p, m, b):
            return 8 * p + 4 * (1 + b - slot_of(m, b)) + 16

        def slot_of(m, b):
            return (1 + 2 * m + b) % E_SLOTS

        def pipeline(eng, step):
            def peeled(p):
                step(p, p % 4, lambda d: 0 <= p + d < PAIRS)

            for p in range(2):
                peeled(p)
            with eng.Fori(0, (PAIRS - 4) // 4) as i:
                for j in range(4):
                    step(4 * i + (2 + j), (2 + j) % 4, lambda d: True)
            for p in range(PAIRS - 2, PAIRS + 2):
                peeled(p)

        def further_rounds(eng, step):
            wanted = eng.value_load(listed[0:1, 0:1], min_val=0, max_val=MAX_MORE)
            with eng.Fori(0, MAX_MORE // 8) as a:
                with eng.If(wanted > a * 8):
                    with eng.Fori(0, 4) as i:
                        for j in range(2):
                            with eng.If(wanted > a * 8 + i * 2 + j):
                                step(a * 8 + i * 2 + j, a * 4 + i, j)

        def round_expert(eng, n):
            return eng.value_load(listed[0:1, bass.ds(n + 1, 1)], min_val=0, max_val=NE - 1)

        def round_start(eng, n):
            return eng.value_load(listed[0:1, bass.ds(n + (1 + MAX_MORE), 1)], min_val=CAP, max_val=T - CAP)

        UNITS = [(br, tt, g) for br in range(2) for tt in range(TT) for g in range(NG)]

        def layer_end(eng, l):
            eng.sem_inc(engine_at_end, 1)
            eng.wait_ge(layer_open, l + 2)
            eng.sem_inc(layer_entered, 1)

        block = ctx.enter_context(nc.Block())

        @block.sync
        def _(sp):
            sp.dma_start(x[:, :, :], a["x"].rearrange("b (t p) d -> p (b t) d", p=P)).then_inc(boot, 16)
            sp.wait_ge(layer_open, 1)
            with sp.Fori(0, L) as l:
                for n in range(2):
                    sp.dma_start(ring_slot(n).rearrange("p (k n) -> p k n", k=KD),
                                 w_in[l, :, :, n * BANK:(n + 1) * BANK]).then_inc(ring_loaded[n], 16)
                sp.dma_start(chan_raw[0:TAPS, :], a["conv_dw"][l]).then_inc(chan_loaded, 16)
                for i, n in enumerate(("conv_db", "conv_ln_g", "conv_ln_b")):
                    sp.dma_start(chan_raw[TAPS + i:TAPS + i + 1, :], a[n][bass.ds(l, 1), :]).then_inc(chan_loaded, 16)
                for i, v in enumerate("kv"):
                    sp.dma_start(pe_raw[:, i, :], a[f"nsa_pe_{v}"][l]).then_inc(pe_loaded, 16)
                    sp.dma_start(w2_kv[:, i, :, :], a[f"nsa_w2_{v}"].rearrange("l (h p) d -> l p h d", p=P)[l]) \
                        .then_inc(w2_loaded, 16)
                for i, n in enumerate(("ln1_g", "ln1_b", "ln2_g", "ln2_b")):
                    sp.dma_start(norm[:, i, :], a[n][bass.ds(l, 1), :].to_broadcast([P, D])).then_inc(norm_loaded, 16)
                sp.dma_start(router_w[:, :, :], a["router_w"].rearrange("l (p k) e -> l p k e", k=KD)[l]) \
                    .then_inc(router_loaded, 16)
                sp.dma_start(router_b[:, :], a["router_b"][bass.ds(l, 1), :].to_broadcast([P, NE])) \
                    .then_inc(router_loaded, 16)
                with sp.Fori(0, (FULL_BLOCKS - 2) // 2) as i:
                    for j in range(2):
                        sp.wait_ge(item_done, 2 * i + j + 1)
                        sp.sem_inc(wait_passed, 1)
                        sp.dma_start(ring_slot(j).rearrange("p (k n) -> p k n", k=KD),
                                     w_in[l, :, :, bass.ds(i * (2 * BANK) + (j + 2) * BANK, BANK)]) \
                            .then_inc(ring_loaded[j], 16)
                sources = {
                    "in": (w_in[l, :, :, FULL_BLOCKS * BANK:D_IN], LAST_COLS),
                    "conv_pw": (a["conv_w_pw"].rearrange("l (p k) n -> l p k n", k=KC)[l], D),
                    "nsa_o": (a["nsa_w_o"].rearrange("l (p k) n -> l p k n", k=KC)[l], D),
                }
                for h in range(2):
                    cols = slice(h * BANK, (h + 1) * BANK)
                    sources[f"ret_o{h}"] = (a["ret_w_o"].rearrange("l (p k) n -> l p k n", k=KD)[l, :, :, cols], BANK)
                    sources[f"out{h}"] = (a["w_out"].rearrange("l (p k) n -> l p k n", k=KD)[l, :, :, cols], BANK)
                    for v in "kv":
                        w1 = a[f"nsa_w1_{v}"].rearrange("l (c d) h -> l d c h", d=DH)
                        sources[f"w1_{v}{h}"] = (w1[l, :, h * CB // 2:(h + 1) * CB // 2, :], CHID)
                for n in range(FULL_BLOCKS, len(ITEMS)):
                    src, cols = sources[ITEMS[n]]
                    parts, k = src.shape[0], src.shape[1]
                    sp.wait_ge(item_done, n - RING + 1)
                    sp.dma_start(ring_slot(n)[0:parts, 0:k * cols].rearrange("p (k n) -> p k n", k=k), src) \
                        .then_inc(ring_loaded[n % RING], 16)

                def load_up(v, s, w1=None, w3=None):
                    for i, w in enumerate((w1, w3) if w1 is not None else (moe_w1[l, v - 1], moe_w3[l, v - 1])):
                        sp.dma_start(w_up[s][:, i, :, :], w).then_inc(up_loaded[s], 16)

                def load_down(v, s, w2=None):
                    sp.dma_start(w_down[s], w2 if w2 is not None else moe_w2[l, v - 1]).then_inc(down_loaded[s], 16)

                def load_ahead(p, m):
                    for b in range(2):
                        sp.wait_ge(pair_up, 2 * p + (b + 1))
                        sp.sem_inc(wait_passed, 1)
                        load_up(2 * p + (5 + b), (2 * m + 5 + b) % E_SLOTS)
                    sp.wait_ge(expert_used, 2 * p + 1)
                    sp.sem_inc(wait_passed, 1)
                    for b in range(2):
                        load_down(2 * p + (3 + b), (2 * m + 3 + b) % E_SLOTS)

                sp.wait_ge(item_done, len(ITEMS))
                load_up(0, 0, a["shared_w1"].rearrange("l (p k) f -> l p k f", k=KD)[l],
                        a["shared_w3"].rearrange("l (p k) f -> l p k f", k=KD)[l])
                load_down(0, 0, a["shared_w2"].rearrange("l (p j) n -> l p j n", j=2)[l])
                load_up(1, 1)
                load_up(2, 2)
                load_up(3, 3)
                load_down(1, 1)
                load_down(2, 2)
                sp.wait_ge(up_done, TT)
                load_up(4, 0)
                with sp.Fori(0, (PAIRS - 2) // 2) as i:
                    for m in range(2):
                        load_ahead(2 * i + m, m)
                sp.wait_ge(expert_used, 2 * (PAIRS - 2) + 1)
                for v in (NE - 1, NE):
                    load_down(v, v % E_SLOTS)
                sp.wait_ge(listed_ready, 1)
                sp.wait_ge(pair_up, NE - 2)
                sp.wait_ge(expert_used, NE - 1)

                def load_more(n, i, j):
                    sp.wait_ge(more_pe, n * PE_STEPS + (PE_FROM - PE_STEPS))
                    sp.sem_inc(wait_passed, 1)
                    e = round_expert(sp, n)
                    for dst, src in ((w_up[MORE[j]][:, 0, :, :], moe_w1[l, e]), (w_up[MORE[j]][:, 1, :, :], moe_w3[l, e]),
                                     (w_down[MORE[j]], moe_w2[l, e])):
                        sp.dma_start(dst, src).then_inc(more_loaded[j], 16)

                further_rounds(sp, load_more)
                layer_end(sp, l)
            sp.dma_start(out.rearrange("b (t p) d -> p (b t) d", p=P), x[:, :, :]).then_inc(stored, 16)
            sp.wait_ge(stored, 16)

        @block.gpsimd
        def _(pool):
            pool.dma_start(consts[:, :], a["consts"]).then_inc(boot_dma, 16)
            pool.memset(pos_i[:, :], 0).then_inc(boot_step, 1)
            pool.wait_ge(boot_step, 1)
            pool.dma_start(pos_i[:, 0:TT], a["positions"].rearrange("b (t p) -> p (b t)", p=P),
                           allow_slow_non_contiguous=True).then_inc(boot_dma, 16)
            ends = a["positions"].rearrange("b (n s) -> (b n) s", s=CS)[1:1 + NCMP, CS - 1:CS]
            for g in range(NG):
                pool.dma_start(pos_i[g * NCMP:(g + 1) * NCMP, TT:TT + 1], ends, allow_slow_non_contiguous=True).then_inc(boot_dma, 16)
            pool.sem_inc(layer_open, 1)
            with pool.Fori(0, L) as l:
                pool.wait_ge(engine_at_end, 4 * l + 4)
                pool.sem_inc(all_at_end, 1)
                pool.sem_clear(range(numbers[0], numbers[-1] + 1))
                pool.sem_inc(layer_open, 1)

        @block.tensor
        def _(pe):
            def turn_model(src, banks_at):
                for k in range(KD):
                    for t in range(TT):
                        last = pe.transpose(ps[:, banks_at + k // 2, (k % 2 * TT + t) * P:(k % 2 * TT + t + 1) * P],
                                            src[:, t, k::KD], ident)
                return last

            def item_ready(n):
                pe.wait_ge(ring_loaded[n % RING], 16 * (n // RING + 1))

            def project(n, pair):
                cols = BANK if n != FULL_BLOCKS else LAST_COLS
                w = ring_slot(n)[:, 0:KD * cols].rearrange("p (k n) -> p k n", k=KD)
                for t in range(TT):
                    for k in range(KD):
                        last = pe.matmul(ps[:, 2 * pair + t, 0:cols], xT[:, k, t * P:(t + 1) * P], w[:, k, :],
                                         start=(k == 0), stop=(k == KD - 1))
                last.then_inc(item_done, 1)

            def full_output(act, k_chunks, half, n):
                item_ready(n)
                w = ring_slot(n)[:, 0:k_chunks * BANK].rearrange("p (k n) -> p k n", k=k_chunks)
                for t in range(TT):
                    for k in range(k_chunks):
                        last = pe.matmul(ps[:, 2 * t + half, :], act[:, k, t * P:(t + 1) * P], w[:, k, :],
                                         start=(k == 0), stop=(k == k_chunks - 1))
                return last

            def wide_output(act, n):
                item_ready(n)
                w = ring_slot(n).rearrange("p (k n) -> p k n", k=KC)
                for t in range(TT):
                    for h in range(2):
                        for k in range(KC):
                            last = pe.matmul(ps[:, 2 * t + h, :], act[:, k, t * P:(t + 1) * P],
                                             w[:, k, h * BANK:(h + 1) * BANK], start=(k == 0), stop=(k == KC - 1))
                return last

            pe.wait_ge(boot, 16)
            pe.wait_ge(boot_dma, 64)
            pe.wait_ge(layer_open, 1)
            with pe.Fori(0, L) as l:
                turn_model(x, 4).then_inc(x_turned, 1)
                pe.wait_ge(xT_act, 1)
                pe.wait_ge(xT_dve, 1)

                def start_block(n):
                    item_ready(n)
                    if n >= 2:
                        pe.wait_ge(z_written, n - 1)
                    project(n, n % 2)

                for n in range(3):
                    start_block(n)
                pe.wait_ge(chan_loaded, 64)
                for k in range(KC):
                    pe.transpose(ps[:, 6, k * CHAN_ROWS:(k + 1) * CHAN_ROWS], chan_raw[:, k::KC],
                                 ident[0:CHAN_ROWS, 0:CHAN_ROWS])
                pe.wait_ge(pe_loaded, 32)
                for v in range(2):
                    last = pe.transpose(ps[0:DH, 7, v * CB:(v + 1) * CB], pe_raw[:, v, :], ident[0:CB, 0:CB])
                last.then_inc(params_turned, 1)
                pe.wait_ge(u_ready, 1)
                for k in range(KC):
                    for t in range(TT):
                        last = pe.transpose(ps[:, 4 + k // 2, (k % 2 * TT + t) * P:(k % 2 * TT + t + 1) * P],
                                            z[:, t, Z_CA + k:Z_CA + CH:KC], ident)
                last.then_inc(u_turned, 1)
                start_block(3)
                with pe.Fori(0, (FULL_BLOCKS - 4) // 2) as i:
                    for j in range(2):
                        pe.wait_ge(ring_loaded[j], i * 16 + 48)
                        pe.wait_ge(z_written, 2 * i + j + 3)
                        project(j, j)
                start_block(FULL_BLOCKS)

                pe.wait_ge(conv_tap, TAPS * KC)
                pe.wait_ge(uT_ready, 1)
                for t in range(TT):
                    for k in range(KC):
                        last = pe.transpose(ps[:, 4 + t, k * P:(k + 1) * P], conv_acc[:, k, t * P:(t + 1) * P], ident)
                last.then_inc(conv_back, 1)
                pe.wait_ge(ret_roped, 1)
                pe.wait_ge(params_ready, 2)
                for h in range(RH):
                    if h >= 2:
                        pe.wait_ge(qk_ready, h - 1)
                    for i, off in enumerate((Z_RQ, Z_RK)):
                        for t in range(TT):
                            last = pe.transpose(ps[:, 6 + h % 2, (i * TT + t) * P:(i * TT + t + 1) * P],
                                                z[:, t, off + h * RDK:off + (h + 1) * RDK], ident)
                    last.then_inc(qk_turned, 1)
                pe.wait_ge(conv_normed, 1)
                for k in range(KC):
                    for t in range(TT):
                        last = pe.transpose(ps[:, 4 + k // 2, (k % 2 * TT + t) * P:(k % 2 * TT + t + 1) * P],
                                            z[:, t, Z_CA + k * P:Z_CA + (k + 1) * P], ident)
                last.then_inc(conv_turned, 1)
                pe.wait_ge(conv_silu, KC)
                pe.wait_ge(z_written, FULL_BLOCKS + 1)
                wide_output(yT, at["conv_pw"]).then_inc(item_done, 1)

                def ret_score(h):
                    pe.wait_ge(qk_ready, h + 1)
                    if h >= 2:
                        pe.wait_ge(ret_masked, h - 1)
                    pe.matmul(ps[:, 4 + h % 2, 0:T], qkT[:, h, 1, 0:P], qkT[:, h, 0, :], start=True, stop=True)
                    pe.matmul(ps[:, 4 + h % 2, T:T + P], qkT[:, h, 1, P:T], qkT[:, h, 0, P:T],
                              start=True, stop=True).then_inc(ret_scores, 1)

                def ret_values(h):
                    pe.wait_ge(ret_masked, h + 1)
                    if h >= 2:
                        pe.wait_ge(ret_o_copied, h - 1)
                    o = ps[:, 6 + h % 2, :]
                    v = [z[:, t, Z_RV + h * RDV:Z_RV + (h + 1) * RDV] for t in range(TT)]
                    pe.matmul(o[:, 0:RDV], ret_p[:, h % 2, 0:P], v[0], start=True, stop=True)
                    pe.matmul(o[:, RDV:2 * RDV], ret_p[:, h % 2, P:2 * P], v[0], start=True, stop=False)
                    pe.matmul(o[:, RDV:2 * RDV], ret_p[:, h % 2, 2 * P:3 * P], v[1], start=False, stop=True) \
                        .then_inc(ret_o, 1)

                ret_score(0)
                for h in range(RH):
                    if h + 1 < RH:
                        ret_score(h + 1)
                    ret_values(h)
                pe.wait_ge(ret_gated, 1)
                turn_model(ret_out, 4).then_inc(ret_turned, 1)
                pe.wait_ge(yT_act, 1)
                pe.wait_ge(yT_dve, 1)
                pe.wait_ge(y_taken, 1)
                full_output(yT, KD, 0, at["ret_o0"]).then_inc(item_done, 1)
                full_output(yT, KD, 1, at["ret_o1"]).then_inc(item_done, 1)

                pe.wait_ge(nsa_roped, 1)
                for t in range(TT):
                    for g in range(NG):
                        for h in range(HPG):
                            c = Z_NQ + (g * HPG + h) * DH
                            last = pe.transpose(ps[0:DH, 4 + t * NG + g, h * P:(h + 1) * P], z[:, t, c:c + DH], ident)
                last.then_inc(nq_turned, 1)
                pe.wait_ge(nq_ready, 4)
                for b, off in enumerate((Z_KS, Z_KW, Z_KC, Z_VC)):
                    for g in range(NG):
                        for t in range(TT):
                            last = pe.transpose(ps[0:DH, 4 + b, (g * TT + t) * P:(g * TT + t + 1) * P],
                                                z[:, t, off + g * DH:off + (g + 1) * DH], ident)
                last.then_inc(nk_turned, 1)
                pe.wait_ge(blocks_ready, 8)
                pe.wait_ge(nk_dve, 2)
                for v, name in enumerate("kv"):
                    for c in range(CB):
                        n = at[f"w1_{name}{c * 2 // CB}"]
                        if c % (CB // 2) == 0:
                            item_ready(n)
                        w = ring_slot(n)[0:DH, :].rearrange("p (c h) -> p c h", c=CB // 2)
                        for half in range(2):
                            last = pe.matmul(ps[:, 6 + half, v * 32:v * 32 + NG * NCMP],
                                             w[:, c % (CB // 2), half * P:(half + 1) * P],
                                             blocks_kv[:, v, c, :, :], start=(c == 0), stop=(c == CB - 1))
                        if c % (CB // 2) == CB // 2 - 1:
                            last.then_inc(item_done, 1)
                pe.wait_ge(hid_ready, 2)
                pe.wait_ge(w2_loaded, 32)
                pe.wait_ge(nk_act, 2)
                for half in range(2):
                    pe.matmul(ps[0:NG * NCMP, 4, 0:DH], hidT[:, 0, half, :], w2_kv[:, 0, half, :],
                              start=(half == 0), stop=(half == 1))
                for g in range(NG):
                    for half in range(2):
                        last = pe.matmul(ps[0:NCMP, 5, g * DH:(g + 1) * DH],
                                         hidT[:, 1, half, g * NCMP:(g + 1) * NCMP], w2_kv[:, 1, half, :],
                                         start=(half == 0), stop=(half == 1))
                last.then_inc(kv_cmp_done, 1)
                pe.wait_ge(kv_cmp_ready, 1)
                pe.transpose(ps[0:DH, 6, 0:NG * NCMP], k_cmp[:, :], ident[0:NG * NCMP, 0:NG * NCMP]) \
                    .then_inc(k_cmp_turned, 1)
                pe.wait_ge(k_cmp_ready, 1)
                for t in range(TT):
                    for h in range(NH):
                        g = h // HPG
                        last = pe.matmul(ps[:, 4, (t * NH + h) * NCMP:(t * NH + h + 1) * NCMP], nqT[:, t, h, :],
                                         k_cmpT[:, g * NCMP:(g + 1) * NCMP], start=True, stop=True)
                last.then_inc(cmp_scores, 1)
                pe.wait_ge(cmp_p, 1)
                pe.wait_ge(y_taken, 2)
                for t in range(TT):
                    for h in range(NH):
                        i = t * NH + h
                        last = pe.transpose(ps[0:NCMP, i // 4, (i % 4) * P:(i % 4 + 1) * P], Ec[:, t, h, :], ident)
                last.then_inc(cmp_turned, 1)
                pe.wait_ge(cmp_pT, 2)
                for t in range(TT):
                    for h in range(NH):
                        last = pe.matmul(ps[:, 6 + t, h * DH:(h + 1) * DH], pcT[:, t, h, :], v_cmp[:, h // HPG, :],
                                         start=True, stop=True)
                last.then_inc(cmp_o, 1)

                def scores(u):
                    br, t, g = UNITS[u]
                    keys = (t + 1) * P
                    if u >= 2:
                        pe.wait_ge(at_masked, u - 1)
                    for h in range(HPG):
                        c = h * keys
                        last = pe.matmul(ps[:, 2 * (u % 2) + c // BANK, c % BANK:c % BANK + keys],
                                         nqT[:, t, g * HPG + h, :], nkT[:, br, g, 0:keys], start=True, stop=True)
                    last.then_inc(at_scores, 1)

                def turn_probs(u):
                    br, t, g = UNITS[u]
                    pe.wait_ge(at_exp, u + 1)
                    if u >= 1:
                        pe.wait_ge(at_pT, u)
                    e = E[:, u % 2, 0:HPG * (t + 1) * P].rearrange("p (h k) -> p h k", h=HPG)
                    for kc in range(t + 1):
                        for h in range(HPG):
                            last = pe.transpose(ps[:, 4 + kc, h * P:(h + 1) * P], e[:, h, kc * P:(kc + 1) * P], ident)
                    last.then_inc(at_turned, 1)

                def values(u):
                    br, t, g = UNITS[u]
                    pe.wait_ge(at_pT, u + 1)
                    if u >= 2:
                        pe.wait_ge(at_o_taken, u - 1)
                    off = (Z_VS, Z_VW)[br] + g * DH
                    for h in range(HPG):
                        for kc in range(t + 1):
                            last = pe.matmul(ps[:, 6 + u % 2, h * DH:(h + 1) * DH],
                                             PT[:, (kc * HPG + h) * P:(kc * HPG + h + 1) * P],
                                             z[:, kc, off:off + DH], start=(kc == 0), stop=(kc == t))
                    last.then_inc(at_o, 1)

                scores(0)
                pe.wait_ge(cmp_o_taken, TT)
                for u in range(len(UNITS)):
                    if u + 1 < len(UNITS):
                        scores(u + 1)
                    turn_probs(u)
                    values(u)
                pe.wait_ge(nsa_ready, 1)
                for k in range(KC):
                    for t in range(TT):
                        last = pe.transpose(ps[:, 4 + k // 2, (k % 2 * TT + t) * P:(k % 2 * TT + t + 1) * P],
                                            z[:, t, Z_NQ + k:Z_NQ + NH * DH:KC], ident)
                last.then_inc(nsa_turned, 1)
                pe.wait_ge(nsa_oT, 1)
                wide_output(yT, at["nsa_o"]).then_inc(item_done, 1)

                pe.wait_ge(m_ready, 1)
                turn_model(m_buf, 4).then_inc(m_turned, 1)
                pe.wait_ge(mT_act, 1)
                pe.wait_ge(mT_dve, 1)
                full_output(xT, KD, 0, at["out0"]).then_inc(item_done, 1)
                full_output(xT, KD, 1, at["out1"]).then_inc(item_done, 1)

                pe.wait_ge(x1_ready, 1)
                turn_model(x, 4).then_inc(x1_turned, 1)
                pe.wait_ge(x1T_act, 1)
                pe.wait_ge(x1T_dve, 1)
                pe.wait_ge(router_loaded, 32)
                for t in range(TT):
                    for k in range(KD):
                        last = pe.matmul(ps[:, 7, t * NE:(t + 1) * NE], xT[:, k, t * P:(t + 1) * P], router_w[:, k, :],
                                         start=(k == 0), stop=(k == KD - 1))
                last.then_inc(router_done, 1)

                pe.sem_inc(more_pe, PE_FROM)
                def up(s, t):
                    w13 = w_up[s].rearrange("p w k f -> p k w f")
                    for k in range(KD):
                        last = pe.matmul(ps[:, 4 + t, :], xT[:, k, t * P:(t + 1) * P], w13[:, k, :, :],
                                         start=(k == 0), stop=(k == KD - 1))
                    last.then_inc(up_done, 1)

                def turn_hidden():
                    for j in range(2):
                        for t in range(TT):
                            last = pe.transpose(ps[:, 6, (j * TT + t) * P:(j * TT + t + 1) * P],
                                                hidden[:, t, j::2], ident)
                    last.then_inc(hidden_turned, 1)

                pe.wait_ge(up_loaded[0], 32)
                for t in range(TT):
                    up(0, t)
                pe.wait_ge(chosen_ready, 1)
                before, ones = const("before"), const("ones")
                pe.matmul(ps[:, 7, 2 * NE:3 * NE], before, marked[:, 0, :], start=True, stop=True)
                pe.matmul(ps[:, 7, 3 * NE:4 * NE], ones, marked[:, 0, :], start=True, stop=False)
                pe.matmul(ps[:, 7, 3 * NE:4 * NE], before, marked[:, 1, :], start=False, stop=True)
                pe.matmul(ps[:, 7, 4 * NE:5 * NE], ones, marked[:, 0, :], start=True, stop=False)
                pe.matmul(ps[:, 7, 4 * NE:5 * NE], ones, marked[:, 1, :], start=False, stop=True) \
                    .then_inc(places_done, 1)
                pe.wait_ge(hidden_done, 2)
                turn_hidden()
                pe.wait_ge(hiddenT_ready, 1)
                pe.wait_ge(down_loaded[0], 16)
                w2 = w_down[0]
                for t in range(TT):
                    for h in range(2):
                        for j in range(2):
                            last = pe.matmul(ps[:, 2 * t + h, :], hiddenT[:, j, t * P:(t + 1) * P],
                                             w2[:, j, h * BANK:(h + 1) * BANK], start=(j == 0), stop=True,
                                             skip_group_check=True)
                last.then_inc(expert_used, 1)

                def turn_picks(q, m):
                    pe.wait_ge(pick_ready, q + 1)
                    for t in range(TT):
                        last = pe.transpose(ps[:, 4, t * P:(t + 1) * P],
                                            pick_gated[:, m % 2, t, :, :].rearrange("p a s -> p (a s)"), ident)
                    last.then_inc(pick_turned, 1)

                def gather(q, m):
                    pe.wait_ge(pickT_ready, q + 1)
                    for k in range(KD):
                        for t in range(TT):
                            last = pe.matmul(ps[:, 4 + k // 4, (k % 4) * P:(k % 4 + 1) * P], x[:, t, k::KD],
                                             pick[:, m % 2, t, :, :], start=(t == 0), stop=(t == TT - 1))
                    last.then_inc(gathered, 1)

                def pair_up_products(p, m, b):
                    for w in range(2):
                        for j in range(2):
                            c = ((b * 2 + w) * 2 + j) * CAP
                            for k in range(KD):
                                last = pe.matmul(ps[:, 6, c:c + CAP], w_up[slot_of(m, b)][:, w, k, j::2],
                                                 xg[:, m % 2, k, b * CAP:(b + 1) * CAP],
                                                 start=(k == 0), stop=(k == KD - 1))
                    last.then_inc(pair_up, 1)

                def pair_down(m, h):
                    for b in range(2):
                        w2 = w_down[slot_of(m, b)]
                        for j in range(2):
                            last = pe.matmul(ps[b * CAP:(b + 1) * CAP, 7, :], hT[:, m % 2, j, b * CAP:(b + 1) * CAP],
                                             w2[:, j, h * BANK:(h + 1) * BANK], start=(j == 0), stop=(j == 1))
                        if h == 1 and b == 0:
                            last.then_inc(expert_used, 1)
                    return last

                def scatter(m, h):
                    for t in range(TT):
                        last = pe.matmul(ps[:, 2 * t + h, :], pickT[:, m, t * P:(t + 1) * P], y_slots[:, h, :],
                                         start=False, stop=True, skip_group_check=True)
                    return last

                def pair_step(p, m, has):
                    if has(0):
                        pe.wait_ge(xg_ready, p + 1)
                    if has(1):
                        turn_picks(p + 1, (m + 1) % 4)
                    if has(0):
                        pe.wait_ge(up_loaded[slot_of(m, 0)], up_loads(p, m, 0))
                        if has(-1):
                            pe.wait_ge(h_ready, 2 * p)
                        pair_up_products(p, m, 0)
                    if has(-2):
                        pe.wait_ge(y1_ready, p - 1)
                        last = scatter((m - 2) % 4, 1)
                        if not has(-1):
                            last.then_inc(main_done, 1)
                    if has(1):
                        gather(p + 1, (m + 1) % 4)
                    if has(-1):
                        pe.wait_ge(h_ready, 2 * p)
                        for b in range(2):
                            pe.wait_ge(down_loaded[slot_of(m - 1, b)], down_loads(p - 1, m - 1, b))
                        pair_down((m - 1) % 4, 0).then_inc(y0_done, 1)
                    if has(0):
                        pe.wait_ge(up_loaded[slot_of(m, 1)], up_loads(p, m, 1))
                        pe.wait_ge(h_ready, 2 * p + 1)
                        pair_up_products(p, m, 1)
                    if has(-1):
                        pe.wait_ge(y0_ready, p)
                        scatter((m - 1) % 4, 0)
                        pair_down((m - 1) % 4, 1).then_inc(expert_used, 1)

                turn_picks(0, 0)
                gather(0, 0)
                pipeline(pe, pair_step)

                def more_step(n, i, j):
                    w13, w2 = w_up[MORE[j]], w_down[MORE[j]]
                    pe.wait_ge(more_dve, n * DVE_STEPS + 2)
                    pe.sem_inc(wait_passed, 1)
                    for t in range(TT):
                        last = pe.transpose(ps[0:CAP, 4, t * P:(t + 1) * P], more_gated[:, t, :], ident)
                    last.then_inc(more_pe, 1)
                    for k in range(KD):
                        for t in range(TT):
                            last = pe.matmul(ps[:, 5, k * CAP:(k + 1) * CAP], x[:, t, k::KD], more_pick[:, t, :],
                                             start=(t == 0), stop=(t == TT - 1))
                    last.then_inc(more_pe, 1)
                    pe.wait_ge(more_act, n * ACT_STEPS + 1)
                    pe.sem_inc(wait_passed, 1)
                    pe.wait_ge(more_loaded[j], i * 48 + 48)
                    for w in range(2):
                        for f in range(2):
                            c = (w * 2 + f) * CAP
                            for k in range(KD):
                                last = pe.matmul(ps[:, 6, c:c + CAP], w13[:, w, k, f::2], more_xg[:, k, :],
                                                 start=(k == 0), stop=(k == KD - 1))
                    last.then_inc(more_pe, 1)
                    pe.wait_ge(more_dve, n * DVE_STEPS + 4)
                    for h in range(2):
                        for f in range(2):
                            last = pe.matmul(ps[0:CAP, (7, 4)[h], :], more_hT[:, f, :],
                                             w2[:, f, h * BANK:(h + 1) * BANK], start=(f == 0), stop=(f == 1))
                    last.then_inc(more_pe, 1)
                    pe.wait_ge(more_act, n * ACT_STEPS + 3)
                    pe.wait_ge(more_dve, n * DVE_STEPS + 5)
                    for t in range(TT):
                        for h in range(2):
                            last = pe.matmul(ps[:, 2 * t + h, :], more_pickT[:, t * P:(t + 1) * P], more_y[:, h, :],
                                             start=False, stop=True, skip_group_check=True)
                    last.then_inc(more_pe, 1)
                    pe.wait_ge(more_pe, n * PE_STEPS + (PE_FROM + PE_STEPS))
                    pe.sem_inc(wait_passed, 1)

                pe.wait_ge(listed_ready, 1)
                pe.wait_ge(main_done, 1)
                further_rounds(pe, more_step)
                pe.sem_inc(experts_done, 1)
                pe.wait_ge(experts_done, 1)
                layer_end(pe, l)

        @block.scalar
        def _(act):
            act.wait_ge(boot_step, 14)
            act.activation(sin[:, :, :], turn_n[:, :, :], ACT.Sin).then_inc(boot_sin, 1)
            act.activation(cos[:, :, :], cos[:, :, :], ACT.Sin).then_inc(boot_sin, 1)
            act.wait_ge(boot_sin, 2)
            act.wait_ge(layer_open, 1)
            with act.Fori(0, L) as l:
                c = Counts(act)

                def copy(dst, src, signal=act_step):
                    c.done(act.activation(dst, src, ACT.Copy), signal)

                xT_flat = xT[:, :, :].rearrange("p k t -> p (k t)")
                yT_flat = yT[:, :, :].rearrange("p k t -> p (k t)")
                act.wait_ge(x_turned, 1)
                copy(xT_flat[:, 0:2 * BANK], banks(4, 2), xT_act)

                def z_block(n):
                    cols = BANK if n != FULL_BLOCKS else LAST_COLS
                    act.wait_ge(item_done, n + 1)
                    pair = 2 * (n % 2)
                    copy(z[:, :, n * BANK:n * BANK + cols], ps[:, pair:pair + 2, 0:cols], z_written)

                z_block(0)
                z_block(1)
                c.done(act.activation(z[:, :, Z_CB:Z_CB + CH], z[:, :, Z_CB:Z_CB + CH], ACT.Sigmoid), conv_gate)
                z_block(2)
                act.wait_ge(params_turned, 1)
                copy(chan[:, :, :].rearrange("p k r -> p (k r)"), ps[:, 6, 0:KC * CHAN_ROWS], params_ready)
                copy(peT[:, :, :].rearrange("p v c -> p (v c)"), ps[0:DH, 7, 0:2 * CB], params_ready)
                act.wait_ge(u_turned, 1)
                act.wait_ge(pad_zeroed, 1)
                for b in range(2):
                    dst = u_pad[:, 2 * b:2 * b + 2, TAPS - 1:TAPS - 1 + T]
                    copy(dst, ps[:, 4 + b, :].rearrange("p (k t) -> p k t", k=2), act_step if b == 0 else uT_ready)
                z_block(3)
                with act.Fori(0, (FULL_BLOCKS - 4) // 2) as i:
                    for j in range(2):
                        act.wait_ge(item_done, 2 * i + j + 5)
                        act.activation(z[:, :, bass.ds(i * (2 * BANK) + (j + 4) * BANK, BANK)],
                                       ps[:, 2 * j:2 * j + 2, :], ACT.Copy).then_inc(z_written, 1)
                c.at[z_written.name] = FULL_BLOCKS
                act.wait_ge(z_written, FULL_BLOCKS)
                z_block(FULL_BLOCKS)
                c.done(act.activation(z[:, :, Z_NG:D_IN], z[:, :, Z_NG:D_IN], ACT.Sigmoid), gates_ready)
                c.done(act.activation(z[:, :, Z_RG:Z_RG + RH * RDV], z[:, :, Z_RG:Z_RG + RH * RDV], ACT.Silu),
                       ret_gate_ready)

                def root(n):
                    act.wait_ge(var_ready, c.at.get(std_ready.name, 0) + 1)
                    c.done(act.activation(rstd[:, 0:n], rstd[:, 0:n], ACT.Sqrt), std_ready)

                for h in range(RH):
                    act.wait_ge(qk_turned, h + 1)
                    copy(qkT[:, h, :, :].rearrange("p i t -> p (i t)"), ps[:, 6 + h % 2, :], qk_ready)
                root(TT)
                act.wait_ge(conv_turned, 1)
                for k in range(KC):
                    c.done(act.activation(yT[:, k, :], ps[:, 4 + k // 2, (k % 2) * T:(k % 2 + 1) * T], ACT.Silu,
                                          bias=chan[:, k, TAPS + 2:TAPS + 3], scale=chan[:, k, TAPS + 1:TAPS + 2]),
                           conv_silu)
                for h in range(RH):
                    act.wait_ge(ret_o, h + 1)
                    copy(ret_out[:, :, h * RDV:(h + 1) * RDV],
                         ps[:, 6 + h % 2, :].rearrange("p (t v) -> p t v", t=TT), ret_o_copied)
                root(RH * TT)
                act.wait_ge(ret_turned, 1)
                copy(yT_flat[:, 0:2 * BANK], banks(4, 2), yT_act)
                act.wait_ge(nq_turned, 1)
                for t in range(TT):
                    for g in range(NG):
                        c.done(act.activation(nqT[:, t, g * HPG:(g + 1) * HPG, :].rearrange("p h q -> p (h q)"),
                                              ps[0:DH, 4 + t * NG + g, :], ACT.Copy, scale=DH ** -0.5), nq_ready)
                act.wait_ge(nk_turned, 1)
                for b in range(2):
                    copy(nkT[:, b, :, :].rearrange("p g t -> p (g t)"), ps[0:DH, 4 + b, :], nk_act)
                act.wait_ge(item_done, at["w1_v1"] + 1)
                for half in range(2):
                    c.done(act.activation(hidT[:, :, half, :],
                                          ps[:, 6 + half, 0:64].rearrange("p (v n) -> p v n", v=2)[:, :, 0:NG * NCMP],
                                          ACT.Silu), hid_ready)
                act.wait_ge(k_cmp_turned, 1)
                copy(k_cmpT[:, :], ps[0:DH, 6, 0:NG * NCMP], k_cmp_ready)
                act.wait_ge(cmp_shifted, 1)
                c.done(act.activation(Ec[:, :, :, :], Ec[:, :, :, :], ACT.Exp), cmp_exp)
                act.wait_ge(cmp_turned, 1)
                for t in range(TT):
                    copy(pcT[:, t, :, :].rearrange("p h q -> p (h q)"), banks(2 * t, 2)[0:NCMP, :], cmp_pT)

                def exps(u):
                    br, t, g = UNITS[u]
                    keys = (t + 1) * P
                    act.wait_ge(at_max, u + 1)
                    for h in range(HPG):
                        e = E[:, u % 2, h * keys:(h + 1) * keys]
                        c.done(act.activation(e, e, ACT.Exp, bias=negmax[:, (u % 2) * HPG + h:(u % 2) * HPG + h + 1],
                                              accum_out=den[:, u, h:h + 1]), at_exp if h == HPG - 1 else act_step)

                def probs(u):
                    n = HPG * (UNITS[u][1] + 1) * P
                    act.wait_ge(at_turned, u + 1)
                    if u >= 1:
                        act.wait_ge(at_o, u)
                    copy(PT[:, 0:n], banks(4, 2)[:, 0:n], at_pT)

                exps(0)
                for u in range(len(UNITS)):
                    if u + 1 < len(UNITS):
                        exps(u + 1)
                    probs(u)
                act.wait_ge(nsa_turned, 1)
                copy(yT_flat[:, 0:2 * BANK], banks(4, 2), nsa_oT)
                act.wait_ge(m_turned, 1)
                copy(xT_flat[:, 0:2 * BANK], banks(4, 2), mT_act)
                root(TT)
                act.wait_ge(x1_turned, 1)
                copy(xT_flat[:, 0:2 * BANK], banks(4, 2), x1T_act)
                act.wait_ge(router_done, 1)
                c.done(act.activation(score[:, :, :].rearrange("p t e -> p (t e)"), ps[:, 7, 0:TT * NE], ACT.Sigmoid),
                       score_ready)

                def silu(t):
                    act.activation(silu_a[:, t, :], ps[:, 4 + t, 0:FE], ACT.Silu).then_inc(silu_done, 1)

                def copy_hidden():
                    act.activation(hiddenT.rearrange("p j t -> p (j t)"), ps[:, 6, :], ACT.Copy) \
                        .then_inc(hiddenT_ready, 1)

                for t in range(TT):
                    act.wait_ge(up_done, t + 1)
                    silu(t)
                act.wait_ge(hidden_turned, 1)
                copy_hidden()

                def copy_gathered(q, m):
                    act.wait_ge(gathered, q + 1)
                    act.activation(xg[:, m % 2, :, :].rearrange("p k s -> p (k s)"), banks(4, 2), ACT.Copy) \
                        .then_inc(xg_ready, 1)

                def pair_silu_of(p, m, b):
                    act.wait_ge(pair_up, 2 * p + (b + 1))
                    act.activation(silu_pair_buf[:, b, :, :].rearrange("p j s -> p (j s)"),
                                   ps[:, 6, b * 4 * CAP:(b * 4 + 2) * CAP], ACT.Silu).then_inc(pair_silu, 1)

                def pair_step(p, m, has):
                    if has(0):
                        pair_silu_of(p, m, 0)
                    if has(1):
                        copy_gathered(p + 1, (m + 1) % 4)
                    if has(-1):
                        act.wait_ge(y0_done, p)
                        act.activation(y_slots[:, 0, :], ps[:, 7, :], ACT.Copy).then_inc(y0_ready, 1)
                    if has(0):
                        pair_silu_of(p, m, 1)

                copy_gathered(0, 0)
                pipeline(act, pair_step)

                def more_step(n, i, j):
                    act.wait_ge(more_pe, n * PE_STEPS + (PE_FROM + 2))
                    act.activation(more_xg.rearrange("p k s -> p (k s)"), ps[:, 5, :], ACT.Copy).then_inc(more_act, 1)
                    act.wait_ge(more_pe, n * PE_STEPS + (PE_FROM + 3))
                    act.activation(more_silu.rearrange("p j s -> p (j s)"), ps[:, 6, 0:2 * CAP], ACT.Silu) \
                        .then_inc(more_act, 1)
                    act.wait_ge(more_pe, n * PE_STEPS + (PE_FROM + 4))
                    act.activation(more_y[:, 0, :], ps[0:CAP, 7, :], ACT.Copy).then_inc(more_act, 1)
                    act.wait_ge(more_pe, n * PE_STEPS + (PE_FROM + 5))
                    act.sem_inc(wait_passed, 1)

                act.wait_ge(listed_ready, 1)
                act.wait_ge(main_done, 1)
                further_rounds(act, more_step)
                root(TT)
                layer_end(act, l)

        @block.vector
        def _(dve):
            magic = 1.5 * 2.0 ** 23
            c1, c2 = 6.28125, 0.0019340515136718750
            c3 = float(2 * np.pi - c1 - c2)
            boot_count = [1]

            def boot_done(ins):
                ins.then_inc(boot_step, 1)
                boot_count[0] += 1
                dve.wait_ge(boot_step, boot_count[0])

            dve.wait_ge(boot_dma, 64)
            dve.wait_ge(boot_step, 1)
            boot_done(dve.tensor_copy(pos[:, :], pos_i[:, :]))
            for i in range(TT + 1):
                boot_done(dve.tensor_scalar(sin[:, i, :], const("freq"), pos[:, i:i + 1], None, ALU.mult))
            boot_done(dve.tensor_scalar(turn_n[:, :, :], sin[:, :, :], float(1 / (2 * np.pi)), magic, ALU.mult, ALU.add))
            boot_done(dve.tensor_scalar(turn_n[:, :, :], turn_n[:, :, :], magic, None, ALU.subtract))
            for part in (c1, c2, c3):
                boot_done(dve.scalar_tensor_tensor(out=sin[:, :, :], in0=turn_n[:, :, :], scalar=-part,
                                                   in1=sin[:, :, :], op0=ALU.mult, op1=ALU.add))
            lim = 3.1415925
            boot_done(dve.tensor_scalar(turn_n[:, :, :], sin[:, :, :], lim, -lim, ALU.min, ALU.max))
            boot_done(dve.tensor_scalar(cos[:, :, :], turn_n[:, :, :], -1.0, None, ALU.mult))
            boot_done(dve.tensor_tensor(cos[:, :, :], cos[:, :, :], turn_n[:, :, :], ALU.min))
            boot_done(dve.tensor_scalar(cos[:, :, :], cos[:, :, :], float(np.pi / 2), None, ALU.add))
            assert boot_count[0] == 14, boot_count
            dve.wait_ge(boot_sin, 2)
            dve.wait_ge(layer_open, 1)

            with dve.Fori(0, L) as l:
                c = Counts(dve)

                def do(ins, signal=dve_step):
                    c.done(ins, signal)

                def tt(dst, in0, in1, op, signal=dve_step):
                    do(dve.tensor_tensor(dst, in0, in1, op), signal)

                def rope(x1, x2, co, si, tmp, signal=dve_step):
                    tt(tmp[0], x1, co, ALU.mult)
                    tt(tmp[1], x2, si, ALU.mult)
                    tt(tmp[2], x2, co, ALU.mult)
                    tt(tmp[3], x1, si, ALU.mult)
                    tt(x1, tmp[0], tmp[1], ALU.subtract)
                    tt(x2, tmp[2], tmp[3], ALU.add, signal)

                def mean_rstd(n):
                    do(dve.tensor_scalar(rstd[:, 0:n], mv[:, 0:n, 1], EPS, None, ALU.add), var_ready)
                    dve.wait_ge(std_ready, c.at[var_ready.name])
                    do(dve.reciprocal(rstd[:, 0:n], rstd[:, 0:n]))

                xT_flat = xT[:, :, :].rearrange("p k t -> p (k t)")
                yT_flat = yT[:, :, :].rearrange("p k t -> p (k t)")
                dve.wait_ge(x_turned, 1)
                do(dve.tensor_copy(xT_flat[:, 2 * BANK:], banks(6, 2)), xT_dve)
                do(dve.memset(u_pad[:, :, 0:TAPS - 1], 0.0), pad_zeroed)

                dve.wait_ge(conv_gate, 1)
                tt(z[:, :, Z_CA:Z_CA + CH], z[:, :, Z_CA:Z_CA + CH], z[:, :, Z_CB:Z_CB + CH], ALU.mult, u_ready)
                dve.wait_ge(params_ready, 2)
                dve.wait_ge(uT_ready, 1)
                for k in range(KC):
                    dve.tensor_scalar(conv_acc[:, k, :], u_pad[:, k, 0:T], chan[:, k, 0:1], chan[:, k, TAPS:TAPS + 1],
                                      ALU.mult, ALU.add).then_inc(conv_tap, 1)
                with dve.Fori(0, (TAPS - 1) // 2) as i:
                    for j in range(2):
                        for k in range(KC):
                            dve.wait_ge(conv_tap, i * (2 * KC) + (j * KC + k + 1))
                            dve.scalar_tensor_tensor(out=conv_acc[:, k, :], in0=u_pad[:, k, bass.ds(2 * i + (j + 1), T)],
                                                     scalar=chan[:, k, bass.ds(2 * i + (j + 1), 1)],
                                                     in1=conv_acc[:, k, :], op0=ALU.mult, op1=ALU.add) \
                                .then_inc(conv_tap, 1)
                dve.wait_ge(conv_tap, TAPS * KC)

                dve.wait_ge(z_written, Z_RV // BANK)
                halves = z[:, :, Z_RQ:Z_RV].rearrange("p t (h i f) -> p t h i f", i=2, f=RF)
                nh = 2 * RH
                tmp = [E[:, 1, 0:512], E[:, 1, 512:1024], PT[:, 0:512], PT[:, 512:1024]]
                tmp = [t_.rearrange("p (h f) -> p h f", h=nh) for t_ in tmp]
                for t in range(TT):
                    co, si = [w[:, t, 0:RF].unsqueeze(1).to_broadcast([P, nh, RF]) for w in (cos, sin)]
                    rope(halves[:, t, :, 0, :], halves[:, t, :, 1, :], co, si, tmp,
                         ret_roped if t == TT - 1 else dve_step)
                dve.wait_ge(z_written, Z_NG // BANK + 1)
                for t in range(TT):
                    for off, heads in ((Z_NQ, NH), (Z_KS, NG), (Z_KW, NG)):
                        v = z[:, t, off:off + heads * DH].rearrange("p (h f) -> p h f", h=heads)
                        co, si = [w[:, t, RF:FR].unsqueeze(1).to_broadcast([P, heads, NF]) for w in (cos, sin)]
                        small = [t_[:, 0:heads, 0:NF] for t_ in tmp]
                        rope(v[:, :, 0:NF], v[:, :, NF:ROT], co, si, small,
                             nsa_roped if (t, off) == (TT - 1, Z_KW) else dve_step)

                dve.wait_ge(conv_back, 1)
                for t in range(TT):
                    do(dve.bn_stats(stats[:, t, :], ps[:, 4 + t, :]))
                    do(dve.bn_aggr(mv[:, t, :], stats[:, t, :]))
                mean_rstd(TT)
                for t in range(TT):
                    do(dve.tensor_scalar(z[:, t, Z_CA:Z_CA + CH], ps[:, 4 + t, :], mv[:, t, 0:1], rstd[:, t:t + 1],
                                         ALU.subtract, ALU.mult), conv_normed if t == TT - 1 else dve_step)

                def merge(branch, signal):
                    for t in range(TT):
                        gate = z[:, t, Z_MG + branch * D:Z_MG + (branch + 1) * D]
                        last = t == TT - 1
                        if branch == 0:
                            tt(m_buf[:, t, :], gate, banks(2 * t, 2), ALU.mult, y_taken if last else dve_step)
                        else:
                            tt(E[:, t, :], gate, banks(2 * t, 2), ALU.mult, y_taken if last else dve_step)
                    if branch:
                        tt(m_buf, m_buf, E[:, :, :], ALU.add, signal)

                dve.wait_ge(item_done, at["conv_pw"] + 1)
                dve.wait_ge(gates_ready, 1)
                merge(0, None)

                def decay_scores(h):
                    dve.wait_ge(ret_scores, h + 1)
                    if h >= 2:
                        dve.wait_ge(ret_o, h - 1)
                    tt(ret_p[:, h % 2, 0:T], ps[:, 4 + h % 2, 0:T], decay[:, h, :], ALU.mult)
                    tt(ret_p[:, h % 2, T:T + P], ps[:, 4 + h % 2, T:T + P], decay[:, h, 0:P], ALU.mult, ret_masked)

                decay_scores(0)
                for h in range(RH):
                    if h + 1 < RH:
                        decay_scores(h + 1)
                    dve.wait_ge(ret_o_copied, h + 1)
                    for t in range(TT):
                        i = h * TT + t
                        do(dve.bn_stats(stats[:, i, :], ret_out[:, t, h * RDV:(h + 1) * RDV]))
                        do(dve.bn_aggr(mv[:, i, :], stats[:, i, :]))
                mean_rstd(RH * TT)
                dve.wait_ge(ret_gate_ready, 1)
                for h in range(RH):
                    for t in range(TT):
                        i = h * TT + t
                        o = ret_out[:, t, h * RDV:(h + 1) * RDV]
                        do(dve.tensor_scalar(o, o, mv[:, i, 0:1], rstd[:, i:i + 1], ALU.subtract, ALU.mult))
                tt(ret_out, ret_out, z[:, :, Z_RG:Z_RG + RH * RDV], ALU.mult, ret_gated)
                dve.wait_ge(ret_turned, 1)
                do(dve.tensor_copy(yT_flat[:, 2 * BANK:], banks(6, 2)), yT_dve)
                dve.wait_ge(item_done, at["ret_o1"] + 1)
                merge(1, dve_step)

                dve.wait_ge(nk_turned, 1)
                for v in range(2):
                    do(dve.tensor_copy(cT[:, v, :, :].rearrange("p g t -> p (g t)"), ps[0:DH, 6 + v, :]), nk_dve)
                for v in range(2):
                    for g in range(NG):
                        by_stride = cT[:, v, g, :].rearrange("p (m s) -> p s m", s=CS)
                        for c2 in range(CB // CS):
                            tt(blocks_kv[:, v, c2 * CS:(c2 + 1) * CS, g, :], by_stride[:, :, c2:c2 + NCMP],
                               peT[:, v, c2 * CS:(c2 + 1) * CS].unsqueeze(2).to_broadcast([DH, CS, NCMP]),
                               ALU.add, blocks_ready)
                dve.wait_ge(kv_cmp_done, 1)
                kn = NG * NCMP
                do(dve.tensor_copy(k_cmp[:, :], ps[0:kn, 4, 0:DH]))
                co, si = cos[0:kn, TT, RF:FR], sin[0:kn, TT, RF:FR]
                rope(k_cmp[:, 0:NF], k_cmp[:, NF:ROT], co, si, [E[0:kn, 0, i * NF:(i + 1) * NF] for i in range(4)])
                do(dve.tensor_copy(v_cmp[:, :, :].rearrange("p g d -> p (g d)"), ps[0:NCMP, 5, 0:NG * DH]), kv_cmp_ready)

                dve.wait_ge(cmp_scores, 1)
                s = ps[:, 4, 0:TT * NH * NCMP].rearrange("p (t h n) -> p t h n", t=TT, h=NH)
                bc = [P, NH, NCMP]
                for t in range(TT):
                    tt(Ec[:, t, :, :], s[:, t, :, :], cmp_add[:, t, :].unsqueeze(1).to_broadcast(bc), ALU.add)
                flat = Ec[:, :, :, :].rearrange("p t h n -> p (t h) n")
                do(dve.tensor_reduce(negmax[:, :], flat, AX.X, ALU.max, negate=True))
                tt(flat, flat, negmax[:, :].unsqueeze(2).to_broadcast([P, TT * NH, NCMP]), ALU.add, cmp_shifted)
                dve.wait_ge(cmp_exp, 1)
                do(dve.tensor_reduce(coef[:, :], flat, AX.X, ALU.add))
                for t in range(TT):
                    tt(Ec[:, t, :, :], Ec[:, t, :, :], cmp_01[:, t, :].unsqueeze(1).to_broadcast(bc), ALU.mult,
                       cmp_p if t == TT - 1 else dve_step)
                do(dve.reciprocal(coef[:, :], coef[:, :]))
                gate3 = z[:, :, Z_NG:Z_NG + NH * 3].rearrange("p t (h b) -> p t h b", b=3)
                tt(coef[:, :].rearrange("p (t h) -> p t h", t=TT), coef[:, :].rearrange("p (t h) -> p t h", t=TT),
                   gate3[:, :, :, 0], ALU.mult)
                dve.wait_ge(cmp_o, 1)
                for t in range(TT):
                    tt(nsa_out[:, t, :].rearrange("p (h d) -> p h d", h=NH), ps[:, 6 + t, :].rearrange("p (h d) -> p h d", h=NH),
                       coef[:, t * NH:(t + 1) * NH].unsqueeze(2).to_broadcast([P, NH, DH]), ALU.mult, cmp_o_taken)

                def mask_scores(u):
                    br, t, g = UNITS[u]
                    keys = (t + 1) * P
                    dve.wait_ge(at_scores, u + 1)
                    if u >= 2:
                        dve.wait_ge(at_turned, u - 1)
                    e = E[:, u % 2, 0:HPG * keys].rearrange("p (h k) -> p h k", h=HPG)
                    sc = banks(2 * (u % 2), 2)[:, 0:HPG * keys].rearrange("p (h k) -> p h k", h=HPG)
                    mk = mask[:, 2 * P - keys:2 * P].unsqueeze(1).to_broadcast([P, HPG, keys])
                    tt(e, sc, mk, ALU.add, at_masked)
                    do(dve.tensor_reduce(negmax[:, (u % 2) * HPG:(u % 2 + 1) * HPG], e, AX.X, ALU.max, negate=True),
                       at_max)

                def add_output(u):
                    br, t, g = UNITS[u]
                    dve.wait_ge(at_o, u + 1)
                    w = coef[:, 0:HPG]
                    do(dve.reciprocal(w, den[:, u, :]))
                    tt(w, w, gate3[:, t, g * HPG:(g + 1) * HPG, br + 1], ALU.mult)
                    add = silu_a[:, 0, :].rearrange("p (h d) -> p h d", h=HPG)
                    tt(add, ps[:, 6 + u % 2, 0:HPG * DH].rearrange("p (h d) -> p h d", h=HPG),
                       w.unsqueeze(2).to_broadcast([P, HPG, DH]), ALU.mult, at_o_taken)
                    o = nsa_out[:, t, g * HPG * DH:(g + 1) * HPG * DH]
                    tt(o, o, silu_a[:, 0, :], ALU.add, nsa_ready if u == len(UNITS) - 1 else dve_step)

                mask_scores(0)
                for u in range(len(UNITS)):
                    if u + 1 < len(UNITS):
                        mask_scores(u + 1)
                    add_output(u)
                dve.wait_ge(item_done, at["nsa_o"] + 1)
                merge(2, m_ready)
                dve.wait_ge(m_turned, 1)
                do(dve.tensor_copy(xT_flat[:, 2 * BANK:], banks(6, 2)), mT_dve)

                def residual_norm(which, signal):
                    for t in range(TT):
                        do(dve.scalar_tensor_tensor(out=x[:, t, :], in0=x[:, t, :], scalar=ALPHA, in1=banks(2 * t, 2),
                                                    op0=ALU.mult, op1=ALU.add), y_taken)
                        for h in range(2):
                            do(dve.bn_stats(stats[:, 2 * t + h, :], x[:, t, h * BANK:(h + 1) * BANK]))
                        do(dve.bn_aggr(mv[:, t, :], stats[:, 2 * t:2 * t + 2, :].rearrange("p a b -> p (a b)")))
                    mean_rstd(TT)
                    for t in range(TT):
                        do(dve.tensor_scalar(x[:, t, :], x[:, t, :], mv[:, t, 0:1], rstd[:, t:t + 1],
                                             ALU.subtract, ALU.mult))
                    gain, bias = [norm[:, 2 * which + i, :].unsqueeze(1).to_broadcast([P, TT, D]) for i in range(2)]
                    tt(x[:, :, :], x[:, :, :], gain, ALU.mult)
                    tt(x[:, :, :], x[:, :, :], bias, ALU.add, signal)

                dve.wait_ge(item_done, at["out1"] + 1)
                dve.wait_ge(norm_loaded, 64)
                residual_norm(0, x1_ready)
                dve.wait_ge(x1_turned, 1)
                do(dve.tensor_copy(xT_flat[:, 2 * BANK:], banks(6, 2)), x1T_dve)

                dve.wait_ge(score_ready, 1)
                dve.wait_ge(router_loaded, 32)
                tt(biased[:, :, :], score[:, :, :], router_b[:, :].unsqueeze(1).to_broadcast([P, TT, NE]), ALU.add)
                per = NE // NEG_
                for t in range(TT):
                    for g in range(NEG_):
                        do(dve.max(best[:, t, g, :], biased[:, t, g * per:(g + 1) * per]))
                do(dve.memset(group[:, :, :], -NEG))
                tt(group[:, :, 0:NEG_], best[:, :, :, 0], best[:, :, :, 1], ALU.add)
                for t in range(TT):
                    do(dve.max(top[:, :], group[:, t, :]))
                    do(dve.match_replace(group_out[:, t, :], top[:, :], group[:, t, :], NEG))
                kept = group_out[:, :, 0:NEG_]
                do(dve.tensor_scalar(kept, kept, NEG, NEG, ALU.not_equal, ALU.mult))
                for t in range(TT):
                    e3 = biased[:, t, :].rearrange("p (g e) -> p g e", g=NEG_)
                    tt(e3, e3, group_out[:, t, 0:NEG_].unsqueeze(2).to_broadcast([P, NEG_, per]), ALU.add)
                    do(dve.max(top[:, :], biased[:, t, :]))
                    do(dve.match_replace(marked[:, t, :], top[:, :], biased[:, t, :], 2 * NEG))
                do(dve.tensor_scalar(marked[:, :, :], marked[:, :, :], 2 * NEG, None, ALU.is_equal))
                tt(biased[:, :, :], marked[:, :, :], score[:, :, :], ALU.mult, chosen_ready)
                do(dve.tensor_reduce(total[:, :], biased[:, :, :], AX.X, ALU.add))
                do(dve.reciprocal(total[:, :], total[:, :]))
                do(dve.memset(gates[:, :, 0:1], 1.0))
                for t in range(TT):
                    do(dve.tensor_scalar(gates[:, t, 1:E_ALL], biased[:, t, :], total[:, t:t + 1], SCALE_ROUTED,
                                         ALU.mult, ALU.mult))

                for t in range(TT):
                    dve.wait_ge(silu_done, t + 1)
                    tt(hidden[:, t, :], ps[:, 4 + t, FE:2 * FE], silu_a[:, t, :], ALU.mult, hidden_done)

                dve.wait_ge(places_done, 1)
                do(dve.scalar_tensor_tensor(out=place[:, :, :],
                                            in0=ps[:, 7, 2 * NE:4 * NE].rearrange("p (t e) -> p t e", t=TT), scalar=1.0,
                                            in1=marked[:, :, :], op0=ALU.add, op1=ALU.mult))
                do(dve.tensor_copy(counts[:, :], ps[0:1, 7, 4 * NE:5 * NE]))

                def list_rounds():
                    wanted = more_rows[:, 0, NE:]
                    do(dve.memset(more_rows[:, :, :], 0.0))
                    for b in range(1, ROUNDS):
                        do(dve.scalar_tensor_tensor(out=wanted, in0=counts[:, :], scalar=float(b * CAP), in1=wanted,
                                                    op0=ALU.is_gt, op1=ALU.add))
                    src, shift = 0, 1
                    while shift < NE:
                        dst = 1 if src != 1 else 2
                        tt(more_rows[:, dst, NE:], more_rows[:, src, NE:], more_rows[:, src, NE - shift:2 * NE - shift],
                           ALU.add)
                        src, shift = dst, shift * 2
                    sums = more_rows[:, src, NE:]
                    shape = [1, MAX_MORE, NE]
                    nth = const("count")[0:1, 0:MAX_MORE]
                    tt(passed, sums.unsqueeze(1).to_broadcast(shape), nth.unsqueeze(2).to_broadcast(shape), ALU.is_lt)
                    experts, starts = [more_rows[:, 3, i * MAX_MORE:(i + 1) * MAX_MORE] for i in range(2)]
                    do(dve.tensor_reduce(experts, passed, AX.X, ALU.add))
                    tt(passed, passed, wanted.unsqueeze(1).to_broadcast(shape), ALU.mult)
                    do(dve.tensor_reduce(starts, passed, AX.X, ALU.add))
                    tt(starts, nth, starts, ALU.subtract)
                    do(dve.tensor_scalar(starts, starts, float(CAP), None, ALU.mult))
                    do(dve.tensor_copy(listed[:, 0:1], sums[:, NE - 1:NE]))
                    do(dve.tensor_copy(listed[:, 1:], more_rows[:, 3, 0:2 * MAX_MORE]), listed_ready)

                slots = const("count")[:, 0:CAP]

                def make_picks(q, m):
                    shape = [P, TT, 2, CAP]
                    sel, gated = pick[:, m % 2, :, :, :], pick_gated[:, m % 2, :, :, :]
                    at_e = place[:, :, bass.ds(2 * q, 2)].unsqueeze(3).to_broadcast(shape)
                    dve.tensor_tensor(sel, slots.unsqueeze(1).unsqueeze(1).to_broadcast(shape), at_e, ALU.is_equal) \
                        .then_inc(pick_made, 1)
                    dve.wait_ge(pick_made, q + 1)
                    dve.tensor_tensor(gated, sel, gates[:, :, bass.ds(2 * q + 1, 2)].unsqueeze(3).to_broadcast(shape),
                                      ALU.mult).then_inc(pick_ready, 1)

                def copy_picks(q, m):
                    dve.wait_ge(pick_turned, q + 1)
                    dve.tensor_copy(pickT[:, m, :], ps[:, 4, 0:T]).then_inc(pickT_ready, 1)

                def pair_hidden(p, m, b):
                    dve.wait_ge(pair_silu, 2 * p + (b + 1))
                    dve.tensor_tensor(hT[:, m % 2, :, b * CAP:(b + 1) * CAP],
                                      ps[:, 6, (b * 4 + 2) * CAP:(b * 4 + 4) * CAP].rearrange("p (j s) -> p j s", j=2),
                                      silu_pair_buf[:, b, :, :], ALU.mult).then_inc(h_ready, 1)

                def pair_step(p, m, has):
                    if has(1):
                        copy_picks(p + 1, (m + 1) % 4)
                    if has(2):
                        if has(0):
                            dve.wait_ge(gathered, p + 1)
                        make_picks(p + 2, (m + 2) % 4)
                    if has(0):
                        pair_hidden(p, m, 0)
                        if isinstance(p, int) and p == 1:
                            list_rounds()
                        pair_hidden(p, m, 1)
                    if has(-1):
                        dve.wait_ge(expert_used, 2 * p + 1)
                        dve.tensor_copy(y_slots[:, 1, :], ps[:, 7, :]).then_inc(y1_ready, 1)

                make_picks(0, 0)
                make_picks(1, 1)
                copy_picks(0, 0)
                pipeline(dve, pair_step)

                def more_step(n, i, j):
                    shape = [P, TT, CAP]
                    e, first = round_expert(dve, n), round_start(dve, n)
                    step = lambda ins, k: (ins.then_inc(more_dve, 1), dve.wait_ge(more_dve, n * DVE_STEPS + k))
                    at_e = place[:, :, bass.ds(e, 1)].to_broadcast(shape)
                    span = const("count")[:, bass.ds(first, CAP)].unsqueeze(1).to_broadcast(shape)
                    step(dve.tensor_tensor(more_pick, span, at_e, ALU.is_equal), 1)
                    step(dve.tensor_tensor(more_gated, more_pick, gates[:, :, bass.ds(e + 1, 1)].to_broadcast(shape),
                                           ALU.mult), 2)
                    dve.wait_ge(more_pe, n * PE_STEPS + (PE_FROM + 1))
                    step(dve.tensor_copy(more_pickT, ps[0:CAP, 4, 0:T]), 3)
                    dve.wait_ge(more_act, n * ACT_STEPS + 2)
                    step(dve.tensor_tensor(more_hT, ps[:, 6, 2 * CAP:4 * CAP].rearrange("p (j s) -> p j s", j=2),
                                           more_silu, ALU.mult), 4)
                    dve.wait_ge(more_pe, n * PE_STEPS + (PE_FROM + 4))
                    step(dve.tensor_copy(more_y[:, 1, :], ps[0:CAP, 4, :]), 5)
                    dve.wait_ge(more_pe, n * PE_STEPS + (PE_FROM + 5))
                    dve.sem_inc(wait_passed, 1)

                dve.wait_ge(main_done, 1)
                further_rounds(dve, more_step)
                dve.wait_ge(experts_done, 1)
                residual_norm(1, dve_step)
                layer_end(dve, l)


_INS = ["x", "positions", "w_in", "conv_dw", "conv_db", "conv_ln_g", "conv_ln_b", "conv_w_pw", "ret_w_o",
        "nsa_pe_k", "nsa_w1_k", "nsa_w2_k", "nsa_pe_v", "nsa_w1_v", "nsa_w2_v", "nsa_w_o", "w_out",
        "ln1_g", "ln1_b", "router_w", "router_b", "moe_w1", "moe_w3", "moe_w2",
        "shared_w1", "shared_w3", "shared_w2", "ln2_g", "ln2_b"]


def kernel(**inputs):
    import numpy as _np
    import concourse.bacc as _bacc
    from concourse import mybir as _mybir
    from concourse.bass_utils import run_bass_kernel_spmd as _run

    nc = _bacc.Bacc("TRN2", target_bir_lowering=False, num_devices=1)
    arrays, args = {}, {}
    for name in _INS + ["consts"]:
        v = _np.ascontiguousarray(shape_constants() if name == "consts" else inputs[name])
        arrays[f"in_{name}_dram"] = v
        args[name] = nc.dram_tensor(f"in_{name}_dram", v.shape, _mybir.dt.from_np(v.dtype), kind="ExternalInput").ap()
    out = nc.dram_tensor("out_0_dram", (1, T, D), _mybir.dt.float32, kind="ExternalOutput").ap()
    build(nc, args, out)
    r = _run(nc, [arrays], core_ids=[0])
    return r.results[0]["out_0_dram"]
```

```python
from contextlib import ExitStack

import numpy as np

import concourse.bass as bass
from concourse import mybir

F32 = mybir.dt.float32
I32 = mybir.dt.int32
F32R = mybir.dt.float32r
ALU = mybir.AluOpType
ACT = mybir.ActivationFunctionType
AX = mybir.AxisListType

P = 128
L = 2
T = 256
TT = T // P
D = 1024
KD = D // P
CH = 512
KC = CH // P
TAPS = 31
RH, RDK, RDV = 4, 128, 256
NH, NG, DH = 8, 2, 64
HPG = NH // NG
CB, CS = 32, 16
NCMP = (T - CB) // CS + 1
CHID = 256
ROT = DH // 4
NE, NEG_, TOPG, TOPK = 64, 8, 4, 8
FE = 256
SCALE_ROUTED = 2.5
ALPHA = (2.0 * L) ** 0.25
EPS = 1e-5
NEG = -1e30
BANK = 512

WIDTHS = (CH, CH, RH * RDK, RH * RDK, RH * RDV, RH * RDV, NH * DH) + (NG * DH,) * 6 + (NH * 3, 3 * D)
(Z_CA, Z_CB, Z_RQ, Z_RK, Z_RV, Z_RG, Z_NQ, Z_KC, Z_VC, Z_KS, Z_VS, Z_KW, Z_VW, Z_NG, Z_MG, D_IN) = \
    [sum(WIDTHS[:i]) for i in range(len(WIDTHS) + 1)]
FULL_BLOCKS = D_IN // BANK
LAST_COLS = D_IN - FULL_BLOCKS * BANK

ITEMS = ["in"] * (FULL_BLOCKS + 1) + ["conv_pw", "ret_o0", "ret_o1", "w1_k", "w1_v",
                                      "nsa_o", "out0", "out1"]
RING = 2
SLOT = KD * BANK
EXPERT = 3 * KD * FE
E_SLOTS = 4
CAP = 64
PAIRS = NE // 2
ROUNDS = T // CAP
MAX_MORE = T * TOPK // CAP
E_ALL = NE + 1
Z0 = RING * SLOT
ARENA = max(Z0 + TT * D_IN, E_SLOTS * EXPERT)

CHAN_ROWS = TAPS + 3
RF = RDK // 2
NF = ROT // 2
FR = RF + NF
CONSTS = {"ident": P, "decay": RH * T, "mask": 2 * P, "cmp_add": TT * NCMP, "cmp_01": TT * NCMP, "freq": FR,
          "before": P, "ones": P, "count": T + CAP}


def shape_constants():
    f = np.float32
    p = np.arange(P)
    out = {"ident": np.eye(P, dtype=f)}
    log_gamma = np.log1p(-np.exp2(f(-5.0) - np.arange(RH, dtype=f))).astype(f)
    diff = np.arange(T)[None, :] - p[:, None]
    full = np.where(diff >= 0, np.exp(log_gamma[:, None, None] * np.maximum(diff, 0).astype(f)), 0) * f(RDK ** -0.5)
    out["decay"] = full.transpose(1, 0, 2).reshape(P, -1)
    tri = np.where(p[None, :] <= p[:, None], 0.0, NEG)
    out["mask"] = np.concatenate([np.zeros((P, P)), tri], 1)
    end = np.arange(NCMP) * CS + CB - 1
    ok = end[None, None, :] <= (np.arange(TT)[None, :, None] * P + p[:, None, None])
    out["cmp_add"] = np.where(ok, 0.0, NEG).reshape(P, -1)
    out["cmp_01"] = np.where(ok, 1.0, 0.0).reshape(P, -1)
    ret = f(1.0) / np.power(f(10000.0), np.linspace(0.0, 1.0, RF, dtype=f))
    nsa = np.power(f(500000.0), -np.arange(0, ROT, 2, dtype=f) / f(ROT))
    out["freq"] = np.tile(np.concatenate([ret, nsa])[None], (P, 1))
    out["before"] = (p[:, None] < p[None, :])
    out["ones"] = np.ones((P, P))
    out["count"] = np.tile(np.arange(1, T + CAP + 1)[None], (P, 1))
    return np.concatenate([out[k].reshape(P, n).astype(f) for k, n in CONSTS.items()], 1)


class Counts:

    def __init__(self, engine):
        self.engine = engine
        self.at = {}

    def done(self, ins, sem):
        ins.then_inc(sem, 1)
        self.at[sem.name] = self.at.get(sem.name, 0) + 1
        self.engine.wait_ge(sem, self.at[sem.name])


def build(nc, a, out):
    with ExitStack() as ctx:
        def sb(name, shape, dt=F32):
            return ctx.enter_context(nc.sbuf_tensor(name, shape, dt))

        def sem(name):
            return ctx.enter_context(nc.semaphore(name))

        consts = sb("consts", [P, sum(CONSTS.values())])
        c_at = dict(zip(CONSTS, np.cumsum([0] + list(CONSTS.values())).tolist()))

        def const(name):
            return consts[:, c_at[name]:c_at[name] + CONSTS[name]]

        ident = const("ident")
        decay = const("decay").rearrange("p (h c) -> p h c", h=RH)
        mask = const("mask")
        cmp_add = const("cmp_add").rearrange("p (t n) -> p t n", t=TT)
        cmp_01 = const("cmp_01").rearrange("p (t n) -> p t n", t=TT)
        arena = sb("arena", [P, ARENA])
        ring = arena[:, 0:RING * SLOT].rearrange("p (s n) -> p s n", s=RING)
        z = arena[:, Z0:Z0 + TT * D_IN].rearrange("p (t n) -> p t n", t=TT)
        x = sb("x", [P, TT, D])
        xT = sb("xT", [P, KD, T])
        yT = sb("yT", [P, KD, T])
        norm = sb("norm", [P, 4, D])
        qkT = sb("qkT", [P, RH, 2, T])
        nq_buf = sb("nq_buf", [P, TT * NH * P])
        nqT = nq_buf[0:DH, :].rearrange("p (t h q) -> p t h q", t=TT, h=NH)
        nk_buf = sb("nk_buf", [P, 2, 2 * NG * T])
        nkT, cT = [nk_buf[0:DH, i, :].rearrange("p (v g t) -> p v g t", v=2, g=NG) for i in range(2)]
        shared_buf = sb("shared_buf", [P, max(CB * NG * NCMP, KC * (TAPS - 1 + T))])
        blocks_kv = shared_buf[:, 0:CB * NG * NCMP].rearrange("p (v c g n) -> p v c g n", v=2, c=CB // 2, g=NG)
        u_pad = shared_buf[:, 0:KC * (TAPS - 1 + T)].rearrange("p (k t) -> p k t", k=KC)
        E = sb("E", [P, 2, 4 * T])
        conv_acc = E[:, 0, :].rearrange("p (k t) -> p k t", k=KC)
        PT = sb("PT", [P, 4 * T])
        ret_p = PT[:, 0:2 * 3 * P].rearrange("p (b c) -> p b c", b=2)
        chan = sb("chan", [P, KC, CHAN_ROWS])
        chan_raw = E[0:CHAN_ROWS, 1, 0:CH]
        pe_raw = E[0:CB, 1, CH:CH + 2 * DH].rearrange("p (v d) -> p v d", v=2)
        peT = sb("peT", [DH, 2, CB])
        w2_kv = sb("w2_kv", [P, 2, 2, DH])
        hidT = sb("hidT", [P, 2, 2, NG * NCMP])
        hid = PT[:, 0:CHID]
        k_cmp = sb("k_cmp", [NG * NCMP, DH])
        k_cmpT = sb("k_cmpT", [DH, NG * NCMP])
        v_cmp = sb("v_cmp", [NCMP, NG, DH])
        pcT = yT[0:NCMP, :, :].rearrange("p k t -> p (k t)").rearrange("p (t h q) -> p t h q", t=TT, h=NH)
        Ec = sb("Ec", [P, TT, NH, NCMP])
        pos_i = sb("pos_i", [P, TT + 1], I32)
        pos = sb("pos", [P, TT + 1])
        cos = sb("cos", [P, TT + 1, FR])
        sin = sb("sin", [P, TT + 1, FR])
        group = sb("group", [P, TT, NEG_ + 8 - TOPG])
        turn_n = sb("turn_n", [P, TT + 1, FR])
        stats = sb("stats", [P, 2 * RH * TT, 6])
        mv = sb("mv", [P, 2 * RH, 2])
        rstd = sb("rstd", [P, 2 * RH])
        negmax = sb("negmax", [P, TT * NH])
        den = sb("den", [P, 2 * TT * NG, HPG])
        coef = sb("coef", [P, TT * NH])
        router_w = sb("router_w", [P, KD, NE])
        router_b = sb("router_b", [P, NE])
        score = sb("score", [P, TT, NE])
        biased = sb("biased", [P, TT, NE])
        best = sb("best", [P, TT, NEG_, 8])
        group_out = sb("group_out", [P, TT, NEG_ + 8 - TOPG])
        top = sb("top", [P, 8])
        marked = sb("marked", [P, TT, NE])
        total = sb("total", [P, TT])
        gates = sb("gates", [P, TT, E_ALL])
        silu_a = PT[:, 0:TT * FE].rearrange("p (t f) -> p t f", t=TT)
        product = yT[:, 0:2, :].rearrange("p k t -> p (k t)")
        hidden = qkT[:, 0, :, :]
        hiddenT = qkT[:, 1, :, :]

        ps = ctx.enter_context(nc.psum_tensor("ps", [P, 8, BANK], F32))

        def banks(b, n):
            return ps[:, b:b + n, :].rearrange("p b n -> p (b n)")

        pick = E[:, 1, 0:512].rearrange("p (b t a s) -> p b t a s", b=2, t=TT, a=2)
        pickT = sb("pickT", [P, 4, T], F32R)
        slot_gate = E[:, 1, 512:516]
        xg = yT[:, :, :].rearrange("p k t -> p (k t)").rearrange("p (b k s) -> p b k s", b=2, k=KD)
        hT = PT[:, 0:512].rearrange("p (b j s) -> p b j s", b=2, j=2)
        silu_pair, h_pair = [PT[:, 512 + i * FE:512 + (i + 1) * FE] for i in range(2)]
        y_slots = sb("y_slots", [P, 2, BANK], F32R)
        passed = nk_buf[0:1, :, :].rearrange("p a b -> p (a b)").rearrange("p (n e) -> p n e", n=MAX_MORE)
        counts = nq_buf[0:1, D:D + NE]
        more_rows = nq_buf[0:1, D + 512:D + 512 + 4 * 2 * NE].rearrange("p (r e) -> p r e", r=4)
        place = sb("place", [P, TT, NE])
        listed = turn_n[0:1, :, :].rearrange("p i f -> p (i f)").bitcast(I32)[:, 0:1 + 2 * MAX_MORE]

        boot = sem("boot")
        boot_dma = sem("boot_dma")
        boot_step = sem("boot_step")
        engine_at_end = sem("engine_at_end")
        all_at_end = sem("all_at_end")
        layer_open = sem("layer_open")
        layer_entered = sem("layer_entered")
        wait_passed = sem("wait_passed")
        stored = sem("stored")
        layer_sems = []

        def lsem(name):
            layer_sems.append(sem(name))
            return layer_sems[-1]

        ring_loaded = [lsem(f"ring_loaded{s}") for s in range(RING)]
        item_done = lsem("item_done")
        chan_loaded, pe_loaded, w2_loaded = lsem("chan_loaded"), lsem("pe_loaded"), lsem("w2_loaded")
        norm_loaded, router_loaded = lsem("norm_loaded"), lsem("router_loaded")
        dve_step, act_step = lsem("dve_step"), lsem("act_step")
        x_turned = lsem("x_turned")
        xT_act, xT_dve = lsem("xT_act"), lsem("xT_dve")
        z_written = lsem("z_written")
        angles_ready, sin_ready = lsem("angles_ready"), lsem("sin_ready")
        conv_gate = lsem("conv_gate")
        u_ready, u_turned, uT_ready = lsem("u_ready"), lsem("u_turned"), lsem("uT_ready")
        params_turned, params_ready = lsem("params_turned"), lsem("params_ready")
        pad_zeroed = lsem("pad_zeroed")
        conv_tap = lsem("conv_tap")
        conv_back = lsem("conv_back")
        var_ready, std_ready = lsem("var_ready"), lsem("std_ready")
        conv_normed, conv_turned, conv_silu = lsem("conv_normed"), lsem("conv_turned"), lsem("conv_silu")
        gates_ready, ret_gate_ready = lsem("gates_ready"), lsem("ret_gate_ready")
        y_taken = lsem("y_taken")
        ret_roped, nsa_roped = lsem("ret_roped"), lsem("nsa_roped")
        qk_turned, qk_ready = lsem("qk_turned"), lsem("qk_ready")
        ret_scores, ret_masked, ret_o, ret_o_copied = \
            lsem("ret_scores"), lsem("ret_masked"), lsem("ret_o"), lsem("ret_o_copied")
        ret_gated, ret_turned, yT_act, yT_dve = \
            lsem("ret_gated"), lsem("ret_turned"), lsem("yT_act"), lsem("yT_dve")
        nq_turned, nq_ready, nk_turned, nk_act, nk_dve = \
            lsem("nq_turned"), lsem("nq_ready"), lsem("nk_turned"), lsem("nk_act"), lsem("nk_dve")
        blocks_ready, hid_done, hid_ready, hid_turned = \
            [lsem(n) for n in ("blocks_ready", "hid_done", "hid_ready", "hid_turned")]
        kv_cmp_done, kv_cmp_ready, k_cmp_turned, k_cmp_ready = \
            lsem("kv_cmp_done"), lsem("kv_cmp_ready"), lsem("k_cmp_turned"), lsem("k_cmp_ready")
        cmp_scores, cmp_shifted, cmp_exp, cmp_p, cmp_turned, cmp_pT, cmp_o = \
            [lsem(f"cmp_{n}") for n in ("scores", "shifted", "exp", "p", "turned", "pT", "o")]
        at_scores, at_masked, at_max, at_exp, at_turned, at_pT, at_o, at_o_taken = \
            [lsem(f"at_{n}") for n in ("scores", "masked", "max", "exp", "turned", "pT", "o", "o_taken")]
        nsa_bank = lsem("nsa_bank")
        nsa_ready, nsa_turned, nsa_oT = lsem("nsa_ready"), lsem("nsa_turned"), lsem("nsa_oT")
        m_ready, m_turned, mT_act, mT_dve = lsem("m_ready"), lsem("m_turned"), lsem("mT_act"), lsem("mT_dve")
        x1_ready, x1_turned, x1T_act, x1T_dve = \
            lsem("x1_ready"), lsem("x1_turned"), lsem("x1T_act"), lsem("x1T_dve")
        out_done = lsem("out_done")
        router_done, score_ready = lsem("router_done"), lsem("score_ready")
        up_loaded = [lsem(f"up_loaded{s}") for s in range(E_SLOTS)]
        down_loaded = [lsem(f"down_loaded{s}") for s in range(E_SLOTS)]
        up_done = lsem("up_done")
        silu_done = lsem("silu_done")
        hidden_done = lsem("hidden_done")
        hidden_turned = lsem("hidden_turned")
        hiddenT_ready = lsem("hiddenT_ready")
        pair_used = lsem("pair_used")
        chosen_ready = lsem("chosen_ready")
        places_done = lsem("places_done")
        listed_ready = lsem("listed_ready")
        pick_ready = lsem("pick_ready")
        pick_turned, pickT_ready = lsem("pick_turned"), lsem("pickT_ready")
        gathered, xg_ready = lsem("gathered"), lsem("xg_ready")
        pair_up, pair_silu, h_ready, h_turned, hT_ready = \
            [lsem(n) for n in ("pair_up", "pair_silu", "h_ready", "h_turned", "hT_ready")]
        y0_done = lsem("y0_done")
        y0_part, y1_part, y0_ready, y1_ready = [lsem(f"y{h}_{n}") for n in ("part", "ready") for h in range(2)]
        scattered = lsem("scattered")
        experts_done = lsem("experts_done")
        numbers = [s.num for s in layer_sems]
        assert numbers == list(range(numbers[0], numbers[-1] + 1))

        w_in = a["w_in"].rearrange("l (p k) n -> l p k n", k=KD)
        moe_w1 = a["moe_w1"].rearrange("l e (p k) f -> l e p k f", k=KD)
        moe_w3 = a["moe_w3"].rearrange("l e (p k) f -> l e p k f", k=KD)
        moe_w2 = a["moe_w2"].rearrange("l e (p j) n -> l e p j n", j=2)

        at = {name: n for n, name in enumerate(ITEMS)}

        def ring_slot(item):
            return ring[:, item % RING, :]

        w_up = [arena[:, s * 2 * KD * FE:(s + 1) * 2 * KD * FE].rearrange("p (w k f) -> p w k f", w=2, k=KD)
                for s in range(E_SLOTS)]
        w_down = [arena[:, (2 * E_SLOTS + s) * KD * FE:(2 * E_SLOTS + s + 1) * KD * FE]
                  .rearrange("p (j n) -> p j n", j=2) for s in range(E_SLOTS)]

        m_buf = z[:, :, 0:D]
        ret_out = z[:, :, Z_RQ:Z_RQ + RH * RDV]
        nsa_out = z[:, :, Z_NQ:Z_NQ + NH * DH]
        def up_loads(p, m, b):
            return 16 * p + 8 * (1 + b - slot_of(m, b)) + 32

        def down_loads(p, m, b):
            return 8 * p + 4 * (1 + b - slot_of(m, b)) + 16

        def slot_of(m, b):
            return (1 + 2 * m + b) % E_SLOTS

        def pipeline(eng, step):
            def peeled(p):
                step(p, p % 4, lambda d: 0 <= p + d < PAIRS)

            for p in range(2):
                peeled(p)
            with eng.Fori(0, (PAIRS - 4) // 4) as i:
                for j in range(4):
                    step(4 * i + (2 + j), (2 + j) % 4, lambda d: True)
            for p in range(PAIRS - 2, PAIRS + 1):
                peeled(p)

        def further_rounds(eng, step):
            wanted = eng.value_load(listed[0:1, 0:1], min_val=0, max_val=MAX_MORE)
            with eng.Fori(0, MAX_MORE // 8) as a:
                with eng.If(wanted > a * 8):
                    with eng.Fori(0, 2) as i:
                        for m in range(2):
                            with eng.If(wanted > a * 8 + i * 4 + 2 * m):
                                step(a * 4 + i * 2 + (PAIRS + m), m)

        def round_expert(eng, p, b):
            return eng.value_load(listed[0:1, bass.ds(2 * p + (1 + b - 2 * PAIRS), 1)], min_val=0, max_val=NE - 1)

        def round_start(eng, p, b):
            return eng.value_load(listed[0:1, bass.ds(2 * p + (1 + b - 2 * PAIRS + MAX_MORE), 1)], min_val=CAP, max_val=T)

        UNITS = [(br, tt, g) for br in range(2) for tt in range(TT) for g in range(NG)]

        def layer_end(eng, l):
            eng.sem_inc(engine_at_end, 1)
            eng.wait_ge(layer_open, l + 2)
            eng.sem_inc(layer_entered, 1)

        block = ctx.enter_context(nc.Block())

        @block.sync
        def _(sp):
            sp.dma_start(consts[:, :], a["consts"]).then_inc(boot, 16)
            sp.dma_start(x[:, :, :], a["x"].rearrange("b (t p) d -> p (b t) d", p=P)).then_inc(boot, 16)
            sp.wait_ge(layer_open, 1)
            with sp.Fori(0, L) as l:
                for n in range(2):
                    sp.dma_start(ring_slot(n).rearrange("p (k n) -> p k n", k=KD),
                                 w_in[l, :, :, n * BANK:(n + 1) * BANK]).then_inc(ring_loaded[n], 16)
                sp.dma_start(chan_raw[0:TAPS, :], a["conv_dw"][l]).then_inc(chan_loaded, 16)
                for i, n in enumerate(("conv_db", "conv_ln_g", "conv_ln_b")):
                    sp.dma_start(chan_raw[TAPS + i:TAPS + i + 1, :], a[n][bass.ds(l, 1), :]).then_inc(chan_loaded, 16)
                for i, v in enumerate("kv"):
                    sp.dma_start(pe_raw[:, i, :], a[f"nsa_pe_{v}"][l]).then_inc(pe_loaded, 16)
                    sp.dma_start(w2_kv[:, i, :, :], a[f"nsa_w2_{v}"].rearrange("l (h p) d -> l p h d", p=P)[l]) \
                        .then_inc(w2_loaded, 16)
                with sp.Fori(0, (FULL_BLOCKS - 2) // 2) as i:
                    for j in range(2):
                        sp.wait_ge(item_done, 2 * i + j + 1)
                        sp.sem_inc(wait_passed, 1)
                        sp.dma_start(ring_slot(j).rearrange("p (k n) -> p k n", k=KD),
                                     w_in[l, :, :, bass.ds(i * (2 * BANK) + (j + 2) * BANK, BANK)]) \
                            .then_inc(ring_loaded[j], 16)
                for i, n in enumerate(("ln1_g", "ln1_b", "ln2_g", "ln2_b")):
                    sp.dma_start(norm[:, i, :], a[n][bass.ds(l, 1), :].to_broadcast([P, D])).then_inc(norm_loaded, 16)
                sp.dma_start(router_w[:, :, :], a["router_w"].rearrange("l (p k) e -> l p k e", k=KD)[l]) \
                    .then_inc(router_loaded, 16)
                sp.dma_start(router_b[:, :], a["router_b"][bass.ds(l, 1), :].to_broadcast([P, NE])) \
                    .then_inc(router_loaded, 16)
                sources = {
                    "in": (w_in[l, :, :, FULL_BLOCKS * BANK:D_IN], LAST_COLS),
                    "conv_pw": (a["conv_w_pw"].rearrange("l (p k) n -> l p k n", k=KC)[l], D),
                    "nsa_o": (a["nsa_w_o"].rearrange("l (p k) n -> l p k n", k=KC)[l], D),
                }
                for h in range(2):
                    cols = slice(h * BANK, (h + 1) * BANK)
                    sources[f"ret_o{h}"] = (a["ret_w_o"].rearrange("l (p k) n -> l p k n", k=KD)[l, :, :, cols], BANK)
                    sources[f"out{h}"] = (a["w_out"].rearrange("l (p k) n -> l p k n", k=KD)[l, :, :, cols], BANK)
                for v in "kv":
                    sources[f"w1_{v}"] = (a[f"nsa_w1_{v}"].rearrange("l (k p) h -> l p k h", p=P)[l], CHID)
                for n in range(FULL_BLOCKS, len(ITEMS)):
                    src, cols = sources[ITEMS[n]]
                    parts, k = src.shape[0], src.shape[1]
                    sp.wait_ge(item_done, n - RING + 1)
                    sp.dma_start(ring_slot(n)[0:parts, 0:k * cols].rearrange("p (k n) -> p k n", k=k), src) \
                        .then_inc(ring_loaded[n % RING], 16)

                def load_up(v, s, w1=None, w3=None):
                    for i, w in enumerate((w1, w3) if w1 is not None else (moe_w1[l, v - 1], moe_w3[l, v - 1])):
                        sp.dma_start(w_up[s][:, i, :, :], w).then_inc(up_loaded[s], 16)

                def load_down(v, s, w2=None):
                    sp.dma_start(w_down[s], w2 if w2 is not None else moe_w2[l, v - 1]).then_inc(down_loaded[s], 16)

                def load_ahead(p, m):
                    sp.wait_ge(pair_up, p + 1)
                    sp.sem_inc(wait_passed, 1)
                    for b in range(2):
                        load_up(2 * p + (5 + b), (2 * m + 5 + b) % E_SLOTS)
                    sp.wait_ge(pair_used, p + 1)
                    sp.sem_inc(wait_passed, 1)
                    for b in range(2):
                        load_down(2 * p + (3 + b), (2 * m + 3 + b) % E_SLOTS)

                sp.wait_ge(out_done, 2 * TT)
                load_up(0, 0, a["shared_w1"].rearrange("l (p k) f -> l p k f", k=KD)[l],
                        a["shared_w3"].rearrange("l (p k) f -> l p k f", k=KD)[l])
                load_down(0, 0, a["shared_w2"].rearrange("l (p j) n -> l p j n", j=2)[l])
                load_up(1, 1)
                load_up(2, 2)
                load_up(3, 3)
                load_down(1, 1)
                load_down(2, 2)
                sp.wait_ge(up_done, TT)
                load_up(4, 0)
                with sp.Fori(0, (PAIRS - 2) // 2) as i:
                    for m in range(2):
                        load_ahead(2 * i + m, m)
                sp.wait_ge(pair_used, PAIRS - 1)
                for v in (NE - 1, NE):
                    load_down(v, v % E_SLOTS)
                sp.wait_ge(listed_ready, 1)

                def load_more(p, m):
                    sp.wait_ge(pair_up, p - 1)
                    sp.sem_inc(wait_passed, 1)
                    experts = [round_expert(sp, p, b) for b in range(2)]
                    for b in range(2):
                        load_up(None, slot_of(m, b), moe_w1[l, experts[b]], moe_w3[l, experts[b]])
                    sp.wait_ge(pair_used, p)
                    sp.sem_inc(wait_passed, 1)
                    for b in range(2):
                        load_down(None, slot_of(m, b), moe_w2[l, experts[b]])

                further_rounds(sp, load_more)
                layer_end(sp, l)
            sp.dma_start(out.rearrange("b (t p) d -> p (b t) d", p=P), x[:, :, :]).then_inc(stored, 16)
            sp.wait_ge(stored, 16)

        @block.gpsimd
        def _(pool):
            pool.memset(pos_i[:, :], 0).then_inc(boot_step, 1)
            pool.wait_ge(boot_step, 1)
            pool.dma_start(pos_i[:, 0:TT], a["positions"].rearrange("b (t p) -> p (b t)", p=P),
                           allow_slow_non_contiguous=True).then_inc(boot_dma, 16)
            ends = a["positions"].rearrange("b (n s) -> (b n) s", s=CS)[1:1 + NCMP, CS - 1:CS]
            for g in range(NG):
                pool.dma_start(pos_i[g * NCMP:(g + 1) * NCMP, TT:TT + 1], ends, allow_slow_non_contiguous=True).then_inc(boot_dma, 16)
            pool.sem_inc(layer_open, 1)
            with pool.Fori(0, L) as l:
                pool.wait_ge(engine_at_end, 4 * l + 4)
                pool.sem_inc(all_at_end, 1)
                pool.sem_clear(range(numbers[0], numbers[-1] + 1))
                pool.sem_inc(layer_open, 1)

        @block.tensor
        def _(pe):
            def turn_model(src, banks_at, ready=None):
                for t in range(TT):
                    if ready:
                        ready(t)
                    for k in range(KD):
                        last = pe.transpose(ps[:, banks_at + k // 2, (k % 2 * TT + t) * P:(k % 2 * TT + t + 1) * P],
                                            src[:, t, k::KD], ident)
                return last

            def item_ready(n):
                pe.wait_ge(ring_loaded[n % RING], 16 * (n // RING + 1))

            def project(n, pair):
                cols = BANK if n != FULL_BLOCKS else LAST_COLS
                w = ring_slot(n)[:, 0:KD * cols].rearrange("p (k n) -> p k n", k=KD)
                for t in range(TT):
                    for k in range(KD):
                        last = pe.matmul(ps[:, 2 * pair + t, 0:cols], xT[:, k, t * P:(t + 1) * P], w[:, k, :],
                                         start=(k == 0), stop=(k == KD - 1))
                last.then_inc(item_done, 1)

            def full_output(act, k_chunks, half, n, tile_done=None):
                item_ready(n)
                w = ring_slot(n)[:, 0:k_chunks * BANK].rearrange("p (k n) -> p k n", k=k_chunks)
                for t in range(TT):
                    for k in range(k_chunks):
                        last = pe.matmul(ps[:, 2 * t + half, :], act[:, k, t * P:(t + 1) * P], w[:, k, :],
                                         start=(k == 0), stop=(k == k_chunks - 1))
                    if tile_done:
                        last.then_inc(tile_done, 1)
                return last

            def wide_output(act, n, bank_done=None):
                item_ready(n)
                w = ring_slot(n).rearrange("p (k n) -> p k n", k=KC)
                for t in range(TT):
                    for h in range(2):
                        for k in range(KC):
                            last = pe.matmul(ps[:, 2 * t + h, :], act[:, k, t * P:(t + 1) * P],
                                             w[:, k, h * BANK:(h + 1) * BANK], start=(k == 0), stop=(k == KC - 1))
                        if bank_done:
                            last.then_inc(bank_done, 1)
                return last

            pe.wait_ge(boot, 32)
            pe.wait_ge(layer_open, 1)
            with pe.Fori(0, L) as l:
                turn_model(x, 4).then_inc(x_turned, 1)
                pe.wait_ge(xT_act, 1)
                pe.wait_ge(xT_dve, 1)

                def start_block(n):
                    item_ready(n)
                    if n >= 2:
                        pe.wait_ge(z_written, n - 1)
                    project(n, n % 2)

                for n in range(3):
                    start_block(n)
                pe.wait_ge(chan_loaded, 64)
                for k in range(KC):
                    pe.transpose(ps[:, 6, k * CHAN_ROWS:(k + 1) * CHAN_ROWS], chan_raw[:, k::KC],
                                 ident[0:CHAN_ROWS, 0:CHAN_ROWS])
                pe.wait_ge(pe_loaded, 32)
                for v in range(2):
                    last = pe.transpose(ps[0:DH, 7, v * CB:(v + 1) * CB], pe_raw[:, v, :], ident[0:CB, 0:CB])
                last.then_inc(params_turned, 1)
                pe.wait_ge(u_ready, 1)
                for k in range(KC):
                    for t in range(TT):
                        last = pe.transpose(ps[:, 4 + k // 2, (k % 2 * TT + t) * P:(k % 2 * TT + t + 1) * P],
                                            z[:, t, Z_CA + k:Z_CA + CH:KC], ident)
                last.then_inc(u_turned, 1)
                start_block(3)
                with pe.Fori(0, (FULL_BLOCKS - 4) // 2) as i:
                    for j in range(2):
                        pe.wait_ge(ring_loaded[j], i * 16 + 48)
                        pe.wait_ge(z_written, 2 * i + j + 3)
                        project(j, j)
                start_block(FULL_BLOCKS)

                pe.wait_ge(conv_tap, TAPS * KC)
                pe.wait_ge(uT_ready, 1)
                for t in range(TT):
                    for k in range(KC):
                        last = pe.transpose(ps[:, 4 + t, k * P:(k + 1) * P], conv_acc[:, k, t * P:(t + 1) * P], ident)
                last.then_inc(conv_back, 1)
                pe.wait_ge(ret_roped, 1)
                pe.wait_ge(params_ready, 2)
                for h in range(RH):
                    if h >= 2:
                        pe.wait_ge(qk_ready, h - 1)
                    for i, off in enumerate((Z_RQ, Z_RK)):
                        for t in range(TT):
                            last = pe.transpose(ps[:, 6 + h % 2, (i * TT + t) * P:(i * TT + t + 1) * P],
                                                z[:, t, off + h * RDK:off + (h + 1) * RDK], ident)
                    last.then_inc(qk_turned, 1)
                pe.wait_ge(conv_normed, 1)
                for k in range(KC):
                    for t in range(TT):
                        last = pe.transpose(ps[:, 4 + k // 2, (k % 2 * TT + t) * P:(k % 2 * TT + t + 1) * P],
                                            z[:, t, Z_CA + k * P:Z_CA + (k + 1) * P], ident)
                last.then_inc(conv_turned, 1)
                pe.wait_ge(conv_silu, KC)
                def ret_score(h):
                    pe.wait_ge(qk_ready, h + 1)
                    if h >= 2:
                        pe.wait_ge(ret_masked, h - 1)
                    pe.matmul(ps[:, 4 + h % 2, 0:T], qkT[:, h, 1, 0:P], qkT[:, h, 0, :], start=True, stop=True)
                    pe.matmul(ps[:, 4 + h % 2, T:T + P], qkT[:, h, 1, P:T], qkT[:, h, 0, P:T],
                              start=True, stop=True).then_inc(ret_scores, 1)

                def ret_values(h):
                    pe.wait_ge(ret_masked, h + 1)
                    if h >= 2:
                        pe.wait_ge(ret_o_copied, h - 1)
                    o = ps[:, 6 + h % 2, :]
                    v = [z[:, t, Z_RV + h * RDV:Z_RV + (h + 1) * RDV] for t in range(TT)]
                    pe.matmul(o[:, 0:RDV], ret_p[:, h % 2, 0:P], v[0], start=True, stop=True)
                    pe.matmul(o[:, RDV:2 * RDV], ret_p[:, h % 2, P:2 * P], v[0], start=True, stop=False)
                    pe.matmul(o[:, RDV:2 * RDV], ret_p[:, h % 2, 2 * P:3 * P], v[1], start=False, stop=True) \
                        .then_inc(ret_o, 1)

                ret_score(0)
                pe.wait_ge(qk_ready, RH)
                for h in range(RH):
                    if h + 1 < RH:
                        ret_score(h + 1)
                    ret_values(h)
                pe.wait_ge(z_written, FULL_BLOCKS + 1)
                wide_output(yT, at["conv_pw"]).then_inc(item_done, 1)
                pe.wait_ge(ret_gated, 2)
                turn_model(ret_out, 4).then_inc(ret_turned, 1)
                pe.wait_ge(yT_act, 1)
                pe.wait_ge(yT_dve, 1)
                pe.wait_ge(y_taken, 1)
                full_output(yT, KD, 0, at["ret_o0"]).then_inc(item_done, 1)
                full_output(yT, KD, 1, at["ret_o1"]).then_inc(item_done, 1)

                pe.wait_ge(nsa_roped, 1)
                for t in range(TT):
                    for g in range(NG):
                        for h in range(HPG):
                            c = Z_NQ + (g * HPG + h) * DH
                            last = pe.transpose(ps[0:DH, 4 + t * NG + g, h * P:(h + 1) * P], z[:, t, c:c + DH], ident)
                last.then_inc(nq_turned, 1)
                pe.wait_ge(nq_ready, 4)
                for b, off in enumerate((Z_KS, Z_KW, Z_KC, Z_VC)):
                    for g in range(NG):
                        for t in range(TT):
                            last = pe.transpose(ps[0:DH, 4 + b, (g * TT + t) * P:(g * TT + t + 1) * P],
                                                z[:, t, off + g * DH:off + (g + 1) * DH], ident)
                last.then_inc(nk_turned, 1)
                def scores(u):
                    br, t, g = UNITS[u]
                    keys = (t + 1) * P
                    if u >= 2:
                        pe.wait_ge(at_masked, u - 1)
                    for h in range(HPG):
                        c = h * keys
                        last = pe.matmul(ps[:, 2 * (u % 2) + c // BANK, c % BANK:c % BANK + keys],
                                         nqT[:, t, g * HPG + h, :], nkT[:, br, g, 0:keys], start=True, stop=True)
                    last.then_inc(at_scores, 1)

                def turn_probs(u):
                    br, t, g = UNITS[u]
                    pe.wait_ge(at_exp, u + 1)
                    if u >= 1:
                        pe.wait_ge(at_pT, u)
                    e = E[:, u % 2, 0:HPG * (t + 1) * P].rearrange("p (h k) -> p h k", h=HPG)
                    for kc in range(t + 1):
                        for h in range(HPG):
                            last = pe.transpose(ps[:, 4 + kc, h * P:(h + 1) * P], e[:, h, kc * P:(kc + 1) * P], ident)
                    last.then_inc(at_turned, 1)

                def values(u):
                    br, t, g = UNITS[u]
                    pe.wait_ge(at_pT, u + 1)
                    if u >= 2:
                        pe.wait_ge(at_o_taken, u - 1)
                    off = (Z_VS, Z_VW)[br] + g * DH
                    for h in range(HPG):
                        for kc in range(t + 1):
                            last = pe.matmul(ps[:, 6 + u % 2, h * DH:(h + 1) * DH],
                                             PT[:, (kc * HPG + h) * P:(kc * HPG + h + 1) * P],
                                             z[:, kc, off:off + DH], start=(kc == 0), stop=(kc == t))
                    last.then_inc(at_o, 1)

                pe.wait_ge(nk_act, 2)
                pe.wait_ge(y_taken, 2)
                scores(0)
                scores(1)
                pe.wait_ge(nk_dve, 2)
                for u in range(len(UNITS)):
                    turn_probs(u)
                    if u + 2 < len(UNITS):
                        scores(u + 2)
                    values(u)
                pe.wait_ge(blocks_ready, 16)
                pe.wait_ge(at_o_taken, len(UNITS))
                w = [ring_slot(at[f"w1_{v}"]).rearrange("p (c h) -> p c h", c=CB // 2) for v in "kv"]
                for v in "kv":
                    item_ready(at[f"w1_{v}"])
                for c in range(CB // 2):
                    for v in range(2):
                        last = pe.matmul(ps[v * 64:v * 64 + NG * NCMP, 6, 0:CHID], blocks_kv[:, v, c, :, :], w[v][:, c, :],
                                         start=(c == 0), stop=(c == CB // 2 - 1))
                last.then_inc(hid_done, 1)
                pe.wait_ge(hid_done, 1)
                pe.sem_inc(item_done, 2)
                pe.wait_ge(hid_ready, 2)
                for v in range(2):
                    rows = slice(v * 64, v * 64 + NG * NCMP)
                    for half in range(2):
                        last = pe.transpose(ps[:, 6 + v, half * 32:half * 32 + NG * NCMP],
                                            hid[rows, half * P:(half + 1) * P], ident[rows, rows])
                last.then_inc(hid_turned, 1)
                pe.wait_ge(hid_ready, 4)
                pe.wait_ge(w2_loaded, 32)
                for half in range(2):
                    pe.matmul(ps[0:NG * NCMP, 4, 0:DH], hidT[:, 0, half, :], w2_kv[:, 0, half, :],
                              start=(half == 0), stop=(half == 1))
                for g in range(NG):
                    for half in range(2):
                        last = pe.matmul(ps[0:NCMP, 5, g * DH:(g + 1) * DH],
                                         hidT[:, 1, half, g * NCMP:(g + 1) * NCMP], w2_kv[:, 1, half, :],
                                         start=(half == 0), stop=(half == 1))
                last.then_inc(kv_cmp_done, 1)
                pe.wait_ge(kv_cmp_ready, 1)
                pe.transpose(ps[0:DH, 6, 0:NG * NCMP], k_cmp[:, :], ident[0:NG * NCMP, 0:NG * NCMP]) \
                    .then_inc(k_cmp_turned, 1)
                pe.wait_ge(k_cmp_ready, 1)
                for t in range(TT):
                    for h in range(NH):
                        g = h // HPG
                        last = pe.matmul(ps[:, 4, (t * NH + h) * NCMP:(t * NH + h + 1) * NCMP], nqT[:, t, h, :],
                                         k_cmpT[:, g * NCMP:(g + 1) * NCMP], start=True, stop=True)
                last.then_inc(cmp_scores, 1)
                pe.wait_ge(cmp_p, 1)
                pe.wait_ge(at_masked, len(UNITS))
                for t in range(TT):
                    for h in range(NH):
                        i = t * NH + h
                        last = pe.transpose(ps[0:NCMP, i // 4, (i % 4) * P:(i % 4 + 1) * P], Ec[:, t, h, :], ident)
                last.then_inc(cmp_turned, 1)
                pe.wait_ge(cmp_pT, 2)
                for t in range(TT):
                    for h in range(NH):
                        last = pe.matmul(ps[:, 6 + t, h * DH:(h + 1) * DH], pcT[:, t, h, :], v_cmp[:, h // HPG, :],
                                         start=True, stop=True)
                last.then_inc(cmp_o, 1)

                pe.wait_ge(nsa_ready, 1)
                for k in range(KC):
                    for t in range(TT):
                        last = pe.transpose(ps[:, 4 + k // 2, (k % 2 * TT + t) * P:(k % 2 * TT + t + 1) * P],
                                            z[:, t, Z_NQ + k:Z_NQ + NH * DH:KC], ident)
                last.then_inc(nsa_turned, 1)
                pe.wait_ge(nsa_oT, 1)
                wide_output(yT, at["nsa_o"], nsa_bank)
                pe.wait_ge(nsa_bank, 2 * TT)
                pe.sem_inc(item_done, 1)

                pe.wait_ge(m_ready, 1)
                turn_model(m_buf, 4).then_inc(m_turned, 1)
                pe.wait_ge(mT_act, 1)
                pe.wait_ge(mT_dve, 1)
                for h in range(2):
                    full_output(xT, KD, h, at[f"out{h}"], out_done)

                turn_model(x, 4, lambda t: pe.wait_ge(x1_ready, t + 1)).then_inc(x1_turned, 1)
                pe.wait_ge(x1T_act, 1)
                pe.wait_ge(x1T_dve, 1)
                pe.wait_ge(router_loaded, 32)
                for t in range(TT):
                    for k in range(KD):
                        last = pe.matmul(ps[:, 7, t * NE:(t + 1) * NE], xT[:, k, t * P:(t + 1) * P], router_w[:, k, :],
                                         start=(k == 0), stop=(k == KD - 1))
                last.then_inc(router_done, 1)

                def up(s, t):
                    w13 = w_up[s].rearrange("p w k f -> p k w f")
                    for k in range(KD):
                        last = pe.matmul(ps[:, 4 + t, :], xT[:, k, t * P:(t + 1) * P], w13[:, k, :, :],
                                         start=(k == 0), stop=(k == KD - 1))
                    last.then_inc(up_done, 1)

                def turn_hidden():
                    for j in range(2):
                        for t in range(TT):
                            last = pe.transpose(ps[:, 6, (j * TT + t) * P:(j * TT + t + 1) * P],
                                                hidden[:, t, j::2], ident)
                    last.then_inc(hidden_turned, 1)

                pe.wait_ge(up_loaded[0], 32)
                for t in range(TT):
                    up(0, t)
                pe.wait_ge(chosen_ready, 1)
                before, ones = const("before"), const("ones")
                pe.matmul(ps[:, 7, 2 * NE:3 * NE], before, marked[:, 0, :], start=True, stop=True)
                pe.matmul(ps[:, 7, 3 * NE:4 * NE], ones, marked[:, 0, :], start=True, stop=False)
                pe.matmul(ps[:, 7, 3 * NE:4 * NE], before, marked[:, 1, :], start=False, stop=True)
                pe.matmul(ps[:, 7, 4 * NE:5 * NE], ones, marked[:, 0, :], start=True, stop=False)
                pe.matmul(ps[:, 7, 4 * NE:5 * NE], ones, marked[:, 1, :], start=False, stop=True) \
                    .then_inc(places_done, 1)
                pe.wait_ge(hidden_done, 2)
                turn_hidden()
                pe.wait_ge(hiddenT_ready, 1)
                pe.wait_ge(down_loaded[0], 16)
                w2 = w_down[0]
                for t in range(TT):
                    for h in range(2):
                        for j in range(2):
                            last = pe.matmul(ps[:, 2 * t + h, :], hiddenT[:, j, t * P:(t + 1) * P],
                                             w2[:, j, h * BANK:(h + 1) * BANK], start=(j == 0), stop=True,
                                             skip_group_check=True)
                last.then_inc(pair_used, 1)

                def turn_picks(q, m, experts=None):
                    pe.wait_ge(pick_ready, q + 1)
                    for t in range(TT):
                        pe.transpose(ps[:, 4, t * P:(t + 1) * P],
                                     pick[:, m % 2, t, :, :].rearrange("p a s -> p (a s)"), ident)
                    for t in range(TT):
                        if experts is None:
                            last = pe.matmul(ps[:, 4, T:T + 2], pick[:, m % 2, t, :, :],
                                             gates[:, t, bass.ds(2 * q + 1, 2)], start=(t == 0), stop=(t == TT - 1))
                    for b in range(2 if experts else 0):
                        for t in range(TT):
                            last = pe.matmul(ps[:, 4, T + b:T + b + 1], pick[:, m % 2, t, :, :],
                                             gates[:, t, bass.ds(experts[b] + 1, 1)], start=(t == 0), stop=(t == TT - 1))
                    last.then_inc(pick_turned, 1)

                def gather(q, m):
                    pe.wait_ge(pickT_ready, q + 1)
                    for k in range(KD):
                        for t in range(TT):
                            last = pe.matmul(ps[:, 4 + k // 4, (k % 4) * P:(k % 4 + 1) * P], x[:, t, k::KD],
                                             pick[:, m % 2, t, :, :], start=(t == 0), stop=(t == TT - 1))
                    last.then_inc(gathered, 1)

                def pair_up_products(m):
                    for k in range(KD):
                        for b in range(2):
                            w13 = w_up[slot_of(m, b)].rearrange("p w k f -> p k w f")
                            last = pe.matmul(ps[b * CAP:(b + 1) * CAP, 6, :], xg[:, m % 2, k, b * CAP:(b + 1) * CAP],
                                             w13[:, k, :, :], start=(k == 0), stop=(k == KD - 1))
                    last.then_inc(pair_up, 1)

                def turn_pair_hidden():
                    for j in range(2):
                        last = pe.transpose(ps[:, 6, j * P:(j + 1) * P], h_pair[:, j::2], ident)
                    last.then_inc(h_turned, 1)

                def pair_down(m, h):
                    for j in range(2):
                        for b in range(2):
                            last = pe.matmul(ps[b * CAP:(b + 1) * CAP, 7, :], hT[:, m % 2, j, b * CAP:(b + 1) * CAP],
                                             w_down[slot_of(m, b)][:, j, h * BANK:(h + 1) * BANK],
                                             start=(j == 0), stop=(j == 1))
                    return last

                def scatter(m, h):
                    for t in range(TT):
                        for part in range(2):
                            last = pe.matmul(ps[:, 2 * t + h, :], pickT[:, m, t * P:(t + 1) * P], y_slots[:, part, :],
                                             start=False, stop=True, skip_group_check=True)
                    return last

                def pair_step(p, m, has):
                    if has(1):
                        if has(0):
                            pe.wait_ge(xg_ready, p + 1)
                        turn_picks(p + 1, (m + 1) % 4)
                    if has(-1):
                        pe.wait_ge(hT_ready, p)
                        for b in range(2):
                            pe.wait_ge(down_loaded[slot_of(m - 1, b)], down_loads(p - 1, m - 1, b))
                        pair_down((m - 1) % 4, 0).then_inc(y0_done, 1)
                    if has(0):
                        pe.wait_ge(xg_ready, p + 1)
                        for b in range(2):
                            pe.wait_ge(up_loaded[slot_of(m, b)], up_loads(p, m, b))
                        pair_up_products(m)
                    if has(-1):
                        pe.wait_ge(y0_ready, p)
                        scatter((m - 1) % 4, 0)
                        pair_down((m - 1) % 4, 1).then_inc(pair_used, 1)
                    if has(1):
                        gather(p + 1, (m + 1) % 4)
                    if has(0):
                        pe.wait_ge(h_ready, p + 1)
                        turn_pair_hidden()
                    if has(-1):
                        pe.wait_ge(y1_ready, p)
                        last = scatter((m - 1) % 4, 1)
                        if not has(0):
                            last.then_inc(scattered, 1)

                turn_picks(0, 0)
                gather(0, 0)
                pipeline(pe, pair_step)

                def pair_round(p, m):
                    turn_picks(p, m, [round_expert(pe, p, b) for b in range(2)])
                    gather(p, m)
                    pe.wait_ge(xg_ready, p + 1)
                    for b in range(2):
                        pe.wait_ge(up_loaded[slot_of(m, b)], up_loads(p, m, b))
                    pair_up_products(m)
                    pe.wait_ge(h_ready, p + 1)
                    turn_pair_hidden()
                    pe.wait_ge(hT_ready, p + 1)
                    for b in range(2):
                        pe.wait_ge(down_loaded[slot_of(m, b)], down_loads(p, m, b))
                    pair_down(m, 0).then_inc(y0_done, 1)
                    pe.wait_ge(y0_ready, p + 1)
                    scatter(m, 0)
                    pair_down(m, 1).then_inc(pair_used, 1)
                    pe.wait_ge(y1_ready, p + 1)
                    scatter(m, 1).then_inc(scattered, 1)
                    pe.wait_ge(scattered, p + (2 - PAIRS))
                    pe.sem_inc(wait_passed, 1)

                pe.wait_ge(listed_ready, 1)
                further_rounds(pe, pair_round)
                pe.wait_ge(scattered, 1)
                pe.sem_inc(experts_done, 1)
                pe.wait_ge(experts_done, 1)
                layer_end(pe, l)

        @block.scalar
        def _(act):
            act.wait_ge(layer_open, 1)
            with act.Fori(0, L) as l:
                c = Counts(act)

                def copy(dst, src, signal=act_step):
                    c.done(act.activation(dst, src, ACT.Copy), signal)

                xT_flat = xT[:, :, :].rearrange("p k t -> p (k t)")
                yT_flat = yT[:, :, :].rearrange("p k t -> p (k t)")
                act.wait_ge(x_turned, 1)
                copy(xT_flat[:, 0:2 * BANK], banks(4, 2), xT_act)

                def z_block(n):
                    cols = BANK if n != FULL_BLOCKS else LAST_COLS
                    act.wait_ge(item_done, n + 1)
                    pair = 2 * (n % 2)
                    copy(z[:, :, n * BANK:n * BANK + cols], ps[:, pair:pair + 2, 0:cols], z_written)

                z_block(0)
                z_block(1)
                c.done(act.activation(z[:, :, Z_CB:Z_CB + CH], z[:, :, Z_CB:Z_CB + CH], ACT.Sigmoid), conv_gate)
                z_block(2)
                act.wait_ge(params_turned, 1)
                copy(chan[:, :, :].rearrange("p k r -> p (k r)"), ps[:, 6, 0:KC * CHAN_ROWS], params_ready)
                copy(peT[:, :, :].rearrange("p v c -> p (v c)"), ps[0:DH, 7, 0:2 * CB], params_ready)
                act.wait_ge(u_turned, 1)
                act.wait_ge(pad_zeroed, 1)
                for b in range(2):
                    dst = u_pad[:, 2 * b:2 * b + 2, TAPS - 1:TAPS - 1 + T]
                    copy(dst, ps[:, 4 + b, :].rearrange("p (k t) -> p k t", k=2), act_step if b == 0 else uT_ready)
                act.wait_ge(angles_ready, 1)
                c.done(act.activation(sin[:, :, :], turn_n[:, :, :], ACT.Sin), sin_ready)
                c.done(act.activation(cos[:, :, :], cos[:, :, :], ACT.Sin), sin_ready)
                z_block(3)
                with act.Fori(0, (FULL_BLOCKS - 4) // 2) as i:
                    for j in range(2):
                        act.wait_ge(item_done, 2 * i + j + 5)
                        act.activation(z[:, :, bass.ds(i * (2 * BANK) + (j + 4) * BANK, BANK)],
                                       ps[:, 2 * j:2 * j + 2, :], ACT.Copy).then_inc(z_written, 1)
                c.at[z_written.name] = FULL_BLOCKS
                act.wait_ge(z_written, FULL_BLOCKS)
                z_block(FULL_BLOCKS)
                def root(n, first=0):
                    act.wait_ge(var_ready, c.at.get(std_ready.name, 0) + 1)
                    c.done(act.activation(rstd[:, first:n], rstd[:, first:n], ACT.Sqrt), std_ready)

                for h in range(RH):
                    act.wait_ge(qk_turned, h + 1)
                    copy(qkT[:, h, :, :].rearrange("p i t -> p (i t)"), ps[:, 6 + h % 2, :], qk_ready)
                root(TT)
                act.wait_ge(conv_turned, 1)
                for k in range(KC):
                    c.done(act.activation(yT[:, k, :], ps[:, 4 + k // 2, (k % 2) * T:(k % 2 + 1) * T], ACT.Silu,
                                          bias=chan[:, k, TAPS + 2:TAPS + 3], scale=chan[:, k, TAPS + 1:TAPS + 2]),
                           conv_silu)
                c.done(act.activation(z[:, :, Z_RG:Z_RG + RH * RDV], z[:, :, Z_RG:Z_RG + RH * RDV], ACT.Silu),
                       ret_gate_ready)
                for h in range(RH):
                    act.wait_ge(ret_o, h + 1)
                    copy(ret_out[:, :, h * RDV:(h + 1) * RDV],
                         ps[:, 6 + h % 2, :].rearrange("p (t v) -> p t v", t=TT), ret_o_copied)
                    if h % 2 and h < RH - 1:
                        root(RH // 2 * TT)
                root(RH * TT, RH // 2 * TT)
                c.done(act.activation(z[:, :, Z_NG:D_IN], z[:, :, Z_NG:D_IN], ACT.Sigmoid), gates_ready)
                act.wait_ge(ret_turned, 1)
                copy(yT_flat[:, 0:2 * BANK], banks(4, 2), yT_act)
                act.wait_ge(nq_turned, 1)
                for t in range(TT):
                    for g in range(NG):
                        c.done(act.activation(nqT[:, t, g * HPG:(g + 1) * HPG, :].rearrange("p h q -> p (h q)"),
                                              ps[0:DH, 4 + t * NG + g, :], ACT.Copy, scale=DH ** -0.5), nq_ready)
                act.wait_ge(nk_turned, 1)
                for b in range(2):
                    copy(nkT[:, b, :, :].rearrange("p g t -> p (g t)"), ps[0:DH, 4 + b, :], nk_act)
                def exps(u):
                    br, t, g = UNITS[u]
                    keys = (t + 1) * P
                    act.wait_ge(at_max, u + 1)
                    for h in range(HPG):
                        e = E[:, u % 2, h * keys:(h + 1) * keys]
                        c.done(act.activation(e, e, ACT.Exp, bias=negmax[:, (u % 2) * HPG + h:(u % 2) * HPG + h + 1],
                                              accum_out=den[:, u, h:h + 1]), at_exp if h == HPG - 1 else act_step)

                def probs(u):
                    n = HPG * (UNITS[u][1] + 1) * P
                    act.wait_ge(at_turned, u + 1)
                    if u >= 1:
                        act.wait_ge(at_o, u)
                    copy(PT[:, 0:n], banks(4, 2)[:, 0:n], at_pT)

                exps(0)
                exps(1)
                for u in range(len(UNITS)):
                    probs(u)
                    if u + 2 < len(UNITS):
                        exps(u + 2)
                act.wait_ge(hid_done, 1)
                for v in range(2):
                    rows = slice(v * 64, v * 64 + NG * NCMP)
                    c.done(act.activation(hid[rows, :], ps[rows, 6, 0:CHID], ACT.Silu), hid_ready)
                act.wait_ge(hid_turned, 1)
                for v in range(2):
                    copy(hidT[:, v, :, :], ps[:, 6 + v, 0:2 * 32].rearrange("p (h n) -> p h n", h=2)[:, :, 0:NG * NCMP],
                         hid_ready)
                act.wait_ge(k_cmp_turned, 1)
                copy(k_cmpT[:, :], ps[0:DH, 6, 0:NG * NCMP], k_cmp_ready)
                act.wait_ge(cmp_shifted, 1)
                c.done(act.activation(Ec[:, :, :, :], Ec[:, :, :, :], ACT.Exp), cmp_exp)
                act.wait_ge(cmp_turned, 1)
                for t in range(TT):
                    copy(pcT[:, t, :, :].rearrange("p h q -> p (h q)"), banks(2 * t, 2)[0:NCMP, :], cmp_pT)
                act.wait_ge(nsa_turned, 1)
                copy(yT_flat[:, 0:2 * BANK], banks(4, 2), nsa_oT)
                act.wait_ge(m_turned, 1)
                copy(xT_flat[:, 0:2 * BANK], banks(4, 2), mT_act)
                root(TT)
                act.wait_ge(x1_turned, 1)
                copy(xT_flat[:, 0:2 * BANK], banks(4, 2), x1T_act)
                act.wait_ge(router_done, 1)
                c.done(act.activation(score[:, :, :].rearrange("p t e -> p (t e)"), ps[:, 7, 0:TT * NE], ACT.Sigmoid),
                       score_ready)

                def silu(t):
                    act.activation(silu_a[:, t, :], ps[:, 4 + t, 0:FE], ACT.Silu).then_inc(silu_done, 1)

                def copy_hidden():
                    act.activation(hiddenT.rearrange("p j t -> p (j t)"), ps[:, 6, :], ACT.Copy) \
                        .then_inc(hiddenT_ready, 1)

                for t in range(TT):
                    act.wait_ge(up_done, t + 1)
                    silu(t)
                act.wait_ge(hidden_turned, 1)
                copy_hidden()

                def copy_gathered(q, m):
                    act.wait_ge(gathered, q + 1)
                    act.activation(xg[:, m % 2, :, :].rearrange("p k s -> p (k s)"), banks(4, 2), ACT.Copy) \
                        .then_inc(xg_ready, 1)

                def pair_silu_of(p):
                    act.wait_ge(pair_up, p + 1)
                    act.activation(silu_pair, ps[:, 6, 0:FE], ACT.Silu).then_inc(pair_silu, 1)

                def gated_output(m, h, signal):
                    g = (m - 1) % 4
                    act.activation(y_slots[:, 0, :], ps[:, 7, :], ACT.Copy, scale=slot_gate[:, g:g + 1]) \
                        .then_inc(signal, 1)

                def pair_step(p, m, has):
                    if has(-1):
                        act.wait_ge(y0_done, p)
                        gated_output(m, 0, y0_part)
                    if has(0):
                        pair_silu_of(p)
                    if has(-1):
                        act.wait_ge(pair_used, p + 1)
                        gated_output(m, 1, y1_part)
                    if has(1):
                        copy_gathered(p + 1, (m + 1) % 4)

                copy_gathered(0, 0)
                pipeline(act, pair_step)

                def pair_round(p, m):
                    copy_gathered(p, m)
                    pair_silu_of(p)
                    act.wait_ge(y0_done, p + 1)
                    gated_output(m + 1, 0, y0_part)
                    act.wait_ge(pair_used, p + 2)
                    gated_output(m + 1, 1, y1_part)

                act.wait_ge(listed_ready, 1)
                further_rounds(act, pair_round)
                root(TT)
                layer_end(act, l)

        @block.vector
        def _(dve):
            dve.wait_ge(layer_open, 1)
            with dve.Fori(0, L) as l:
                c = Counts(dve)

                def do(ins, signal=dve_step):
                    c.done(ins, signal)

                def tt(dst, in0, in1, op, signal=dve_step):
                    do(dve.tensor_tensor(dst, in0, in1, op), signal)

                def rope(x1, x2, co, si, tmp, signal=dve_step):
                    tt(tmp[0], x1, co, ALU.mult)
                    tt(tmp[1], x2, si, ALU.mult)
                    tt(tmp[2], x2, co, ALU.mult)
                    tt(tmp[3], x1, si, ALU.mult)
                    tt(x1, tmp[0], tmp[1], ALU.subtract)
                    tt(x2, tmp[2], tmp[3], ALU.add, signal)

                def mean_rstd(n, first=0):
                    do(dve.tensor_scalar(rstd[:, first:n], mv[:, first:n, 1], EPS, None, ALU.add), var_ready)
                    dve.wait_ge(std_ready, c.at[var_ready.name])
                    do(dve.reciprocal(rstd[:, first:n], rstd[:, first:n]))

                xT_flat = xT[:, :, :].rearrange("p k t -> p (k t)")
                yT_flat = yT[:, :, :].rearrange("p k t -> p (k t)")
                dve.wait_ge(x_turned, 1)
                do(dve.tensor_copy(xT_flat[:, 2 * BANK:], banks(6, 2)), xT_dve)
                do(dve.memset(u_pad[:, :, 0:TAPS - 1], 0.0), pad_zeroed)

                magic = 1.5 * 2.0 ** 23
                c1, c2 = 6.28125, 0.0019340515136718750
                c3 = float(2 * np.pi - c1 - c2)
                dve.wait_ge(boot_dma, 48)
                dve.wait_ge(boot, 32)
                do(dve.tensor_copy(pos[:, :], pos_i[:, :]))
                for i in range(TT + 1):
                    do(dve.tensor_scalar(sin[:, i, :], const("freq"), pos[:, i:i + 1], None, ALU.mult))
                do(dve.tensor_scalar(turn_n[:, :, :], sin[:, :, :], float(1 / (2 * np.pi)), magic, ALU.mult, ALU.add))
                do(dve.tensor_scalar(turn_n[:, :, :], turn_n[:, :, :], magic, None, ALU.subtract))
                for part in (c1, c2, c3):
                    do(dve.scalar_tensor_tensor(out=sin[:, :, :], in0=turn_n[:, :, :], scalar=-part,
                                                in1=sin[:, :, :], op0=ALU.mult, op1=ALU.add))
                lim = 3.1415925
                do(dve.tensor_scalar(turn_n[:, :, :], sin[:, :, :], lim, -lim, ALU.min, ALU.max))
                do(dve.tensor_scalar(cos[:, :, :], turn_n[:, :, :], -1.0, None, ALU.mult))
                do(dve.tensor_tensor(cos[:, :, :], cos[:, :, :], turn_n[:, :, :], ALU.min))
                do(dve.tensor_scalar(cos[:, :, :], cos[:, :, :], float(np.pi / 2), None, ALU.add), angles_ready)

                dve.wait_ge(conv_gate, 1)
                tt(z[:, :, Z_CA:Z_CA + CH], z[:, :, Z_CA:Z_CA + CH], z[:, :, Z_CB:Z_CB + CH], ALU.mult, u_ready)
                dve.wait_ge(params_ready, 2)
                dve.wait_ge(uT_ready, 1)
                for k in range(KC):
                    dve.tensor_scalar(conv_acc[:, k, :], u_pad[:, k, 0:T], chan[:, k, 0:1], chan[:, k, TAPS:TAPS + 1],
                                      ALU.mult, ALU.add).then_inc(conv_tap, 1)
                with dve.Fori(0, (TAPS - 1) // 2) as i:
                    for j in range(2):
                        for k in range(KC):
                            dve.wait_ge(conv_tap, i * (2 * KC) + (j * KC + k + 1))
                            dve.scalar_tensor_tensor(out=conv_acc[:, k, :], in0=u_pad[:, k, bass.ds(2 * i + (j + 1), T)],
                                                     scalar=chan[:, k, bass.ds(2 * i + (j + 1), 1)],
                                                     in1=conv_acc[:, k, :], op0=ALU.mult, op1=ALU.add) \
                                .then_inc(conv_tap, 1)
                dve.wait_ge(conv_tap, TAPS * KC)

                dve.wait_ge(z_written, Z_RV // BANK)
                dve.wait_ge(sin_ready, 2)
                halves = z[:, :, Z_RQ:Z_RV].rearrange("p t (h i f) -> p t h i f", i=2, f=RF)
                nh = 2 * RH
                tmp = [E[:, 1, 0:512], E[:, 1, 512:1024], PT[:, 0:512], PT[:, 512:1024]]
                tmp = [t_.rearrange("p (h f) -> p h f", h=nh) for t_ in tmp]
                for t in range(TT):
                    co, si = [w[:, t, 0:RF].unsqueeze(1).to_broadcast([P, nh, RF]) for w in (cos, sin)]
                    rope(halves[:, t, :, 0, :], halves[:, t, :, 1, :], co, si, tmp,
                         ret_roped if t == TT - 1 else dve_step)
                dve.wait_ge(z_written, Z_NG // BANK + 1)
                for t in range(TT):
                    for off, heads in ((Z_NQ, NH), (Z_KS, NG), (Z_KW, NG)):
                        v = z[:, t, off:off + heads * DH].rearrange("p (h f) -> p h f", h=heads)
                        co, si = [w[:, t, RF:FR].unsqueeze(1).to_broadcast([P, heads, NF]) for w in (cos, sin)]
                        small = [t_[:, 0:heads, 0:NF] for t_ in tmp]
                        rope(v[:, :, 0:NF], v[:, :, NF:ROT], co, si, small,
                             nsa_roped if (t, off) == (TT - 1, Z_KW) else dve_step)

                dve.wait_ge(conv_back, 1)
                for t in range(TT):
                    do(dve.bn_stats(stats[:, t, :], ps[:, 4 + t, :]))
                    do(dve.bn_aggr(mv[:, t, :], stats[:, t, :]))
                mean_rstd(TT)
                for t in range(TT):
                    do(dve.tensor_scalar(z[:, t, Z_CA:Z_CA + CH], ps[:, 4 + t, :], mv[:, t, 0:1], rstd[:, t:t + 1],
                                         ALU.subtract, ALU.mult), conv_normed if t == TT - 1 else dve_step)

                def merge(branch, signal, ready):
                    order = [(h, t) for h in range(2) for t in range(TT)]
                    for h, t in order if branch < 2 else sorted(order, key=lambda b: b[1]):
                        ready(h, t)
                        last = (h, t) == (1, TT - 1)
                        cols = slice(h * BANK, (h + 1) * BANK)
                        gate = z[:, t, Z_MG + branch * D + h * BANK:Z_MG + branch * D + (h + 1) * BANK]
                        product = m_buf[:, t, cols] if branch == 0 else E[:, t, cols]
                        tt(product, gate, ps[:, 2 * t + h, :], ALU.mult, y_taken if last else dve_step)
                        if branch:
                            tt(m_buf[:, t, cols], m_buf[:, t, cols], product, ALU.add, signal if last else dve_step)

                def decay_scores(h):
                    dve.wait_ge(ret_scores, h + 1)
                    if h >= 2:
                        dve.wait_ge(ret_o, h - 1)
                    tt(ret_p[:, h % 2, 0:T], ps[:, 4 + h % 2, 0:T], decay[:, h, :], ALU.mult)
                    tt(ret_p[:, h % 2, T:T + P], ps[:, 4 + h % 2, T:T + P], decay[:, h, 0:P], ALU.mult, ret_masked)

                def norm_heads(first, end, signal):
                    mean_rstd(end * TT, first * TT)
                    dve.wait_ge(ret_gate_ready, 1)
                    for h in range(first, end):
                        for t in range(TT):
                            i = h * TT + t
                            o = ret_out[:, t, h * RDV:(h + 1) * RDV]
                            do(dve.tensor_scalar(o, o, mv[:, i, 0:1], rstd[:, i:i + 1], ALU.subtract, ALU.mult))
                    o = ret_out[:, :, first * RDV:end * RDV]
                    tt(o, o, z[:, :, Z_RG + first * RDV:Z_RG + end * RDV], ALU.mult, signal)

                decay_scores(0)
                decay_scores(1)
                for h in range(RH):
                    if h + 2 < RH:
                        decay_scores(h + 2)
                    dve.wait_ge(ret_o_copied, h + 1)
                    for t in range(TT):
                        i = h * TT + t
                        do(dve.bn_stats(stats[:, i, :], ret_out[:, t, h * RDV:(h + 1) * RDV]))
                        do(dve.bn_aggr(mv[:, i, :], stats[:, i, :]))
                    if h % 2:
                        norm_heads(h - 1, h + 1, ret_gated)
                merge(0, None, lambda h, t: (dve.wait_ge(item_done, at["conv_pw"] + 1), dve.wait_ge(gates_ready, 1)))

                dve.wait_ge(ret_turned, 1)
                do(dve.tensor_copy(yT_flat[:, 2 * BANK:], banks(6, 2)), yT_dve)
                merge(1, dve_step, lambda h, t: dve.wait_ge(item_done, at[f"ret_o{h}"] + 1))

                dve.wait_ge(nk_turned, 1)
                for v in range(2):
                    do(dve.tensor_copy(cT[:, v, :, :].rearrange("p g t -> p (g t)"), ps[0:DH, 6 + v, :]), nk_dve)
                def blocks(v, g):
                    by_stride = cT[:, v, g, :].rearrange("p (m s) -> p s m", s=CS)
                    for c2 in range(CB // CS):
                        for odd in range(2):
                            rows, half = slice(odd * DH, (odd + 1) * DH), CS // 2
                            tt(blocks_kv[rows, v, c2 * half:(c2 + 1) * half, g, :],
                               by_stride[:, odd::2, c2:c2 + NCMP],
                               peT[:, v, c2 * CS + odd:(c2 + 1) * CS:2].unsqueeze(2).to_broadcast([DH, half, NCMP]),
                               ALU.add, blocks_ready)

                def mask_scores(u):
                    br, t, g = UNITS[u]
                    keys = (t + 1) * P
                    dve.wait_ge(at_scores, u + 1)
                    if u >= 2:
                        dve.wait_ge(at_turned, u - 1)
                    e = E[:, u % 2, 0:HPG * keys].rearrange("p (h k) -> p h k", h=HPG)
                    sc = banks(2 * (u % 2), 2)[:, 0:HPG * keys].rearrange("p (h k) -> p h k", h=HPG)
                    mk = mask[:, 2 * P - keys:2 * P].unsqueeze(1).to_broadcast([P, HPG, keys])
                    tt(e, sc, mk, ALU.add, at_masked)
                    do(dve.tensor_reduce(negmax[:, (u % 2) * HPG:(u % 2 + 1) * HPG], e, AX.X, ALU.max, negate=True),
                       at_max)

                def add_output(u):
                    br, t, g = UNITS[u]
                    dve.wait_ge(at_o, u + 1)
                    w = coef[:, 0:HPG]
                    do(dve.reciprocal(w, den[:, u, :]))
                    tt(w, w, gate3[:, t, g * HPG:(g + 1) * HPG, br + 1], ALU.mult)
                    o = nsa_out[:, t, g * HPG * DH:(g + 1) * HPG * DH]
                    dst = product[:, 0:HPG * DH] if br else o
                    tt(dst.rearrange("p (h d) -> p h d", h=HPG), ps[:, 6 + u % 2, 0:HPG * DH].rearrange("p (h d) -> p h d", h=HPG),
                       w.unsqueeze(2).to_broadcast([P, HPG, DH]), ALU.mult, at_o_taken)
                    if br:
                        tt(o, o, dst, ALU.add)

                gate3 = z[:, :, Z_NG:Z_NG + NH * 3].rearrange("p t (h b) -> p t h b", b=3)
                mask_scores(0)
                mask_scores(1)
                for u in range(len(UNITS)):
                    if u + 2 < len(UNITS):
                        mask_scores(u + 2)
                    if u < 2 * NG:
                        blocks(u // NG, u % NG)
                    add_output(u)

                dve.wait_ge(kv_cmp_done, 1)
                kn = NG * NCMP
                do(dve.tensor_copy(k_cmp[:, :], ps[0:kn, 4, 0:DH]))
                co, si = cos[0:kn, TT, RF:FR], sin[0:kn, TT, RF:FR]
                rope(k_cmp[:, 0:NF], k_cmp[:, NF:ROT], co, si, [E[0:kn, 0, i * NF:(i + 1) * NF] for i in range(4)])
                do(dve.tensor_copy(v_cmp[:, :, :].rearrange("p g d -> p (g d)"), ps[0:NCMP, 5, 0:NG * DH]), kv_cmp_ready)

                dve.wait_ge(cmp_scores, 1)
                s = ps[:, 4, 0:TT * NH * NCMP].rearrange("p (t h n) -> p t h n", t=TT, h=NH)
                bc = [P, NH, NCMP]
                for t in range(TT):
                    tt(Ec[:, t, :, :], s[:, t, :, :], cmp_add[:, t, :].unsqueeze(1).to_broadcast(bc), ALU.add)
                flat = Ec[:, :, :, :].rearrange("p t h n -> p (t h) n")
                do(dve.tensor_reduce(negmax[:, :], flat, AX.X, ALU.max, negate=True))
                tt(flat, flat, negmax[:, :].unsqueeze(2).to_broadcast([P, TT * NH, NCMP]), ALU.add, cmp_shifted)
                dve.wait_ge(cmp_exp, 1)
                do(dve.tensor_reduce(coef[:, :], flat, AX.X, ALU.add))
                for t in range(TT):
                    tt(Ec[:, t, :, :], Ec[:, t, :, :], cmp_01[:, t, :].unsqueeze(1).to_broadcast(bc), ALU.mult,
                       cmp_p if t == TT - 1 else dve_step)
                do(dve.reciprocal(coef[:, :], coef[:, :]))
                tt(coef[:, :].rearrange("p (t h) -> p t h", t=TT), coef[:, :].rearrange("p (t h) -> p t h", t=TT),
                   gate3[:, :, :, 0], ALU.mult)
                dve.wait_ge(cmp_o, 1)
                for t in range(TT):
                    tt(product.rearrange("p (h d) -> p h d", h=NH), ps[:, 6 + t, :].rearrange("p (h d) -> p h d", h=NH),
                       coef[:, t * NH:(t + 1) * NH].unsqueeze(2).to_broadcast([P, NH, DH]), ALU.mult)
                    tt(nsa_out[:, t, :], nsa_out[:, t, :], product, ALU.add, nsa_ready if t == TT - 1 else dve_step)
                merge(2, m_ready, lambda h, t: dve.wait_ge(nsa_bank, 2 * t + h + 1))
                dve.wait_ge(m_turned, 1)
                do(dve.tensor_copy(xT_flat[:, 2 * BANK:], banks(6, 2)), mT_dve)

                def residual_norm(which, signal, ready=None):
                    for h in range(2):
                        for t in range(TT):
                            if ready:
                                ready(h, t)
                            half = x[:, t, h * BANK:(h + 1) * BANK]
                            do(dve.scalar_tensor_tensor(out=half, in0=half, scalar=ALPHA, in1=ps[:, 2 * t + h, :],
                                                        op0=ALU.mult, op1=ALU.add))
                            do(dve.bn_stats(stats[:, 2 * t + h, :], half))
                    for t in range(TT):
                        do(dve.bn_aggr(mv[:, t, :], stats[:, 2 * t:2 * t + 2, :].rearrange("p a b -> p (a b)")))
                    mean_rstd(TT)
                    for t in range(TT):
                        do(dve.scalar_tensor_tensor(out=x[:, t, :], in0=x[:, t, :], scalar=mv[:, t, 0:1],
                                                    in1=norm[:, 2 * which, :], op0=ALU.subtract, op1=ALU.mult))
                        do(dve.scalar_tensor_tensor(out=x[:, t, :], in0=x[:, t, :], scalar=rstd[:, t:t + 1],
                                                    in1=norm[:, 2 * which + 1, :], op0=ALU.mult, op1=ALU.add), signal)

                dve.wait_ge(norm_loaded, 64)
                residual_norm(0, x1_ready, lambda h, t: dve.wait_ge(out_done, 2 * h + t + 1))
                dve.wait_ge(x1_turned, 1)
                do(dve.tensor_copy(xT_flat[:, 2 * BANK:], banks(6, 2)), x1T_dve)

                dve.wait_ge(score_ready, 1)
                dve.wait_ge(router_loaded, 32)
                tt(biased[:, :, :], score[:, :, :], router_b[:, :].unsqueeze(1).to_broadcast([P, TT, NE]), ALU.add)
                per = NE // NEG_
                for t in range(TT):
                    for g in range(NEG_):
                        do(dve.max(best[:, t, g, :], biased[:, t, g * per:(g + 1) * per]))
                do(dve.memset(group[:, :, :], -NEG))
                tt(group[:, :, 0:NEG_], best[:, :, :, 0], best[:, :, :, 1], ALU.add)
                for t in range(TT):
                    do(dve.max(top[:, :], group[:, t, :]))
                    do(dve.match_replace(group_out[:, t, :], top[:, :], group[:, t, :], NEG))
                kept = group_out[:, :, 0:NEG_]
                do(dve.tensor_scalar(kept, kept, NEG, NEG, ALU.not_equal, ALU.mult))
                for t in range(TT):
                    e3 = biased[:, t, :].rearrange("p (g e) -> p g e", g=NEG_)
                    tt(e3, e3, group_out[:, t, 0:NEG_].unsqueeze(2).to_broadcast([P, NEG_, per]), ALU.add)
                    do(dve.max(top[:, :], biased[:, t, :]))
                    do(dve.match_replace(marked[:, t, :], top[:, :], biased[:, t, :], 2 * NEG))
                do(dve.tensor_scalar(marked[:, :, :], marked[:, :, :], 2 * NEG, None, ALU.is_equal))
                tt(biased[:, :, :], marked[:, :, :], score[:, :, :], ALU.mult, chosen_ready)
                do(dve.tensor_reduce(total[:, :], biased[:, :, :], AX.X, ALU.add))
                do(dve.reciprocal(total[:, :], total[:, :]))
                do(dve.memset(gates[:, :, 0:1], 1.0))
                for t in range(TT):
                    do(dve.tensor_scalar(gates[:, t, 1:E_ALL], biased[:, t, :], total[:, t:t + 1], SCALE_ROUTED,
                                         ALU.mult, ALU.mult))

                for t in range(TT):
                    dve.wait_ge(silu_done, t + 1)
                    tt(hidden[:, t, :], ps[:, 4 + t, FE:2 * FE], silu_a[:, t, :], ALU.mult, hidden_done)

                dve.wait_ge(places_done, 1)
                do(dve.scalar_tensor_tensor(out=place[:, :, :],
                                            in0=ps[:, 7, 2 * NE:4 * NE].rearrange("p (t e) -> p t e", t=TT), scalar=1.0,
                                            in1=marked[:, :, :], op0=ALU.add, op1=ALU.mult))
                do(dve.tensor_copy(counts[:, :], ps[0:1, 7, 4 * NE:5 * NE]))

                def list_rounds():
                    wanted = more_rows[:, 0, NE:]
                    do(dve.memset(more_rows[:, :, :], 0.0))
                    for b in range(1, ROUNDS):
                        do(dve.scalar_tensor_tensor(out=wanted, in0=counts[:, :], scalar=float(b * CAP), in1=wanted,
                                                    op0=ALU.is_gt, op1=ALU.add))
                    src, shift = 0, 1
                    while shift < NE:
                        dst = 1 if src != 1 else 2
                        tt(more_rows[:, dst, NE:], more_rows[:, src, NE:], more_rows[:, src, NE - shift:2 * NE - shift],
                           ALU.add)
                        src, shift = dst, shift * 2
                    sums = more_rows[:, src, NE:]
                    shape = [1, MAX_MORE, NE]
                    nth = const("count")[0:1, 0:MAX_MORE]
                    tt(passed, sums.unsqueeze(1).to_broadcast(shape), nth.unsqueeze(2).to_broadcast(shape), ALU.is_lt)
                    experts, starts = [more_rows[:, 3, i * MAX_MORE:(i + 1) * MAX_MORE] for i in range(2)]
                    do(dve.tensor_reduce(experts, passed, AX.X, ALU.add))
                    tt(passed, passed, wanted.unsqueeze(1).to_broadcast(shape), ALU.mult)
                    do(dve.tensor_reduce(starts, passed, AX.X, ALU.add))
                    tt(starts, nth, starts, ALU.subtract)
                    do(dve.tensor_scalar(starts, starts, float(CAP), None, ALU.mult))
                    beyond = more_rows[:, 2, 0:MAX_MORE]
                    do(dve.tensor_scalar(beyond, experts, NE - 0.5, float(T), ALU.is_gt, ALU.mult))
                    tt(starts, starts, beyond, ALU.max)
                    do(dve.tensor_scalar(starts, starts, float(CAP), float(T), ALU.max, ALU.min))
                    do(dve.tensor_scalar(experts, experts, float(NE - 1), None, ALU.min))
                    do(dve.tensor_copy(listed[:, 0:1], sums[:, NE - 1:NE]))
                    do(dve.tensor_copy(listed[:, 1:], more_rows[:, 3, 0:2 * MAX_MORE]), listed_ready)

                slots = const("count")[:, 0:CAP]

                def make_picks(q, m):
                    shape = [P, TT, 2, CAP]
                    at_e = place[:, :, bass.ds(2 * q, 2)].unsqueeze(3).to_broadcast(shape)
                    dve.tensor_tensor(pick[:, m % 2, :, :, :], slots.unsqueeze(1).unsqueeze(1).to_broadcast(shape), at_e,
                                      ALU.is_equal).then_inc(pick_ready, 1)

                def copy_picks(q, m):
                    dve.wait_ge(pick_turned, q + 1)
                    for b in range(2):
                        rows = slice(b * CAP, (b + 1) * CAP)
                        dve.tensor_copy(slot_gate[rows, m:m + 1], ps[rows, 4, T + b:T + b + 1])
                    dve.tensor_copy(pickT[:, m, :], ps[:, 4, 0:T]).then_inc(pickT_ready, 1)

                def pair_hidden(p):
                    dve.wait_ge(pair_silu, p + 1)
                    dve.tensor_tensor(h_pair, ps[:, 6, FE:2 * FE], silu_pair, ALU.mult).then_inc(h_ready, 1)

                def copy_hidden(p, m):
                    dve.wait_ge(h_turned, p + 1)
                    dve.tensor_copy(hT[:, m % 2, :, :].rearrange("p j s -> p (j s)"), ps[:, 6, 0:2 * P]) \
                        .then_inc(hT_ready, 1)

                def output_rest(m, h, signal):
                    g = (m - 1) % 4
                    dve.scalar_tensor_tensor(out=y_slots[:, 1, :], in0=ps[:, 7, :], scalar=slot_gate[:, g:g + 1],
                                             in1=y_slots[:, 0, :].bitcast(F32), op0=ALU.mult, op1=ALU.subtract) \
                        .then_inc(signal, 1)

                def pair_step(p, m, has):
                    if has(1):
                        copy_picks(p + 1, (m + 1) % 4)
                    if has(-1):
                        dve.wait_ge(y0_part, p)
                        output_rest(m, 0, y0_ready)
                    if has(2):
                        if has(0):
                            dve.wait_ge(gathered, p + 1)
                        make_picks(p + 2, (m + 2) % 4)
                    if has(0):
                        pair_hidden(p)
                    if has(-1):
                        dve.wait_ge(y1_part, p)
                        output_rest(m, 1, y1_ready)
                    if has(0):
                        copy_hidden(p, m)
                    if isinstance(p, int) and p == 0:
                        list_rounds()

                make_picks(0, 0)
                make_picks(1, 1)
                copy_picks(0, 0)
                pipeline(dve, pair_step)

                def pair_round(p, m):
                    for b in range(2):
                        e, first = round_expert(dve, p, b), round_start(dve, p, b)
                        shape = [P, TT, CAP]
                        made = dve.tensor_tensor(pick[:, m, :, b, :],
                                                 const("count")[:, bass.ds(first, CAP)].unsqueeze(1).to_broadcast(shape),
                                                 place[:, :, bass.ds(e, 1)].to_broadcast(shape), ALU.is_equal)
                    made.then_inc(pick_ready, 1)
                    copy_picks(p, m)
                    pair_hidden(p)
                    copy_hidden(p, m)
                    dve.wait_ge(y0_part, p + 1)
                    output_rest(m + 1, 0, y0_ready)
                    dve.wait_ge(y1_part, p + 1)
                    output_rest(m + 1, 1, y1_ready)

                further_rounds(dve, pair_round)
                dve.wait_ge(experts_done, 1)
                residual_norm(1, dve_step)
                layer_end(dve, l)


_INS = ["x", "positions", "w_in", "conv_dw", "conv_db", "conv_ln_g", "conv_ln_b", "conv_w_pw", "ret_w_o",
        "nsa_pe_k", "nsa_w1_k", "nsa_w2_k", "nsa_pe_v", "nsa_w1_v", "nsa_w2_v", "nsa_w_o", "w_out",
        "ln1_g", "ln1_b", "router_w", "router_b", "moe_w1", "moe_w3", "moe_w2",
        "shared_w1", "shared_w3", "shared_w2", "ln2_g", "ln2_b"]


def kernel(**inputs):
    import numpy as _np
    import concourse.bacc as _bacc
    from concourse import mybir as _mybir
    from concourse.bass_utils import run_bass_kernel_spmd as _run

    nc = _bacc.Bacc("TRN2", target_bir_lowering=False, num_devices=1)
    arrays, args = {}, {}
    for name in _INS + ["consts"]:
        v = _np.ascontiguousarray(shape_constants() if name == "consts" else inputs[name])
        arrays[f"in_{name}_dram"] = v
        args[name] = nc.dram_tensor(f"in_{name}_dram", v.shape, _mybir.dt.from_np(v.dtype), kind="ExternalInput").ap()
    out = nc.dram_tensor("out_0_dram", (1, T, D), _mybir.dt.float32, kind="ExternalOutput").ap()
    build(nc, args, out)
    r = _run(nc, [arrays], core_ids=[0])
    return r.results[0]["out_0_dram"]
```
